# Optimizing a Trainium2 kernel written in Bass

```python
import math
import jax, jax.numpy as jnp
from jax import lax
import numpy as np

D_MODEL = 1024
BATCH = 1
SEQ = 256
DEPTH = 1

N_META = 16
BLOCK = 128
PAD_FRONT = BLOCK - N_META
HEAD_DIM = 64
FOX_HEADS = 8
SWA_Q_HEADS = 8
SWA_KV_HEADS = 2
WINDOW = 128
N_BUCKETS = 32
MAX_DISTANCE = 128
D_FF = 2816
EPS = 1e-6
NEG = -1e30
FORGET_BIAS_INIT = 2.0
FOX_W = FOX_HEADS * HEAD_DIM
SWA_QW = SWA_Q_HEADS * HEAD_DIM
SWA_KVW = SWA_KV_HEADS * HEAD_DIM
D_IN = 3 * FOX_W + FOX_HEADS + SWA_QW + 2 * SWA_KVW + 2 * D_MODEL


def rms_norm(x, g):
    xf = x.astype(jnp.float32)
    ms = jnp.mean(xf * xf, axis=-1, keepdims=True)
    return (xf * lax.rsqrt(ms + EPS) * g.astype(jnp.float32)).astype(x.dtype)

def swiglu(h, w_in, w_out):
    gu = h @ w_in
    gate, up = jnp.split(gu, 2, axis=-1)
    return (jax.nn.silu(gate) * up) @ w_out

def t5_bucket(dist):
    n = jnp.maximum(dist, 0)
    max_exact = N_BUCKETS // 2
    nf = jnp.maximum(n, 1).astype(jnp.float32)
    large = max_exact + (jnp.log(nf / max_exact) / math.log(MAX_DISTANCE / max_exact)
                         * (N_BUCKETS - max_exact)).astype(jnp.int32)
    large = jnp.minimum(large, N_BUCKETS - 1)
    return jnp.where(n < max_exact, n, large)

def fox_attention(q, k, v, log_f):
    b, p, h, dh = q.shape
    nb = p // BLOCK
    c_k = jnp.cumsum(log_f, axis=1).transpose(0, 2, 1)
    k_pos = jnp.arange(p)
    k_valid = k_pos >= PAD_FRONT
    qb = q.reshape(b, nb, BLOCK, h, dh).transpose(1, 0, 2, 3, 4)
    cqb = c_k.reshape(b, h, nb, BLOCK).transpose(2, 0, 1, 3)
    scale = dh ** -0.5

    def one_block(args):
        qi, cqi, i = args
        q_pos = i * BLOCK + jnp.arange(BLOCK)
        s = jnp.einsum('bqhd,bkhd->bhqk', qi, k, preferred_element_type=jnp.float32) * scale
        s = s + cqi[..., :, None] - c_k[:, :, None, :]
        mask = (k_pos[None, :] <= q_pos[:, None]) & k_valid[None, :]
        s = jnp.where(mask[None, None], s, NEG)
        pr = jax.nn.softmax(s, axis=-1)
        return jnp.einsum('bhqk,bkhd->bqhd', pr.astype(v.dtype), v)

    out = lax.map(one_block, (qb, cqb, jnp.arange(nb)))
    return out.transpose(1, 0, 2, 3, 4).reshape(b, p, h * dh)

def swa_attention(q, k, v, sinks, rel_bias_table):
    b, p, hq, dh = q.shape
    kv = k.shape[2]
    r = hq // kv
    nb = p // BLOCK
    scale = dh ** -0.5
    qb = q.reshape(b, nb, BLOCK, kv, r, dh)

    def band(a):
        a_ext = jnp.concatenate([jnp.zeros_like(a[:, :BLOCK]), a], axis=1)
        a_ext = a_ext.reshape(b, nb + 1, BLOCK, kv, dh)
        return jnp.concatenate([a_ext[:, :-1], a_ext[:, 1:]], axis=2)

    kb, vb = band(k), band(v)
    km, vm = k[:, PAD_FRONT:BLOCK], v[:, PAD_FRONT:BLOCK]
    q_pos = jnp.arange(nb)[:, None] * BLOCK + jnp.arange(BLOCK)[None, :]
    band_pos = (jnp.arange(nb)[:, None] - 1) * BLOCK + jnp.arange(2 * BLOCK)[None, :]
    meta_pos = PAD_FRONT + jnp.arange(N_META)
    d_band = q_pos[:, :, None] - band_pos[:, None, :]
    m_band = (d_band >= 0) & (d_band < WINDOW) & (band_pos[:, None, :] >= PAD_FRONT)
    d_meta = q_pos[:, :, None] - meta_pos[None, None, :]
    m_meta = d_meta >= WINDOW
    table = rel_bias_table.astype(jnp.float32)
    bias_band = table[t5_bucket(d_band)].transpose(0, 3, 1, 2).reshape(nb, kv, r, BLOCK, 2 * BLOCK)
    bias_meta = table[t5_bucket(d_meta)].transpose(0, 3, 1, 2).reshape(nb, kv, r, BLOCK, N_META)

    s_band = jnp.einsum('bnqgrd,bnkgd->bngrqk', qb, kb, preferred_element_type=jnp.float32) * scale + bias_band[None]
    s_band = jnp.where(m_band[None, :, None, None], s_band, NEG)
    s_meta = jnp.einsum('bnqgrd,bmgd->bngrqm', qb, km, preferred_element_type=jnp.float32) * scale + bias_meta[None]
    s_meta = jnp.where(m_meta[None, :, None, None], s_meta, NEG)
    s = jnp.concatenate([s_band, s_meta], axis=-1)
    sink = sinks.astype(jnp.float32).reshape(kv, r)[None, None, :, :, None, None]
    mx = jnp.maximum(jnp.max(s, axis=-1, keepdims=True), sink)
    pr = jnp.exp(s - mx)
    pr = pr / (jnp.sum(pr, axis=-1, keepdims=True) + jnp.exp(sink - mx))
    pr = pr.astype(v.dtype)
    out = (jnp.einsum('bngrqk,bnkgd->bnqgrd', pr[..., :2 * BLOCK], vb)
           + jnp.einsum('bngrqm,bmgd->bnqgrd', pr[..., 2 * BLOCK:], vm))
    return out.reshape(b, p, hq * dh)

def token_mixer(h, rel_bias_table, w_in, forget_bias, fox_q_norm, fox_k_norm,
                swa_q_norm, swa_k_norm, swa_sinks, w_branch_fox, w_branch_swa, w_out):
    b, p, _ = h.shape
    proj = h @ w_in
    widths = [FOX_W, FOX_W, FOX_W, FOX_HEADS, SWA_QW, SWA_KVW, SWA_KVW, D_MODEL]
    idx = list(np.cumsum(widths))
    qa, ka, va, fa, qb, kb, vb, ga, gb = jnp.split(proj, idx, axis=-1)
    qa = rms_norm(qa.reshape(b, p, FOX_HEADS, HEAD_DIM), fox_q_norm)
    ka = rms_norm(ka.reshape(b, p, FOX_HEADS, HEAD_DIM), fox_k_norm)
    va = va.reshape(b, p, FOX_HEADS, HEAD_DIM)
    log_f = jax.nn.log_sigmoid(fa.astype(jnp.float32) + forget_bias.astype(jnp.float32))
    qb = rms_norm(qb.reshape(b, p, SWA_Q_HEADS, HEAD_DIM), swa_q_norm)
    kb = rms_norm(kb.reshape(b, p, SWA_KV_HEADS, HEAD_DIM), swa_k_norm)
    vb = vb.reshape(b, p, SWA_KV_HEADS, HEAD_DIM)
    o_fox = fox_attention(qa, ka, va, log_f)
    o_swa = swa_attention(qb, kb, vb, swa_sinks, rel_bias_table)
    y = jax.nn.sigmoid(ga) * (o_fox @ w_branch_fox) + jax.nn.sigmoid(gb) * (o_swa @ w_branch_swa)
    return y @ w_out

def first_inputs(seed: int = 0) -> dict:
    key = jax.random.key(seed)
    ks = jax.random.split(key, 24)
    f32 = jnp.float32

    def nrm(k, shape, scale):
        return jax.random.normal(k, shape, f32) * scale

    def gain(k, shape):
        return 1.0 + 0.1 * jax.random.normal(k, shape, f32)

    return {
        "x": nrm(ks[0], (BATCH, SEQ, D_MODEL), 1.0),
        "meta_tokens": nrm(ks[1], (N_META, D_MODEL), 1.0),
        "rel_bias_table": nrm(ks[2], (N_BUCKETS, SWA_Q_HEADS), 0.5),
        "ffn1_norm": gain(ks[3], (DEPTH, D_MODEL)),
        "ffn1_w_in": nrm(ks[4], (DEPTH, D_MODEL, 2 * D_FF), D_MODEL ** -0.5),
        "ffn1_w_out": nrm(ks[5], (DEPTH, D_FF, D_MODEL), D_FF ** -0.5),
        "mix_norm": gain(ks[6], (DEPTH, D_MODEL)),
        "w_in": nrm(ks[7], (DEPTH, D_MODEL, D_IN), D_MODEL ** -0.5),
        "forget_bias": FORGET_BIAS_INIT + 0.1 * jax.random.normal(ks[8], (DEPTH, FOX_HEADS), f32),
        "fox_q_norm": gain(ks[9], (DEPTH, HEAD_DIM)),
        "fox_k_norm": gain(ks[10], (DEPTH, HEAD_DIM)),
        "swa_q_norm": gain(ks[11], (DEPTH, HEAD_DIM)),
        "swa_k_norm": gain(ks[12], (DEPTH, HEAD_DIM)),
        "swa_sinks": nrm(ks[13], (DEPTH, SWA_Q_HEADS), 0.5),
        "w_branch_fox": nrm(ks[14], (DEPTH, FOX_W, D_MODEL), FOX_W ** -0.5),
        "w_branch_swa": nrm(ks[15], (DEPTH, SWA_QW, D_MODEL), SWA_QW ** -0.5),
        "w_out": nrm(ks[16], (DEPTH, D_MODEL, D_MODEL), D_MODEL ** -0.5),
        "ffn2_norm": gain(ks[17], (DEPTH, D_MODEL)),
        "ffn2_w_in": nrm(ks[18], (DEPTH, D_MODEL, 2 * D_FF), D_MODEL ** -0.5),
        "ffn2_w_out": nrm(ks[19], (DEPTH, D_FF, D_MODEL), D_FF ** -0.5),
    }

def first_block(x, meta_tokens, rel_bias_table, ffn1_norm, ffn1_w_in, ffn1_w_out, mix_norm,
              w_in, forget_bias, fox_q_norm, fox_k_norm, swa_q_norm, swa_k_norm, swa_sinks,
              w_branch_fox, w_branch_swa, w_out, ffn2_norm, ffn2_w_in, ffn2_w_out):
    b = x.shape[0]
    pad = jnp.zeros((b, PAD_FRONT, D_MODEL), x.dtype)
    meta = jnp.broadcast_to(meta_tokens.astype(x.dtype)[None], (b, N_META, D_MODEL))
    h = jnp.concatenate([pad, meta, x], axis=1)
    for l in range(DEPTH):
        h = h + 0.5 * swiglu(rms_norm(h, ffn1_norm[l]), ffn1_w_in[l], ffn1_w_out[l])
        h = h + token_mixer(rms_norm(h, mix_norm[l]), rel_bias_table, w_in[l], forget_bias[l],
                            fox_q_norm[l], fox_k_norm[l], swa_q_norm[l], swa_k_norm[l],
                            swa_sinks[l], w_branch_fox[l], w_branch_swa[l], w_out[l])
        h = h + 0.5 * swiglu(rms_norm(h, ffn2_norm[l]), ffn2_w_in[l], ffn2_w_out[l])
    return h[:, BLOCK:]


DEPTH_2 = 2

N_MIXERS = 2
N_A = (DEPTH_2 + 1) // 2
N_B = DEPTH_2 // 2

CHUNK = 128
A_WIDTH = D_MODEL
A_GROUPS = 8
A_GROUP_DIM = A_WIDTH // A_GROUPS

N_HEADS = 8
HEAD_DIM_2 = D_MODEL // N_HEADS // 2
V_HEAD_DIM = 2 * HEAD_DIM_2
QK_WIDTH = N_HEADS * 2 * HEAD_DIM_2
V_WIDTH = N_HEADS * V_HEAD_DIM
Q_BLOCK = 128
ROT_DIM = HEAD_DIM_2 // 4
ROPE_THETA = 500000.0

D_FF_2 = 4 * D_MODEL

PLE_DIM = 256
MAX_POS_OFFSET = 4096

RMS_EPS = 1e-6
LN_EPS = 1e-5
SUBLN_EPS = 1e-5


def _rmsnorm(x, g, eps=RMS_EPS):
    xf = x.astype(jnp.float32)
    y = xf * lax.rsqrt(jnp.mean(xf * xf, axis=-1, keepdims=True) + eps)
    return (y * g.astype(jnp.float32)).astype(x.dtype)

def _layernorm(x, g, b):
    xf = x.astype(jnp.float32)
    mu = jnp.mean(xf, axis=-1, keepdims=True)
    var = jnp.mean(jnp.square(xf - mu), axis=-1, keepdims=True)
    y = (xf - mu) * lax.rsqrt(var + LN_EPS)
    return (y * g.astype(jnp.float32) + b.astype(jnp.float32)).astype(x.dtype)

def _rotary_tables(positions, dtype):
    inv_freq = ROPE_THETA ** (-(jnp.arange(0, ROT_DIM, 2, dtype=jnp.float32) / ROT_DIM))
    ang = positions.astype(jnp.float32)[..., None] * inv_freq
    cos = jnp.cos(ang)[:, :, None, None, :].astype(dtype)
    sin = jnp.sin(ang)[:, :, None, None, :].astype(dtype)
    return cos, sin

def _partial_rotary(x, cos, sin):
    xr, xp = x[..., :ROT_DIM], x[..., ROT_DIM:]
    x1, x2 = jnp.split(xr, 2, axis=-1)
    return jnp.concatenate([x1 * cos - x2 * sin, x2 * cos + x1 * sin, xp], axis=-1)

def _chunked_gmlp(a, w_in, ln_g, ln_b, w_s, b_s, w_out):
    B, S, _ = a.shape
    z = jax.nn.gelu(a @ w_in)
    u, v = jnp.split(z, 2, axis=-1)
    v = _layernorm(v, ln_g, ln_b)
    v = v.reshape(B, S // CHUNK, CHUNK, A_GROUPS, A_GROUP_DIM)
    w_causal = w_s * jnp.tril(jnp.ones((CHUNK, CHUNK), dtype=w_s.dtype))
    s = jnp.einsum('gts,bnsgd->bntgd', w_causal, v) + b_s.T[:, :, None]
    y = u * s.reshape(B, S, A_WIDTH)
    return y @ w_out

def _diff_attention(a, positions, w_qkv, lam_q1, lam_k1, lam_q2, lam_k2, subln_g, w_o, lambda_init):
    B, S, _ = a.shape
    qkv = a @ w_qkv
    q, k, v = jnp.split(qkv, [QK_WIDTH, 2 * QK_WIDTH], axis=-1)
    q = q.reshape(B, S, N_HEADS, 2, HEAD_DIM_2)
    k = k.reshape(B, S, N_HEADS, 2, HEAD_DIM_2)
    v = v.reshape(B, S, N_HEADS, V_HEAD_DIM)
    cos, sin = _rotary_tables(positions, q.dtype)
    q = _partial_rotary(q, cos, sin)
    k = _partial_rotary(k, cos, sin)
    f32 = jnp.float32
    lam = (jnp.exp(jnp.sum(lam_q1.astype(f32) * lam_k1.astype(f32)))
           - jnp.exp(jnp.sum(lam_q2.astype(f32) * lam_k2.astype(f32))) + lambda_init)
    scale = HEAD_DIM_2 ** -0.5
    outs = []
    for blk in range(S // Q_BLOCK):
        q0 = blk * Q_BLOCK
        q1 = q0 + Q_BLOCK
        qb = q[:, q0:q1]
        kb = k[:, :q1]
        vb = v[:, :q1]
        sc = jnp.einsum('bqhcd,bkhcd->bhcqk', qb, kb).astype(f32) * scale
        mask = (q0 + jnp.arange(Q_BLOCK))[:, None] >= jnp.arange(q1)[None, :]
        sc = jnp.where(mask, sc, -jnp.inf)
        pr = jax.nn.softmax(sc, axis=-1)
        attn = (pr[:, :, 0] - lam * pr[:, :, 1]).astype(vb.dtype)
        outs.append(jnp.einsum('bhqk,bkhe->bqhe', attn, vb))
    o = jnp.concatenate(outs, axis=1)
    o = _rmsnorm(o, subln_g, SUBLN_EPS) * (1.0 - lambda_init)
    return o.reshape(B, S, V_WIDTH) @ w_o

def _sqrelu_mlp(x, w_up, w_down):
    return jnp.square(jax.nn.relu(x @ w_up)) @ w_down

def second_inputs(seed: int = 0) -> dict:
    key = jax.random.key(seed)
    ks = jax.random.split(key, 32)
    f32 = jnp.float32

    def nrm(k, shape, scale):
        return jax.random.normal(k, shape, f32) * scale

    def gain(k, shape):
        return 1.0 + 0.05 * jax.random.normal(k, shape, f32)

    x = nrm(ks[0], (BATCH, SEQ, D_MODEL), 1.0)
    p = nrm(ks[1], (DEPTH_2, BATCH, SEQ, PLE_DIM), 1.0)
    offsets = jax.random.randint(ks[2], (BATCH, 1), 0, MAX_POS_OFFSET, dtype=jnp.int32)
    positions = (offsets + jnp.arange(SEQ, dtype=jnp.int32)[None, :]).astype(jnp.int32)
    return {
        "x": x,
        "p": p,
        "positions": positions,
        "g_mix_pre": gain(ks[3], (DEPTH_2, D_MODEL)),
        "g_mix_post": gain(ks[4], (DEPTH_2, D_MODEL)),
        "g_ffn_pre": gain(ks[5], (DEPTH_2, D_MODEL)),
        "g_ffn_post": gain(ks[6], (DEPTH_2, D_MODEL)),
        "g_ple_pre": gain(ks[7], (DEPTH_2, D_MODEL)),
        "g_ple_post": gain(ks[8], (DEPTH_2, D_MODEL)),
        "a_w_in": nrm(ks[9], (N_A, D_MODEL, 2 * A_WIDTH), D_MODEL ** -0.5),
        "a_ln_g": gain(ks[10], (N_A, A_WIDTH)),
        "a_ln_b": nrm(ks[11], (N_A, A_WIDTH), 0.02),
        "a_w_s": nrm(ks[12], (N_A, A_GROUPS, CHUNK, CHUNK), CHUNK ** -0.5),
        "a_b_s": 1.0 + nrm(ks[13], (N_A, A_GROUPS, CHUNK), 0.1),
        "a_w_out": nrm(ks[14], (N_A, A_WIDTH, D_MODEL), A_WIDTH ** -0.5),
        "b_w_qkv": nrm(ks[15], (N_B, D_MODEL, 2 * QK_WIDTH + V_WIDTH), D_MODEL ** -0.5),
        "b_lam_q1": nrm(ks[16], (N_B, HEAD_DIM_2), 0.1),
        "b_lam_k1": nrm(ks[17], (N_B, HEAD_DIM_2), 0.1),
        "b_lam_q2": nrm(ks[18], (N_B, HEAD_DIM_2), 0.1),
        "b_lam_k2": nrm(ks[19], (N_B, HEAD_DIM_2), 0.1),
        "b_subln_g": gain(ks[20], (N_B, V_HEAD_DIM)),
        "b_w_o": nrm(ks[21], (N_B, V_WIDTH, D_MODEL), V_WIDTH ** -0.5),
        "f_w_up": nrm(ks[22], (DEPTH_2, D_MODEL, D_FF_2), D_MODEL ** -0.5),
        "f_w_down": nrm(ks[23], (DEPTH_2, D_FF_2, D_MODEL), D_FF_2 ** -0.5),
        "ple_w_proj": nrm(ks[24], (DEPTH_2, PLE_DIM, D_MODEL), PLE_DIM ** -0.5),
        "ple_w_gate": nrm(ks[25], (DEPTH_2, D_MODEL, D_MODEL), D_MODEL ** -0.5),
        "ple_b_gate": nrm(ks[26], (DEPTH_2, D_MODEL), 0.02),
    }

def second_block(x, p, positions, g_mix_pre, g_mix_post, g_ffn_pre, g_ffn_post, g_ple_pre, g_ple_post,
              a_w_in, a_ln_g, a_ln_b, a_w_s, a_b_s, a_w_out,
              b_w_qkv, b_lam_q1, b_lam_k1, b_lam_q2, b_lam_k2, b_subln_g, b_w_o,
              f_w_up, f_w_down, ple_w_proj, ple_w_gate, ple_b_gate):
    h = x
    for i in range(DEPTH_2):
        j = i // N_MIXERS
        a = _rmsnorm(h, g_mix_pre[i])
        if i % N_MIXERS == 0:
            m = _chunked_gmlp(a, a_w_in[j], a_ln_g[j], a_ln_b[j], a_w_s[j], a_b_s[j], a_w_out[j])
        else:
            lambda_init = 0.8 - 0.6 * math.exp(-0.3 * i)
            m = _diff_attention(a, positions, b_w_qkv[j], b_lam_q1[j], b_lam_k1[j], b_lam_q2[j],
                                b_lam_k2[j], b_subln_g[j], b_w_o[j], lambda_init)
        h = h + _rmsnorm(m, g_mix_post[i])
        f = _sqrelu_mlp(_rmsnorm(h, g_ffn_pre[i]), f_w_up[i], f_w_down[i])
        h = h + _rmsnorm(f, g_ffn_post[i])
        gate = jax.nn.sigmoid(_rmsnorm(h, g_ple_pre[i]) @ ple_w_gate[i] + ple_b_gate[i])
        e = gate * (p[i] @ ple_w_proj[i])
        h = h + _rmsnorm(e, g_ple_post[i])
    return h


def setup_inputs(seed=0):
    out = dict(first_inputs(seed))
    for name, value in second_inputs(seed + 1).items():
        if name != "x":
            out[name + "_2"] = value
    return out


def reference(
    x, meta_tokens, rel_bias_table, ffn1_norm, ffn1_w_in, ffn1_w_out, mix_norm, w_in,
    forget_bias, fox_q_norm, fox_k_norm, swa_q_norm, swa_k_norm, swa_sinks, w_branch_fox,
    w_branch_swa, w_out, ffn2_norm, ffn2_w_in, ffn2_w_out, p_2, positions_2, g_mix_pre_2,
    g_mix_post_2, g_ffn_pre_2, g_ffn_post_2, g_ple_pre_2, g_ple_post_2, a_w_in_2, a_ln_g_2,
    a_ln_b_2, a_w_s_2, a_b_s_2, a_w_out_2, b_w_qkv_2, b_lam_q1_2, b_lam_k1_2, b_lam_q2_2,
    b_lam_k2_2, b_subln_g_2, b_w_o_2, f_w_up_2, f_w_down_2, ple_w_proj_2, ple_w_gate_2,
    ple_b_gate_2,
):
    x = first_block(
        x, meta_tokens, rel_bias_table, ffn1_norm, ffn1_w_in, ffn1_w_out, mix_norm, w_in,
        forget_bias, fox_q_norm, fox_k_norm, swa_q_norm, swa_k_norm, swa_sinks, w_branch_fox,
        w_branch_swa, w_out, ffn2_norm, ffn2_w_in, ffn2_w_out,
    )
    return second_block(
        x, p_2, positions_2, g_mix_pre_2, g_mix_post_2, g_ffn_pre_2, g_ffn_post_2, g_ple_pre_2,
        g_ple_post_2, a_w_in_2, a_ln_g_2, a_ln_b_2, a_w_s_2, a_b_s_2, a_w_out_2, b_w_qkv_2,
        b_lam_q1_2, b_lam_k1_2, b_lam_q2_2, b_lam_k2_2, b_subln_g_2, b_w_o_2, f_w_up_2,
        f_w_down_2, ple_w_proj_2, ple_w_gate_2, ple_b_gate_2,
    )


_drawn_inputs = setup_inputs


def setup_inputs(seed=0):
    import zlib

    import numpy as np

    out = dict(_drawn_inputs(seed))
    spreads = {}
    factors = {'forget_bias': 28.88,
     'fox_q_norm': 3.124,
     'fox_k_norm': 3.106,
     'swa_q_norm': 5.824,
     'swa_k_norm': 6.53,
     'swa_sinks': 8.0,
     'g_ple_pre_2': 4.957,
     'a_ln_g_2': 3.549,
     'a_ln_b_2': 7.77,
     'b_lam_q1_2': 8.0,
     'b_lam_k1_2': 4.471,
     'b_lam_q2_2': 8.0,
     'b_subln_g_2': 2.701,
     'ple_b_gate_2': 25.636}
    for name, (base, spread) in spreads.items():
        noise = np.random.default_rng([zlib.crc32(name.encode()), seed]).standard_normal(out[name].shape)
        drawn = base * np.exp(spread * noise) if base else spread * noise
        out[name] = __import__('jax').numpy.asarray(drawn.astype(out[name].dtype))
    for name, factor in factors.items():
        out[name] = (out[name] * factor).astype(out[name].dtype)
    return out
```

```python
import math
from collections import deque
from contextlib import ExitStack

import numpy as np

import concourse.bass as bass
from concourse import mybir

F32 = mybir.dt.float32
F32R = mybir.dt.float32r
I32 = mybir.dt.int32
ALU = mybir.AluOpType
ACT = mybir.ActivationFunctionType
X = mybir.AxisListType.X

P = 128
D = 1024
SEQ = 256
N_META = 16
D_FF = 2816
D_FF_2 = 4096
HEADS = 8
HD = 64
SWA_KV = 2
WINDOW = 128
N_BUCKETS = 32
MAX_DISTANCE = 128
PLE_DIM = 256
ROT = 16
ROPE_THETA = 500000.0
NEG = -1e30
EPS = 1e-6
LN_EPS = 1e-5
SUBLN_EPS = 1e-5
META = 2
TILES = (0, 1)
ALL_TILES = (0, 1, META)
ROWS = (P, P, N_META)
FIRST_TOKEN = (0, P, SEQ)
KEYS = N_META + SEQ
KC = D // P
COLS = 512
PIECE_K = 2
RAW_SLOTS = 4
SPLIT_SLOTS = 6

FOX_W = HEADS * HD
KV_W = SWA_KV * HD
C_QA, C_KA, C_VA = 0, FOX_W, 2 * FOX_W
C_FA = 3 * FOX_W
C_QB = C_FA + HEADS
C_KB = C_QB + FOX_W
C_GA = C_KB + 2 * KV_W
C_GB = C_GA + D

U_WINDOW = 3 * P - 1
U_META = P + N_META - 1
U_ALL = U_WINDOW + 2 * U_META


def bias_selector():
    distance = np.concatenate([2 * P - 1 - np.arange(U_WINDOW), P + N_META - 1 - np.arange(U_META),
                               2 * P + N_META - 1 - np.arange(U_META)])
    seen = np.ones(U_ALL, bool)
    seen[:U_WINDOW] = (distance[:U_WINDOW] >= 0) & (distance[:U_WINDOW] < WINDOW)
    half = N_BUCKETS // 2
    n = np.maximum(distance, 0)
    far = np.log(np.maximum(n, 1).astype(np.float32) / half) / math.log(MAX_DISTANCE / half) * half
    bucket = np.where(n < half, n, np.minimum(half + far.astype(np.int32), N_BUCKETS - 1))
    out = np.zeros((N_BUCKETS + 1, U_ALL), np.float32)
    out[bucket[seen], np.nonzero(seen)[0]] = 1.0
    out[N_BUCKETS, ~seen] = NEG
    return out


def rotary_frequencies():
    return (ROPE_THETA ** (-(np.arange(0, ROT, 2, dtype=np.float32) / ROT))).astype(np.float32)


class Queue:

    def __init__(self, sem):
        self.sem, self.count, self.steps, self.reached = sem, 0, [], {}

    def wait(self, *marks):
        for sem, value in marks:
            if self.reached.get(sem.name, 0) < value:
                self.reached[sem.name] = value
                self.steps.append(lambda e, sem=sem, value=value: e.wait_ge(sem, value))

    def run(self, make, *marks):
        self.wait(*marks)
        self.count += 1
        self.steps.append(lambda e: make(e).then_inc(self.sem, 1))
        return (self.sem, self.count)

    def quiet(self, make, *marks):
        self.wait(*marks)
        self.steps.append(make)

    def dma(self, out, in_, sem, n, *marks, **kw):
        self.wait(*marks)
        self.steps.append(lambda e: e.dma_start(out, in_, **kw).then_inc(sem, 16))
        return (sem, 16 * n)

    def play(self, engine):
        for step in self.steps:
            step(engine)


class Slots:

    def __init__(self, buffers):
        self.free = deque((b, ()) for b in buffers)

    def take(self):
        return self.free.popleft()

    def give(self, buffer, *marks):
        self.free.append((buffer, marks))


class Block:

    def __init__(self, matrix, first, n, tiles=TILES, name=None):
        self.matrix, self.c0, self.n, self.tiles, self.name = matrix, first, n, tiles, name
        self.pieces = matrix.shape[0] // (P * PIECE_K)
        self.at = None

    def source(self, j):
        rows = self.matrix[j * PIECE_K * P:(j + 1) * PIECE_K * P, self.c0:self.c0 + self.n]
        return rows.rearrange("(c p) n -> p c n", p=P)


class Operand:

    def __init__(self, hi, lo):
        self.hi, self.lo, self.ready, self.free = hi, lo, {}, {}

    def forget(self, t):
        for key in [key for key in self.ready if key[0] == t]:
            del self.ready[key]


def column_blocks(matrix, width, tiles=TILES, name=None):
    return [Block(matrix, c, min(COLS, width - c), tiles, (name, c // COLS)) for c in range(0, width, COLS)]


def plan(w):

    def glu(w_in, w_out, tiles):
        up = []
        for c in range(0, D_FF, COLS):
            n = min(COLS, D_FF - c)
            up.append([Block(w_in, c, n, tiles, ("gate", c // COLS)), Block(w_in, D_FF + c, n, tiles, ("up", c // COLS))])
        return [([b], 4 if b is up[0][0] else 0) for pair in up for b in pair], [(column_blocks(w_out, D, tiles), SPLIT_SLOTS)]

    def thin(blocks, first=4):
        return [([b], first if b is blocks[0] else 0) for b in blocks]

    s = {}
    s["ffn1_in"], s["ffn1_out"] = glu(w["ffn1_w_in"][0], w["ffn1_w_out"][0], ALL_TILES)
    w_in = w["w_in"][0]
    s["mix_in"] = thin([Block(w_in, C_KA, FOX_W, ALL_TILES, "ka"), Block(w_in, C_VA, FOX_W, ALL_TILES, "va"),
                        Block(w_in, C_KB, 2 * KV_W, ALL_TILES, "kvb"),
                        Block(w_in, C_QA, FOX_W, TILES, "qa"), Block(w_in, C_QB, FOX_W, TILES, "qb")]
                       + [Block(w_in, C_GA + COLS * i, COLS, TILES, ("gates", i)) for i in range(4)])
    s["branch"] = [([Block(w["w_branch_fox"][0], COLS * i, COLS, TILES, ("fox", i)),
                     Block(w["w_branch_swa"][0], COLS * i, COLS, TILES, ("swa", i))], 4) for i in range(2)]
    s["mix_out"] = [(column_blocks(w["w_out"][0], D), SPLIT_SLOTS)]
    s["ffn2_in"], s["ffn2_out"] = glu(w["ffn2_w_in"][0], w["ffn2_w_out"][0], TILES)
    s["gmlp_in"] = thin(column_blocks(w["a_w_in_2"][0], 2 * D))
    s["gmlp_out"] = [(column_blocks(w["a_w_out_2"][0], D), SPLIT_SLOTS)]
    s["qkv"] = thin(column_blocks(w["b_w_qkv_2"][0], 3 * D))
    s["attn_out"] = [(column_blocks(w["b_w_o_2"][0], D), SPLIT_SLOTS)]
    for i in range(2):
        s["mlp_in", i] = thin(column_blocks(w["f_w_up_2"][i], D_FF_2))
        s["mlp_out", i] = [(column_blocks(w["f_w_down_2"][i], D), SPLIT_SLOTS)]
        s["ple", i] = [([Block(w["ple_w_gate_2"][i], COLS * c, COLS, TILES, ("gate", c)),
                         Block(w["ple_w_proj_2"][i], COLS * c, COLS, TILES, ("proj", c))], 5) for c in range(2)]
    order = ["ffn1_in", "ffn1_out", "mix_in", "branch", "mix_out", "ffn2_in", "ffn2_out",
             "gmlp_in", "gmlp_out", ("mlp_in", 0), ("mlp_out", 0), ("ple", 0),
             "qkv", "attn_out", ("mlp_in", 1), ("mlp_out", 1), ("ple", 1)]
    stream = []
    for name in order:
        for blocks, _ in s[name]:
            for b in blocks:
                b.at = len(stream)
                stream += [(b, j) for j in range(b.pieces)]
    return s, stream


def two_blocks(nc, w, out):
    stages, stream = plan(w)
    hold = ExitStack()

    def sb(name, shape, dt=F32, where=hold):
        return where.enter_context(nc.sbuf_tensor(name, shape, dt))

    def sem(name):
        return hold.enter_context(nc.semaphore(name))

    pe, act, dve, pool, sp = (Queue(sem(n)) for n in ("pe_done", "act_done", "dve_done", "pool_done", "sp_done"))
    last_square = []

    raw = sb("weights_raw", [P, RAW_SLOTS, PIECE_K, COLS])
    w_hi = sb("weights_hi", [P, SPLIT_SLOTS, PIECE_K, COLS], F32R)
    w_lo = sb("weights_lo", [P, SPLIT_SLOTS, PIECE_K, COLS], F32R)
    h_main = sb("h", [P, 2, D])
    h_meta = sb("h_meta", [N_META, D])
    row_main = sb("row", [P, 2, D])
    row_meta = sb("row_meta", [N_META, D])
    x_t = Operand(sb("x_t_hi", [P, KC, KEYS], F32R), sb("x_t_lo", [P, KC, KEYS], F32R))
    p_rows = sb("p_rows", [P, 2, PLE_DIM])
    p_t = Operand(sb("p_t_hi", [P, PLE_DIM // P, SEQ], F32R), sb("p_t_lo", [P, PLE_DIM // P, SEQ], F32R))
    gains_sb = sb("gains", [P, 3, D])
    temps = Slots([sb(f"temp{i}", [P, COLS]) for i in range(4)])
    junk = sb("squares", [P, COLS])
    stats = sb("stats", [P, 1024])
    ident = sb("identity", [P, P])
    flip = sb("anti_identity", [P, P])
    causal = sb("causal_neg", [P, P])
    upto = sb("upto_and_ones", [P, 2 * P])
    after = sb("ones_and_after", [P, KEYS])
    minus_half = sb("minus_half", [P, 16])
    fa_raw = sb("w_fa", [P, KC, HEADS])
    fa_hi = sb("w_fa_hi", [P, KC, HEADS], F32R)
    fa_lo = sb("w_fa_lo", [P, KC, HEADS], F32R)
    head_gains = sb("head_gains", [P, 4, HD])
    forget_b = sb("forget_bias", [P, HEADS])
    sinks = sb("sinks", [P, HEADS])
    banks = Slots([hold.enter_context(nc.psum_tensor(f"bank{i}", [P, 512], F32)) for i in range(8)])

    h = [h_main[:, 0, :], h_main[:, 1, :], h_meta[:, :]]
    row = [row_main[:, 0, :], row_main[:, 1, :], row_meta[:, :]]
    h_ready = {}
    row_free = {t: () for t in ALL_TILES}
    used = [0]

    def stat(n=1):
        used[0] += n
        assert used[0] <= 1024
        return stats[:, used[0] - n:used[0]]

    def mm(o, lhs, rhs, start, stop, *marks):
        return pe.run(lambda e: e.matmul(o, lhs, rhs, start=start, stop=stop), *marks)

    def mm_quiet(o, lhs, rhs, start, stop, *marks):
        pe.quiet(lambda e: e.matmul(o, lhs, rhs, start=start, stop=stop), *marks)

    def turn(o, i, *marks):
        n = i.shape[0]
        return pe.run(lambda e: e.transpose(o, i, ident[0:n, 0:n]), *marks)

    def act_fn(o, i, f, *marks, **kw):
        return act.run(lambda e: e.activation(o, i, f, **kw), *marks)

    def tt(o, a, b, op, *marks, q=dve):
        return q.run(lambda e: e.tensor_tensor(o, a, b, op), *marks)

    def ts(o, a, s1, s2, op0, op1, *marks, q=dve):
        return q.run(lambda e: e.tensor_scalar(o, a, s1, s2, op0, op1) if op1 is not None
                     else e.tensor_scalar(o, a, s1, None, op0), *marks)

    def stt(o, a, s, b, op0, op1, *marks):
        return dve.run(lambda e: e.scalar_tensor_tensor(out=o, in0=a, scalar=s, in1=b, op0=op0, op1=op1), *marks)

    def reduce(o, a, op, *marks):
        return dve.run(lambda e: e.tensor_reduce(o, a, X, op), *marks)

    def rsqrt_mean(o, total, n, eps, *marks):
        m = stat(total.shape[1])[0:total.shape[0], :]
        a = ts(m, total, 1.0 / n, eps, ALU.mult, ALU.add, *marks, q=pool)
        return tt(o, m, minus_half[0:total.shape[0], 0:total.shape[1]], ALU.pow, a, half_set, q=pool)

    later = deque()

    def defer(fn, units=3):
        later.append([units, fn])

    def tick():
        for item in later:
            item[0] -= 1
        while later and later[0][0] <= 0:
            later.popleft()[1]()

    def flush():
        while later:
            later.popleft()[1]()

    raw_sems = [sem(f"raw{i}_loaded") for i in range(RAW_SLOTS)]
    loads, splits, released = [], [], []

    def load_next():
        n = len(loads)
        b, j = stream[n]
        marks = splits[n - RAW_SLOTS] if n >= RAW_SLOTS else ()
        loads.append(sp.dma(raw[:, n % RAW_SLOTS, :, 0:b.n], b.source(j), raw_sems[n % RAW_SLOTS],
                            n // RAW_SLOTS + 1, *marks))

    def split_next():
        n = len(splits)
        b, j = stream[n]
        source = raw[:, n % RAW_SLOTS, :, 0:b.n]
        hi, lo = w_hi[:, n % SPLIT_SLOTS, :, 0:b.n], w_lo[:, n % SPLIT_SLOTS, :, 0:b.n]
        former = (released[n - SPLIT_SLOTS],) if n >= SPLIT_SLOTS else ()
        a = act_fn(hi, source, ACT.Copy, loads[n], *former)
        v = tt(lo, source, hi.bitcast(F32), ALU.subtract, a)
        splits.append((a, v))
        if len(loads) < len(stream):
            load_next()

    def advance():
        while len(splits) < min(len(released) + SPLIT_SLOTS, len(stream)):
            split_next()

    def release(mark):
        released.append(mark)
        advance()

    gain_order = [w["ffn1_norm"][0:1], w["mix_norm"][0:1], w["ffn2_norm"][0:1],
                  w["g_mix_pre_2"][0:1], w["a_ln_g_2"][0:1], w["a_ln_b_2"][0:1], w["g_mix_post_2"][0:1],
                  w["g_ffn_pre_2"][0:1], w["g_ffn_post_2"][0:1], w["g_ple_pre_2"][0:1], w["ple_b_gate_2"][0:1],
                  w["g_ple_post_2"][0:1],
                  w["g_mix_pre_2"][1:2], w["g_mix_post_2"][1:2],
                  w["g_ffn_pre_2"][1:2], w["g_ffn_post_2"][1:2], w["g_ple_pre_2"][1:2], w["ple_b_gate_2"][1:2],
                  w["g_ple_post_2"][1:2]]
    gain_sems = [sem(f"gain{i}_loaded") for i in range(3)]
    gain_marks = []

    def load_gain(*marks):
        n = len(gain_marks)
        if n < len(gain_order):
            gain_marks.append(sp.dma(gains_sb[:, n % 3, :], gain_order[n].broadcast_to([P, D]), gain_sems[n % 3], n // 3 + 1, *marks))

    class Gain:

        def __init__(self, n, uses):
            self.n, self.left, self.marks = n, uses, []

        def ap(self, rows, c0=0, n=D):
            return gains_sb[0:rows, self.n % 3, c0:c0 + n]

        def mark(self):
            return gain_marks[self.n]

        def done(self, mark):
            self.marks.append(mark)
            self.left -= 1
            if not self.left:
                load_gain(*self.marks)

    small_sems = [0]

    def small(q, o, i, *marks, **kw):
        small_sems[0] += 1
        return q.dma(o, i, sem(f"small{small_sems[0]}"), 1, *marks, **kw)

    h_ready[0] = small(act, h_main[:, 0, :], w["x"][0, 0:P, :])
    h_ready[1] = small(act, h_main[:, 1, :], w["x"][0, P:SEQ, :])
    h_ready[META] = small(act, h_meta[:, :], w["meta_tokens"])
    load_gain()
    for _ in range(RAW_SLOTS):
        load_next()
    load_gain()
    load_gain()

    m_id = pool.run(lambda e: e.memset(ident[:, :], 0.0))
    half_set = pool.run(lambda e: e.memset(minus_half[:, :], -0.5))

    def select(o, i, base, cm, pattern, cmp, fill, *marks):
        return pool.run(lambda e: e.affine_select(out=o, in_=i, compare_op=cmp, fill=fill, base=base,
                                                  pattern=pattern, channel_multiplier=cm), *marks)

    ident_set = select(ident[:, :], ident[:, :], 0, 1, [[-1, P]], ALU.not_equal, 1.0, m_id)
    a = pool.run(lambda e: e.memset(flip[:, :], 0.0))
    flip_set = select(flip[:, :], flip[:, :], -(P - 1), 1, [[1, P]], ALU.not_equal, 1.0, a)
    a = pool.run(lambda e: e.memset(causal[:, :], 0.0))
    causal_set = select(causal[:, :], causal[:, :], 0, 1, [[-1, P]], ALU.is_ge, NEG, a)
    a = pool.run(lambda e: e.memset(upto[:, :], 1.0))
    upto_set = select(upto[:, 0:P], upto[:, 0:P], 0, -1, [[1, P]], ALU.is_ge, 0.0, a)
    a = pool.run(lambda e: e.memset(after[:, :], 1.0))
    after_set = select(after[:, P + N_META:KEYS], after[:, P + N_META:KEYS], 0, 1, [[-1, P]], ALU.is_gt, 0.0, a)

    sel_sb = row_main[0:N_BUCKETS + 1, 1, 0:U_ALL]
    table_sb = row_main[0:N_BUCKETS + 1, 1, U_ALL:U_ALL + HEADS]
    a = pool.run(lambda e: e.memset(table_sb, 1.0))
    m_table = small(pool, table_sb[0:N_BUCKETS, :], w["rel_bias_table"], a)
    m_sel = small(pool, sel_sb, w["bias_selector"])
    m_fa = small(pool, fa_raw[:, :, :], w["w_in"][0][:, C_FA:C_FA + HEADS].rearrange("(c p) n -> p c n", p=P))
    m_fb = small(pool, forget_b[:, :], w["forget_bias"].broadcast_to([P, HEADS]))
    m_sink = small(pool, sinks[:, :], w["swa_sinks"].broadcast_to([P, HEADS]))
    m_hg = [small(pool, head_gains[:, i, :], w[k].broadcast_to([P, HD]))
            for i, k in enumerate(("fox_q_norm", "fox_k_norm", "swa_q_norm", "swa_k_norm"))]

    advance()

    def turn_split(source, t, chunks, to, first_chunk, *marks):
        n, c0 = ROWS[t], FIRST_TOKEN[t]
        last = None
        for c in range(0, chunks, 4):
            k = min(4, chunks - c)
            bank, free = banks.take()
            for i in range(k):
                last = turn(bank[:, i * n:(i + 1) * n], source[0:n, (c + i) * P:(c + i + 1) * P], *marks, *free, ident_set)
            got = bank[:, 0:k * n].rearrange("p (c n) -> p c n", n=n)
            hi = to.hi[:, first_chunk + c:first_chunk + c + k, c0:c0 + n]
            lo = to.lo[:, first_chunk + c:first_chunk + c + k, c0:c0 + n]
            a = act_fn(hi, got, ACT.Copy, last, *to.free.get(t, ()))
            v = tt(lo, got, hi.bitcast(F32), ALU.subtract, a)
            banks.give(bank, v)
            for i in range(k):
                to.ready[t, first_chunk + c + i] = (a, v)
        return last

    def products(groups, x, epilogue, first_chunk=None):
        for blocks, tail in groups:
            pieces = [(b, j) for b in blocks for j in range(b.pieces)]
            tail = min(tail, len(pieces))
            held = {}

            def go(b, j, t):
                operand = x(b) if first_chunk is not None else x
                k0 = first_chunk(b) if first_chunk is not None else 0
                if (b, t) not in held:
                    held[b, t], free = banks.take()
                    pe.wait(*free)
                n, c0, slot = ROWS[t], FIRST_TOKEN[t], (b.at + j) % SPLIT_SLOTS
                o = held[b, t][0:n, 0:b.n]
                mark = None
                for i in range(PIECE_K):
                    k = k0 + j * PIECE_K + i
                    if (t, k) not in operand.ready:
                        flush()
                    xh, xl = operand.hi[:, k, c0:c0 + n], operand.lo[:, k, c0:c0 + n]
                    wh, wl = w_hi[:, slot, i, 0:b.n], w_lo[:, slot, i, 0:b.n]
                    last = j == b.pieces - 1 and i == PIECE_K - 1
                    mm_quiet(o, xh, wh, j == 0 and i == 0, False, *operand.ready[t, k], *splits[b.at + j])
                    mm_quiet(o, xh, wl, False, False)
                    if i == PIECE_K - 1:
                        mark = mm(o, xl, wh, False, last)
                    else:
                        mm_quiet(o, xl, wh, False, last)
                operand.free[t] = (mark,)
                if t == b.tiles[-1]:
                    release(mark)
                if j == b.pieces - 1:
                    epilogue(b, t, held.pop((b, t)), mark)
                tick()

            cut = len(pieces) - tail
            for b, j in pieces[:cut]:
                for t in b.tiles:
                    go(b, j, t)
            for t in pieces[-1][0].tiles if tail else ():
                for b, j in pieces[cut:]:
                    go(b, j, t)

    def pre_norm(t, gain, units=4):
        n = ROWS[t]
        ss, r = stat()[0:n, :], stat()[0:n, :]
        a = act_fn(row[t][0:n, :], h[t][0:n, :], ACT.Square, h_ready[t], *row_free[t], accum_out=ss)
        p = rsqrt_mean(r, ss, D, EPS, a)
        v = stt(row[t][0:n, :], h[t][0:n, :], r, gain.ap(n), ALU.mult, ALU.mult, p, gain.mark())
        gain.done(v)
        x_t.forget(t)

        def turn_it():
            row_free[t] = (turn_split(row[t], t, KC, x_t, 0, v),)

        defer(turn_it, units)

    parts = {}

    def post_norm_part(t, half, source, mark, bank, gain, then):
        ss = stat()
        a = act_fn(junk[:, :], source, ACT.Square, mark, *last_square, accum_out=ss)
        last_square[:] = [a]
        parts.setdefault(t, []).append((half, source, bank, a, ss))
        if len(parts[t]) < 2:
            return
        both = parts.pop(t)
        total, r = stat(), stat()
        p = tt(total, both[0][4], both[1][4], ALU.add, both[0][3], both[1][3], q=pool)
        p = rsqrt_mean(r, total, D, EPS, p)
        for half, source, bank, _, _ in both:
            tmp, free = temps.take()
            v = stt(tmp[:, :], source, r, gain.ap(P, half * COLS, COLS), ALU.mult, ALU.mult, p, gain.mark(), *free)
            to = h[t][:, half * COLS:(half + 1) * COLS]
            if bank is not None:
                banks.give(bank, v)
            last = tt(to, tmp[:, :], to, ALU.add, v)
            temps.give(tmp, last)
        gain.done(v)
        h_ready[t] = last
        then(t)

    def glu(name, tiles, region, then):
        hid = Operand(sb(f"{name}_hid_hi", [P, D_FF // P, KEYS], F32R, region),
                      sb(f"{name}_hid_lo", [P, D_FF // P, KEYS], F32R, region))
        fresh = region_marks()
        held = {}

        def hidden(b, t, bank, mark):
            n = ROWS[t]
            if b.name[0] == "gate":
                buf, free = temps.take()
                a = act_fn(buf[0:n, 0:b.n], bank[0:n, 0:b.n], ACT.Silu, mark, *free)
                held[t] = (buf, a)
                banks.give(bank, a)
                return
            buf, a = held.pop(t)
            v = tt(buf[0:n, 0:b.n], bank[0:n, 0:b.n], buf[0:n, 0:b.n], ALU.mult, mark, a)
            banks.give(bank, v)

            def turn_it():
                act.wait(*fresh)
                dve.wait(*fresh)
                temps.give(buf, turn_split(buf, t, b.n // P, hid, b.name[1] * (COLS // P), v))

            defer(turn_it, 2)

        products(stages[name + "_in"], x_t, hidden)

        def residual(b, t, bank, mark):
            n, c = ROWS[t], b.c0
            to = h[t][0:n, c:c + b.n]
            v = stt(to, bank[0:n, 0:b.n], 0.5, to, ALU.mult, ALU.add, mark)
            banks.give(bank, v)
            if b.c0 + b.n == D:
                h_ready[t] = v
                then(t)

        products(stages[name + "_out"], hid, residual)

    def region_marks():
        return [(q.sem, q.count) for q in (pe, act, dve, pool) if q.count]

    pre = Gain(0, 3)
    pre_norm(0, pre, 0)

    bias_dram = nc.dram_tensor("bias_rows", [HEADS, U_ALL], F32, kind="Internal").ap()
    bias_marks = []
    for i, c in enumerate(range(0, U_ALL, 512)):
        n = min(512, U_ALL - c)
        bank, free = banks.take()
        a = mm(bank[0:HEADS, 0:n], table_sb, sel_sb[:, c:c + n], True, True, m_table, m_sel, *free)
        tmp, _ = temps.take()
        v = dve.run(lambda e, o=tmp[0:HEADS, 0:n], s=bank[0:HEADS, 0:n]: e.tensor_copy(o, s), a)
        banks.give(bank, v)
        bias_marks.append(small(act, bias_dram[:, c:c + n], tmp[0:HEADS, 0:n], v))
        temps.give(tmp, bias_marks[-1])
        row_free[1] = (a,)
    pre_norm(1, pre, 0)
    pre_norm(META, pre, 0)
    flush()

    mix_pre = Gain(1, 3)
    region = ExitStack()
    glu("ffn1", ALL_TILES, region, lambda t: pre_norm(t, mix_pre))
    region.close()

    region = ExitStack()

    def rsb(name, shape, dt=F32):
        return sb(name, shape, dt, region)

    fresh = region_marks()
    va, va_m = rsb("va", [P, 2, FOX_W]), rsb("va_meta", [N_META, FOX_W])
    vb, vb_m = rsb("vb", [P, 2, KV_W]), rsb("vb_meta", [N_META, KV_W])
    gates = rsb("gates", [P, 2, 2 * D])
    qa_t, qb_t = rsb("qa_t", [P, 4, SEQ]), rsb("qb_t", [P, 4, SEQ])
    ka_t, kb_t = rsb("ka_t", [P, 4, KEYS]), rsb("kb_t", [P, SWA_KV, KEYS])
    window_b = rsb("window_bias", [P, HEADS, 2 * P])
    meta_b = rsb("meta_bias", [P, 2, HEADS, N_META])
    prob = Slots([rsb(f"prob{i}", [P, KEYS]) for i in range(2)])
    prob_t = Slots([rsb(f"prob_t{i}", [P, 3, P]) for i in range(2)])
    decay = Slots([rsb(f"decay{i}", [P, 3, P]) for i in range(2)])
    log_f = rsb("log_f", [P, 3, HEADS])

    def diagonals(u0, width):
        return bass.AP(bias_dram.tensor, u0, [[1, P], [U_ALL, HEADS], [1, width]])

    bias_loaded = [small(pool, window_b[:, :, :], diagonals(0, 2 * P), *fresh, *bias_marks),
                   small(pool, meta_b[:, 0, :, :], diagonals(U_WINDOW, N_META)),
                   small(pool, meta_b[:, 1, :, :], diagonals(U_WINDOW + U_META, N_META))]
    act.wait(*fresh)
    dve.wait(*fresh)

    key0 = (N_META, N_META + P, 0)
    v_ready, gate_ready = {}, {}

    def head_norm(t, source, heads, gain_i, twice, mark):
        n = ROWS[t]
        width = heads * HD
        sq, free = temps.take()
        a = act_fn(sq[0:n, 0:width], source, ACT.Square, mark, *free)
        ss, r = stat(heads)[0:n, :], stat(heads)[0:n, :]
        v = reduce(ss, sq[0:n, 0:width].rearrange("p (h d) -> p h d", d=HD), ALU.add, a)
        p = rsqrt_mean(r, ss, HD, EPS, v)
        buf = sq
        by_head = buf[0:n, 0:width].rearrange("p (h d) -> p h d", d=HD)
        v = tt(by_head, source.rearrange("p (h d) -> p h d", d=HD),
               r.unsqueeze(2).broadcast_to([n, heads, HD]), ALU.mult, p)
        g = head_gains[0:n, gain_i, :].unsqueeze(1).broadcast_to([n, heads, HD])
        if not twice:
            v = tt(by_head, by_head, g, ALU.mult, v, m_hg[gain_i])
        else:
            for c in range(2):
                v2 = tt(buf[0:n, 2 * width:4 * width].rearrange("p (h c d) -> p h c d", c=2, d=HD)[:, :, c, :],
                        by_head, g, ALU.mult, v, m_hg[gain_i])
            v = v2
        return buf, v

    def store_turned(t, buf, c0, chunks, to, col0, mark, scale, ready):
        def turn_it():
            n = ROWS[t]
            bank, free = banks.take()
            last = None
            for i in range(chunks):
                last = turn(bank[:, i * n:(i + 1) * n], buf[0:n, c0 + i * P:c0 + (i + 1) * P], mark, *free)
            a = act_fn(to[:, 0:chunks, col0:col0 + n], bank[:, 0:chunks * n].rearrange("p (c n) -> p c n", n=n),
                       ACT.Copy, last, scale=scale)
            banks.give(bank, a)
            temps.give(buf, last)
            ready.append(a)

        defer(turn_it, 3)

    fox_ready, swa_ready = [], []

    def mixer_in(b, t, bank, mark):
        n = ROWS[t]
        got = bank[0:n, 0:b.n]
        if b.name == "ka":
            buf, v = head_norm(t, got, HEADS, 1, False, mark)
            banks.give(bank, v)
            store_turned(t, buf, 0, 4, ka_t, key0[t], v, 1.0, fox_ready)
        elif b.name == "qa":
            buf, v = head_norm(t, got, HEADS, 0, False, mark)
            banks.give(bank, v)
            store_turned(t, buf, 0, 4, qa_t, P * t, v, HD ** -0.5, fox_ready)
        elif b.name == "qb":
            buf, v = head_norm(t, got, HEADS, 2, False, mark)
            banks.give(bank, v)
            store_turned(t, buf, 0, 4, qb_t, P * t, v, HD ** -0.5, swa_ready)
        elif b.name == "va":
            to = va[:, t, :] if t != META else va_m[:, :]
            a = act_fn(to, got, ACT.Copy, mark)
            v_ready["fox", t] = a
            banks.give(bank, a)
        elif b.name == "kvb":
            buf, v = head_norm(t, bank[0:n, 0:KV_W], SWA_KV, 3, True, mark)
            store_turned(t, buf, 2 * KV_W, SWA_KV, kb_t, key0[t], v, 1.0, swa_ready)
            to = vb[:, t, :] if t != META else vb_m[:, :]
            a = act_fn(to, bank[0:n, KV_W:2 * KV_W], ACT.Copy, mark, v)
            v_ready["swa", t] = a
            banks.give(bank, a)
        else:
            i = b.name[1]
            a = act_fn(gates[:, t, i * COLS:(i + 1) * COLS], got, ACT.Sigmoid, mark)
            gate_ready[t, i] = a
            banks.give(bank, a)

    mix_groups = stages["mix_in"]
    products(mix_groups[:1], x_t, mixer_in)
    a_fa = act_fn(fa_hi[:, :, :], fa_raw[:, :, :], ACT.Copy, m_fa)
    v_fa = tt(fa_lo[:, :, :], fa_raw[:, :, :], fa_hi[:, :, :].bitcast(F32), ALU.subtract, a_fa)
    flush()
    fa_marks = {}
    f_bank, free = banks.take()
    for t in ALL_TILES:
        n, c0 = ROWS[t], FIRST_TOKEN[t]
        o = f_bank[0:n, t * HEADS:(t + 1) * HEADS]
        for k in range(KC):
            xh, xl = x_t.hi[:, k, c0:c0 + n], x_t.lo[:, k, c0:c0 + n]
            mm_quiet(o, xh, fa_hi[:, k, :], k == 0, False, v_fa, *free, *x_t.ready[t, k])
            mm_quiet(o, xh, fa_lo[:, k, :], False, False)
            fa_marks[t] = mm(o, xl, fa_hi[:, k, :], False, k == KC - 1)
    log_f_ready = {}
    fx, fl, fe = stat(3 * HEADS), stat(3 * HEADS), stat(3 * HEADS)
    for t in ALL_TILES:
        n, s = ROWS[t], slice(t * HEADS, (t + 1) * HEADS)
        v = tt(fx[0:n, s], f_bank[0:n, s], forget_b[0:n, :], ALU.add, fa_marks[META], m_fb)
        v1 = ts(fl[0:n, s], fx[0:n, s], -1.0, None, ALU.mult, None, v)
        v2 = tt(fl[0:n, s], fl[0:n, s], fx[0:n, s], ALU.min, v1)
        a = act_fn(fe[0:n, s], fl[0:n, s], ACT.Exp, v2)
        a = act_fn(fe[0:n, s], fe[0:n, s], ACT.Ln, a, bias=1.0)
        log_f_ready[t] = stt(log_f[0:n, t, :], fx[0:n, s], 0.0, fe[0:n, s], ALU.min, ALU.subtract, a)
    banks.give(f_bank, v)
    products(mix_groups[1:], x_t, mixer_in)
    flush()

    def key_parts(t):
        return [(0, N_META, META), (N_META, P, 0)] + ([(N_META + P, P, 1)] if t else [])

    def fox_scores(t, hd):
        keys = N_META + P * (t + 1)
        c, b = hd // 2, HD * (hd % 2)
        d, free_d = decay.take()
        ones, tri = upto[:, P:2 * P], upto[:, 0:P]
        ms = [ts(d[0:N_META, 0, :], ones[0:N_META, :], log_f[0:N_META, META, hd:hd + 1], None, ALU.mult, None,
                 log_f_ready[META], upto_set, *free_d, q=pool),
              ts(d[:, 1, :], ones if t else tri, log_f[:, 0, hd:hd + 1], None, ALU.mult, None, log_f_ready[0], q=pool)]
        if t:
            ms.append(ts(d[:, 2, :], tri, log_f[:, 1, hd:hd + 1], None, ALU.mult, None, log_f_ready[1], q=pool))
        bank, free = banks.take()
        o = bank[:, 0:keys]
        mm_quiet(o, qa_t[b:b + HD, c, P * t:P * t + P], ka_t[b:b + HD, c, 0:keys], True, False, *fox_ready, *free)
        mm_quiet(bank[:, 0:N_META], d[0:N_META, 0, :], after[0:N_META, P + N_META:P + 2 * N_META], False, False,
                 after_set, *ms)
        mm_quiet(bank[:, 0:N_META + P], d[:, 1, :], after[:, P:KEYS], False, False)
        if t:
            mm_quiet(o, d[:, 2, :], after[:, 0:KEYS], False, False)
        last = mm(bank[:, keys - P:keys], ident[:, :], causal[:, :], False, True, causal_set)
        decay.give(d, last)
        return bank, last, keys

    def swa_scores(t, hd):
        keys = N_META + P * (t + 1)
        c, b, g = hd // 2, HD * (hd % 2), hd // (HEADS // SWA_KV)
        bank, free = banks.take()
        o = bank[:, 0:keys]
        mm_quiet(o, qb_t[b:b + HD, c, P * t:P * t + P], kb_t[b:b + HD, g, 0:keys], True, False, *swa_ready, *free)
        mm_quiet(bank[:, 0:N_META], flip[:, :], meta_b[:, t, hd, :], False, False, flip_set, *bias_loaded)
        last = mm(bank[:, N_META:keys], flip[:, :], window_b[:, hd, P * (1 - t):2 * P], False, True)
        return bank, last, keys

    def softmax(bank, mark, keys, sink, o_sum):
        mx, neg = stat(), stat()
        v = reduce(mx, bank[:, 0:keys], ALU.max, mark)
        if sink is None:
            v = ts(neg, mx, -1.0, None, ALU.mult, None, v)
        else:
            v = ts(neg, mx, sink, -1.0, ALU.max, ALU.mult, v, m_sink)
        pr, free = prob.take()
        if sink is None:
            a = act_fn(pr[:, 0:keys], bank[:, 0:keys], ACT.Exp, v, *free, bias=neg, accum_out=o_sum)
        else:
            part, extra = stat(), stat()
            a = act_fn(pr[:, 0:keys], bank[:, 0:keys], ACT.Exp, v, *free, bias=neg, accum_out=part)
            a2 = act_fn(extra, neg, ACT.Exp, v, bias=sink)
            tt(o_sum, part, extra, ALU.add, a2)
        banks.give(bank, a)
        return pr, a

    def turn_prob(pr, mark, t):
        bank, free = banks.take()
        last = None
        for i, (k0, n, _) in enumerate(key_parts(t)):
            last = turn(bank[0:n, i * P:(i + 1) * P], pr[:, k0:k0 + n], mark, *free)
        prob.give(pr, last)
        pt, free = prob_t.take()
        v = dve.run(lambda e, o=pt[0:N_META, 0, :], s=bank[0:N_META, 0:P]: e.tensor_copy(o, s), last, *free)
        k = t + 1
        a = act_fn(pt[:, 1:1 + k, :], bank[:, P:P + P * k].rearrange("p (k n) -> p k n", n=P), ACT.Copy, v)
        banks.give(bank, a)
        return pt, a

    sums = {kind: stat(2 * HEADS) for kind in ("fox", "swa")}
    attn_rows = {}

    def attend(kind, t):
        o_bank, o_free = banks.take()
        total = sums[kind][:, t * HEADS:(t + 1) * HEADS]
        scored, turned = {}, {}
        for i in range(HEADS + 2):
            if i < HEADS:
                sc = fox_scores(t, i) if kind == "fox" else swa_scores(t, i)
                scored[i] = softmax(*sc, None if kind == "fox" else sinks[:, i:i + 1], total[:, i:i + 1])
            if 1 <= i <= HEADS:
                turned[i - 1] = turn_prob(*scored.pop(i - 1), t)
            if i >= 2:
                hd = i - 2
                pt, mark = turned.pop(hd)
                ks = key_parts(t)
                for j, (_, n, part) in enumerate(ks):
                    if kind == "fox":
                        v = (va[:, part, :] if part != META else va_m[:, :])[:, hd * HD:(hd + 1) * HD]
                    else:
                        g = hd // (HEADS // SWA_KV)
                        v = (vb[:, part, :] if part != META else vb_m[:, :])[:, g * HD:(g + 1) * HD]
                    last = mm(o_bank[:, hd * HD:(hd + 1) * HD], pt[0:n, j, :], v, j == 0, j == len(ks) - 1,
                              mark, *o_free, *[v_ready[kind, p] for _, _, p in ks])
                prob_t.give(pt, last)
        inv = stat(HEADS)
        v = dve.run(lambda e: e.reciprocal(inv, total), scored_end(), (dve.sem, dve.count))
        c0 = 0 if kind == "fox" else FOX_W
        to = row[t][:, c0:c0 + FOX_W].rearrange("p (h d) -> p h d", d=HD)
        v = tt(to, o_bank[:, :].rearrange("p (h d) -> p h d", d=HD), inv.unsqueeze(2).broadcast_to([P, HEADS, HD]),
               ALU.mult, v, last, *row_free[t])
        banks.give(o_bank, v)
        attn_rows[kind, t] = v

    def scored_end():
        return (act.sem, act.count)

    for kind in ("fox", "swa"):
        for t in TILES:
            attend(kind, t)
            if kind == "swa":
                x_t.forget(t)
                row_free[t] = (turn_split(row[t], t, KC, x_t, 0, attn_rows["fox", t], attn_rows["swa", t]),)

    def branch(b, t, bank, mark):
        kind, i = b.name
        c = i * COLS + (0 if kind == "fox" else D)
        g = gates[:, t, c:c + COLS]
        v = tt(g, bank[:, :], g, ALU.mult, mark, gate_ready[t, c // COLS])
        banks.give(bank, v)
        if kind == "swa":
            y = gates[:, t, i * COLS:(i + 1) * COLS]
            v = tt(y, y, g, ALU.add, v)
            if i == 1:
                def turn_it():
                    x_t.forget(t)
                    turn_split(gates[:, t, 0:D], t, KC, x_t, 0, v)

                defer(turn_it, 1)

    products(stages["branch"], lambda b: x_t, branch, lambda b: 0 if b.name[0] == "fox" else 4)

    ffn2_pre = Gain(2, 2)

    def mixer_out(b, t, bank, mark):
        to = h[t][:, b.c0:b.c0 + b.n]
        v = tt(to, bank[:, :], to, ALU.add, mark)
        banks.give(bank, v)
        if b.c0 + b.n == D:
            h_ready[t] = v
            pre_norm(t, ffn2_pre)

    products(stages["mix_out"], x_t, mixer_out)
    region.close()

    region = ExitStack()
    gmlp_pre = Gain(3, 2)
    glu("ffn2", TILES, region, lambda t: pre_norm(t, gmlp_pre))
    region.close()

    def load_p(layer):
        marks = p_free[0]
        m = small(pool, p_rows[:, :, :], w["p_2"][layer, 0].rearrange("(t p) n -> p t n", p=P), *marks)

        def turn_it():
            for t in TILES:
                p_t.forget(t)
                last = turn_split(p_rows[:, t, :], t, PLE_DIM // P, p_t, 0, m)
            p_free[0] = (last,)

        return turn_it

    p_free = [()]

    def mlp(i, region, pre_next):
        hid = Operand(sb(f"mlp{i}_hid_hi", [P, D_FF_2 // P, SEQ], F32R, region),
                      sb(f"mlp{i}_hid_lo", [P, D_FF_2 // P, SEQ], F32R, region))
        fresh = region_marks()

        def hidden(b, t, bank, mark):
            buf, free = temps.take()
            a = act_fn(buf[:, :], bank[:, :], ACT.Relu, mark, *free)
            banks.give(bank, a)
            v = tt(buf[:, :], buf[:, :], buf[:, :], ALU.mult, a)

            def turn_it():
                act.wait(*fresh)
                dve.wait(*fresh)
                temps.give(buf, turn_split(buf, t, COLS // P, hid, b.name[1] * (COLS // P), v))

            defer(turn_it, 2)

        products(stages["mlp_in", i], x_t, hidden)
        gain = Gain(gain_at["ffn_post", i], 2)
        products(stages["mlp_out", i], hid,
                 lambda b, t, bank, mark: post_norm_part(t, b.name[1], bank[:, :], mark, bank, gain, pre_next))

    gain_at = {("ffn_post", 0): 8, ("ffn_post", 1): 15, ("ple_b", 0): 10, ("ple_b", 1): 17,
               ("ple_post", 0): 11, ("ple_post", 1): 18}

    def ple(i, then):
        bias, gain = Gain(gain_at["ple_b", i], 4), Gain(gain_at["ple_post", i], 2)
        held = {}

        def gated(b, t, bank, mark):
            kind, c = b.name
            if kind == "gate":
                buf, free = temps.take()
                v = tt(buf[:, :], bank[:, :], bias.ap(P, c * COLS, COLS), ALU.add, mark, bias.mark(), *free)
                banks.give(bank, v)
                bias.done(v)
                held[t] = (buf, act_fn(buf[:, :], buf[:, :], ACT.Sigmoid, v))
            else:
                buf, a = held.pop(t)
                to = row[t][:, c * COLS:(c + 1) * COLS]
                v = tt(to, bank[:, :], buf[:, :], ALU.mult, mark, a, *row_free[t])
                banks.give(bank, v)
                temps.give(buf, v)
                post_norm_part(t, c, to, v, None, gain, then)

        products(stages["ple", i], lambda b: x_t if b.name[0] == "gate" else p_t, gated, lambda b: 0)

    region = ExitStack()
    fresh = region_marks()
    z = rsb("z", [P, 2, 2 * D])
    ws_rows = rsb("w_s_rows", [P, HEADS, P])
    ws_t = rsb("w_s_t", [P, HEADS, P])
    b_s = rsb("b_s", [P, HEADS])
    m_ws = small(pool, ws_rows[:, :, :], w["a_w_s_2"][0].rearrange("g t s -> t g s"), *fresh)
    m_bs = small(pool, b_s[:, :], w["a_b_s_2"][0].rearrange("g t -> t g"), allow_slow_non_contiguous=True)
    turn_p = load_p(0)
    act.wait(*fresh)
    dve.wait(*fresh)
    ws_marks = []

    def turn_ws():
        for g0 in range(0, HEADS, 4):
            bank, free = banks.take()
            for i in range(4):
                last = turn(bank[:, i * P:(i + 1) * P], ws_rows[:, g0 + i, :], m_ws, *free)
            v = tt(ws_t[:, g0:g0 + 4, :], bank[:, :].rearrange("p (g t) -> p g t", t=P),
                   upto[:, 0:P].unsqueeze(1).broadcast_to([P, 4, P]), ALU.mult, last, upto_set)
            banks.give(bank, v)
            ws_marks.append(v)

    z_sum = {t: [] for t in TILES}
    z_marks = {t: [] for t in TILES}
    ln_g, ln_b = Gain(4, 2), Gain(5, 2)

    def gmlp_in(b, t, bank, mark):
        i = b.name[1]
        kw = {}
        if i >= 2:
            s = stat()
            z_sum[t].append(s)
            kw = {"accum_out": s}
        a = act_fn(z[:, t, i * COLS:(i + 1) * COLS], bank[:, :], ACT.Gelu_apprx_tanh, mark, **kw)
        banks.give(bank, a)
        z_marks[t].append(a)
        if i == 3:
            v_rows = z[:, t, D:2 * D]
            total, minus_mean, ss, r = stat(), stat(), stat(), stat()
            v = tt(total, z_sum[t][0], z_sum[t][1], ALU.add, a)
            v = ts(minus_mean, total, -1.0 / D, None, ALU.mult, None, v)
            a = act_fn(row[t][:, :], v_rows, ACT.Square, v, *row_free[t], bias=minus_mean, accum_out=ss)
            p = rsqrt_mean(r, ss, D, LN_EPS, a)
            v = ts(v_rows, v_rows, minus_mean, r, ALU.add, ALU.mult, p)
            v = tt(v_rows, v_rows, ln_g.ap(P), ALU.mult, v, ln_g.mark())
            ln_g.done(v)
            v = tt(v_rows, v_rows, ln_b.ap(P), ALU.add, v, ln_b.mark())
            ln_b.done(v)
            for g0 in range(0, HEADS, 4):
                bank, free = banks.take()
                for g in range(g0, g0 + 4):
                    last = mm(bank[:, (g - g0) * P:(g - g0 + 1) * P], ws_t[:, g, :], v_rows[:, g * P:(g + 1) * P],
                              True, True, v, *ws_marks, *free)
                for g in range(g0, g0 + 4):
                    u = z[:, t, g * P:(g + 1) * P]
                    o = stt(u, bank[:, (g - g0) * P:(g - g0 + 1) * P], b_s[:, g:g + 1], u, ALU.add, ALU.mult,
                            last, m_bs, *z_marks[t])
                banks.give(bank, o)
            x_t.forget(t)
            turn_split(z[:, t, 0:D], t, KC, x_t, 0, o)

    defer(turn_ws, 8)
    defer(turn_p, 1)
    products(stages["gmlp_in"], x_t, gmlp_in)
    mix_post, ffn_pre = Gain(6, 2), Gain(7, 2)
    products(stages["gmlp_out"], x_t,
             lambda b, t, bank, mark: post_norm_part(t, b.name[1], bank[:, :], mark, bank, mix_post,
                                                     lambda t: pre_norm(t, ffn_pre)))
    region.close()

    region = ExitStack()
    ple_pre = Gain(9, 2)
    mlp(0, region, lambda t: pre_norm(t, ple_pre))
    region.close()
    attn_pre = Gain(12, 2)
    ple(0, lambda t: pre_norm(t, attn_pre))

    lambda_init = 0.8 - 0.6 * math.exp(-0.3)
    region = ExitStack()
    fresh = region_marks()
    qk = rsb("qk_rows", [P, 2, 2 * D])
    vv = rsb("v_rows", [P, 2, D])
    q_t, k_t = rsb("q_t", [P, HEADS, SEQ]), rsb("k_t", [P, HEADS, SEQ])
    prob2 = Slots([rsb(f"prob2_{i}", [P, 2, SEQ]) for i in range(2)])
    diff = Slots([rsb(f"diff{i}", [P, SEQ]) for i in range(2)])
    diff_t = Slots([rsb(f"diff_t{i}", [P, 2, P]) for i in range(2)])
    rot = [rsb(f"rot{i}", [P, 32, ROT // 2]) for i in range(4)]
    pos_i = rsb("positions", [P, 2], I32)
    lam_in = rsb("lambda_in", [P, 4, HD])
    subln = rsb("subln_g", [P, P])
    freq = rsb("frequencies", [P, ROT // 2])
    angles = rsb("angles", [P, 8, 2, ROT // 2])
    dve.wait(*fresh)
    act.wait(*fresh)
    m_pos = small(pool, pos_i[:, :], w["positions_2"][0].rearrange("(t p) -> p t", p=P), *fresh,
                  allow_slow_non_contiguous=True)
    m_lam = [small(pool, lam_in[:, i, :], w[k].broadcast_to([P, HD]))
             for i, k in enumerate(("b_lam_q1_2", "b_lam_k1_2", "b_lam_q2_2", "b_lam_k2_2"))]
    m_sub = small(pool, subln[:, :], w["b_subln_g_2"].broadcast_to([P, P]))
    m_frq = small(pool, freq[:, :], w["frequencies"].broadcast_to([P, ROT // 2]))
    turn_p = load_p(1)

    lam_sum, lam_exp, minus_lam = stat(2), stat(2), stat()
    v = tt(lam_in[:, 0, :], lam_in[:, 0, :], lam_in[:, 1, :], ALU.mult, m_lam[0], m_lam[1])
    v2 = tt(lam_in[:, 2, :], lam_in[:, 2, :], lam_in[:, 3, :], ALU.mult, m_lam[2], m_lam[3])
    v = reduce(lam_sum[:, 0:1], lam_in[:, 0, :], ALU.add, v)
    v = reduce(lam_sum[:, 1:2], lam_in[:, 2, :], ALU.add, v2)
    a = act_fn(lam_exp, lam_sum, ACT.Exp, v)
    v = tt(minus_lam, lam_exp[:, 1:2], lam_exp[:, 0:1], ALU.subtract, a)
    lam_ready = ts(minus_lam, minus_lam, lambda_init, None, ALU.subtract, None, v)
    sub_ready = ts(subln[:, :], subln[:, :], 1.0 - lambda_init, None, ALU.mult, None, m_sub)

    two_pi = 2 * math.pi
    part1 = 6.28125
    part2 = float(np.float32(np.round((two_pi - part1) * 2 ** 20) / 2 ** 20))
    part3 = float(np.float32(two_pi - part1 - part2))
    big = 1.5 * 2.0 ** 23
    pos_f = stat(2)
    v = dve.run(lambda e: e.tensor_copy(pos_f, pos_i[:, :]), m_pos)
    ang, turns, cut, rest = (angles[:, i, :, :] for i in range(4))
    sin_, cos_ = angles[:, 4, :, :], angles[:, 5, :, :]
    for t in TILES:
        v0 = ts(ang[:, t, :], freq[:, :], pos_f[:, t:t + 1], None, ALU.mult, None, v, m_frq)
    trig_ready = []
    for shift, o in ((0.0, sin_), (0.25, cos_)):
        v1 = ts(turns, ang, 1.0 / two_pi, shift, ALU.mult, ALU.add, v0, *trig_ready)
        v1 = ts(turns, turns, big, None, ALU.add, None, v1)
        v1 = ts(turns, turns, big, None, ALU.subtract, None, v1)
        v1 = stt(rest, turns, -part1, ang, ALU.mult, ALU.add, v1)
        v1 = stt(rest, turns, -part2, rest, ALU.mult, ALU.add, v1)
        v1 = stt(rest, turns, -part3, rest, ALU.mult, ALU.add, v1)
        v1 = ts(rest, rest, two_pi * shift, None, ALU.add, None, v1)
        limit = 3.1415925
        v1 = ts(rest, rest, limit, -limit, ALU.min, ALU.max, v1)
        trig_ready = [act_fn(o, rest, ACT.Sin, v1)]

    kv_marks, rot_free = [], []
    qk_marks = {t: [] for t in TILES}
    turned_qk = []

    def qkv(b, t, bank, mark):
        i = b.name[1]
        if i >= 4:
            a = act_fn(vv[:, t, (i - 4) * COLS:(i - 3) * COLS], bank[:, :], ACT.Copy, mark)
            banks.give(bank, a)
            kv_marks.append(a)
            return
        a = act_fn(qk[:, t, i * COLS:(i + 1) * COLS], bank[:, :], ACT.Copy, mark)
        banks.give(bank, a)
        qk_marks[t].append(a)
        if i < 3:
            return
        x = qk[:, t, :].rearrange("p (g d) -> p g d", d=HD)
        x1, x2 = x[:, :, 0:ROT // 2], x[:, :, ROT // 2:ROT]
        c = cos_[:, t, :].unsqueeze(1).broadcast_to([P, 32, ROT // 2])
        s = sin_[:, t, :].unsqueeze(1).broadcast_to([P, 32, ROT // 2])
        tt(rot[0][:, :, :], x1, c, ALU.mult, *trig_ready, *qk_marks[t], *rot_free)
        tt(rot[1][:, :, :], x2, s, ALU.mult)
        tt(rot[2][:, :, :], x2, c, ALU.mult)
        v = tt(rot[3][:, :, :], x1, s, ALU.mult)
        tt(x1, rot[0][:, :, :], rot[1][:, :, :], ALU.subtract, v)
        v = tt(x2, rot[2][:, :, :], rot[3][:, :, :], ALU.add)
        rot_free[:] = [v]

        def turn_it():
            for to, c0, scale in ((q_t, 0, HD ** -0.5), (k_t, D, 1.0)):
                for g in range(0, HEADS, 4):
                    bank, free = banks.take()
                    for j in range(4):
                        last = turn(bank[:, j * P:(j + 1) * P], qk[:, t, c0 + (g + j) * P:c0 + (g + j + 1) * P],
                                    v, *free)
                    a = act_fn(to[:, g:g + 4, P * t:P * t + P], bank[:, :].rearrange("p (g n) -> p g n", n=P),
                               ACT.Copy, last, scale=scale)
                    banks.give(bank, a)
                    turned_qk.append(a)

        defer(turn_it, 3)

    defer(turn_p, 4)
    products(stages["qkv"], x_t, qkv)
    flush()

    def diff_scores(t, hd):
        keys = P * (t + 1)
        bank, free = banks.take()
        last = free[0] if free else ident_set
        for c in range(2):
            b = HD * c
            mm_quiet(bank[:, c * SEQ:c * SEQ + keys], q_t[b:b + HD, hd, P * t:P * t + P], k_t[b:b + HD, hd, 0:keys],
                     True, False, *turned_qk, *free, last)
            last = mm(bank[:, c * SEQ + keys - P:c * SEQ + keys], ident[:, :], causal[:, :], False, True)
        mx, neg, total, inv = stat(2), stat(2), stat(2), stat(2)
        got = bank[:, :].rearrange("p (c k) -> p c k", c=2)
        v = reduce(mx, got[:, :, 0:keys], ALU.max, last)
        v = ts(neg, mx, -1.0, None, ALU.mult, None, v)
        pr, free = prob2.take()
        for c in range(2):
            a = act_fn(pr[:, c, 0:keys], got[:, c, 0:keys], ACT.Exp, v, *free, bias=neg[:, c:c + 1],
                       accum_out=total[:, c:c + 1])
        banks.give(bank, a)
        v = dve.run(lambda e: e.reciprocal(inv, total), a)
        w1 = stat()
        v = tt(w1, inv[:, 1:2], minus_lam, ALU.mult, v, lam_ready)
        v = ts(pr[:, 1, 0:keys], pr[:, 1, 0:keys], w1, None, ALU.mult, None, v)
        df, free = diff.take()
        v = stt(df[:, 0:keys], pr[:, 0, 0:keys], inv[:, 0:1], pr[:, 1, 0:keys], ALU.mult, ALU.add, v, *free)
        prob2.give(pr, v)
        return df, v

    def turn_diff(df, mark, t):
        bank, free = banks.take()
        for i in range(t + 1):
            last = turn(bank[:, i * P:(i + 1) * P], df[:, i * P:(i + 1) * P], mark, *free)
        diff.give(df, last)
        dt_, free = diff_t.take()
        a = act_fn(dt_[:, 0:t + 1, :], bank[:, 0:(t + 1) * P].rearrange("p (k n) -> p k n", n=P), ACT.Copy, last, *free)
        banks.give(bank, a)
        return dt_, a

    for t in TILES:
        scored, turned = {}, {}
        o_bank, o_marks = {}, {}
        for i in range(HEADS + 2):
            if i < HEADS:
                scored[i] = diff_scores(t, i)
            if 1 <= i <= HEADS:
                turned[i - 1] = turn_diff(*scored.pop(i - 1), t)
            if i >= 2:
                hd = i - 2
                if hd % 4 == 0:
                    o_bank[hd // 4], o_free = banks.take()
                dt_, mark = turned.pop(hd)
                for k in range(t + 1):
                    last = mm(o_bank[hd // 4][:, (hd % 4) * P:(hd % 4 + 1) * P], dt_[:, k, :],
                              vv[:, k, hd * P:(hd + 1) * P], k == 0, k == t, mark, *o_free, *kv_marks)
                diff_t.give(dt_, last)
                if hd % 4 == 3:
                    g = hd // 4
                    got = o_bank[g][:, :].rearrange("p (h d) -> p h d", d=P)
                    sq, free = temps.take()
                    a = act_fn(sq[:, :], o_bank[g][:, :], ACT.Square, last, *free)
                    ss, r = stat(4), stat(4)
                    v = reduce(ss, sq[:, :].rearrange("p (h d) -> p h d", d=P), ALU.add, a)
                    temps.give(sq, v)
                    p = rsqrt_mean(r, ss, P, SUBLN_EPS, v)
                    to = row[t][:, g * COLS:(g + 1) * COLS].rearrange("p (h d) -> p h d", d=P)
                    v = tt(to, got, r.unsqueeze(2).broadcast_to([P, 4, P]), ALU.mult, p, *row_free[t])
                    banks.give(o_bank[g], v)
                    v = tt(to, to, subln[:, :].unsqueeze(1).broadcast_to([P, 4, P]), ALU.mult, v, sub_ready)
        x_t.forget(t)
        row_free[t] = (turn_split(row[t], t, KC, x_t, 0, v),)

    attn_post, ffn_pre2 = Gain(13, 2), Gain(14, 2)
    products(stages["attn_out"], x_t,
             lambda b, t, bank, mark: post_norm_part(t, b.name[1], bank[:, :], mark, bank, attn_post,
                                                     lambda t: pre_norm(t, ffn_pre2)))
    region.close()

    region = ExitStack()
    ple_pre2 = Gain(16, 2)
    mlp(1, region, lambda t: pre_norm(t, ple_pre2))
    region.close()

    stored = []

    def store(t):
        stored.append(small(sp, out[0, t * P:(t + 1) * P, :], h[t], h_ready[t]))

    ple(1, store)
    flush()
    sp.wait(*stored)

    with hold:
        with nc.Block() as block:
            @block.sync
            def _(engine):
                sp.play(engine)

            @block.scalar
            def _(engine):
                act.play(engine)

            @block.vector
            def _(engine):
                dve.play(engine)

            @block.gpsimd
            def _(engine):
                pool.play(engine)

            @block.tensor
            def _(engine):
                pe.play(engine)


_INS = [
    "x", "meta_tokens", "rel_bias_table", "ffn1_norm", "ffn1_w_in", "ffn1_w_out", "mix_norm", "w_in",
    "forget_bias", "fox_q_norm", "fox_k_norm", "swa_q_norm", "swa_k_norm", "swa_sinks", "w_branch_fox",
    "w_branch_swa", "w_out", "ffn2_norm", "ffn2_w_in", "ffn2_w_out", "p_2", "positions_2", "g_mix_pre_2",
    "g_mix_post_2", "g_ffn_pre_2", "g_ffn_post_2", "g_ple_pre_2", "g_ple_post_2", "a_w_in_2", "a_ln_g_2",
    "a_ln_b_2", "a_w_s_2", "a_b_s_2", "a_w_out_2", "b_w_qkv_2", "b_lam_q1_2", "b_lam_k1_2", "b_lam_q2_2",
    "b_lam_k2_2", "b_subln_g_2", "b_w_o_2", "f_w_up_2", "f_w_down_2", "ple_w_proj_2", "ple_w_gate_2",
    "ple_b_gate_2",
]


def kernel(**inputs):
    import concourse.bacc as bacc
    from concourse.bass_utils import run_bass_kernel_spmd

    nc = bacc.Bacc("TRN2", target_bir_lowering=False, num_devices=1)
    arrays, aps = {}, {}
    given = {name: np.ascontiguousarray(inputs[name]) for name in _INS}
    given["bias_selector"] = bias_selector()
    given["frequencies"] = rotary_frequencies()[None, :]
    for name, a in given.items():
        arrays[f"in_{name}"] = a
        aps[name] = nc.dram_tensor(f"in_{name}", a.shape, mybir.dt.from_np(a.dtype), kind="ExternalInput").ap()
    out = nc.dram_tensor("out_0", (1, SEQ, D), F32, kind="ExternalOutput").ap()
    two_blocks(nc, aps, out)
    r = run_bass_kernel_spmd(nc, [arrays], core_ids=[0])
    return r.results[0]["out_0"]
```

```python
import math
from collections import deque
from contextlib import ExitStack

import numpy as np

import concourse.bass as bass
from concourse import mybir

F32 = mybir.dt.float32
F32R = mybir.dt.float32r
I32 = mybir.dt.int32
ALU = mybir.AluOpType
ACT = mybir.ActivationFunctionType
X = mybir.AxisListType.X

P = 128
D = 1024
SEQ = 256
N_META = 16
D_FF = 2816
D_FF_2 = 4096
HEADS = 8
HD = 64
SWA_KV = 2
WINDOW = 128
N_BUCKETS = 32
MAX_DISTANCE = 128
PLE_DIM = 256
ROT = 16
ROPE_THETA = 500000.0
NEG = -1e30
EPS = 1e-6
LN_EPS = 1e-5
SUBLN_EPS = 1e-5
META = 2
TILES = (0, 1)
ALL_TILES = (0, 1, META)
ROWS = (P, P, N_META)
FIRST_TOKEN = (0, P, SEQ)
KEYS = N_META + SEQ
FOX_D = HD + 2
KC = D // P
COLS = 512
PIECE_K = 2
RAW_SLOTS = 4
SPLIT_SLOTS = 6

FOX_W = HEADS * HD
KV_W = SWA_KV * HD
C_QA, C_KA, C_VA = 0, FOX_W, 2 * FOX_W
C_FA = 3 * FOX_W
C_QB = C_FA + HEADS
C_KB = C_QB + FOX_W
C_GA = C_KB + 2 * KV_W
C_GB = C_GA + D

U_WINDOW = 3 * P - 1
U_META = P + N_META - 1
U_ALL = U_WINDOW + 2 * U_META


def bias_selector():
    distance = np.concatenate([2 * P - 1 - np.arange(U_WINDOW), P + N_META - 1 - np.arange(U_META),
                               2 * P + N_META - 1 - np.arange(U_META)])
    seen = np.ones(U_ALL, bool)
    seen[:U_WINDOW] = (distance[:U_WINDOW] >= 0) & (distance[:U_WINDOW] < WINDOW)
    half = N_BUCKETS // 2
    n = np.maximum(distance, 0)
    far = np.log(np.maximum(n, 1).astype(np.float32) / half) / math.log(MAX_DISTANCE / half) * half
    bucket = np.where(n < half, n, np.minimum(half + far.astype(np.int32), N_BUCKETS - 1))
    out = np.zeros((N_BUCKETS + 1, U_ALL), np.float32)
    out[bucket[seen], np.nonzero(seen)[0]] = 1.0
    out[N_BUCKETS, ~seen] = NEG
    return out


def rotary_frequencies():
    return (ROPE_THETA ** (-(np.arange(0, ROT, 2, dtype=np.float32) / ROT))).astype(np.float32)


class Queue:

    def __init__(self, sem):
        self.sem, self.count, self.steps, self.reached = sem, 0, [], {}

    def wait(self, *marks):
        for sem, value in marks:
            if self.reached.get(sem.name, 0) < value:
                self.reached[sem.name] = value
                self.steps.append(lambda e, sem=sem, value=value: e.wait_ge(sem, value))

    def run(self, make, *marks):
        self.wait(*marks)
        self.count += 1
        self.steps.append(lambda e: make(e).then_inc(self.sem, 1))
        return (self.sem, self.count)

    def quiet(self, make, *marks):
        self.wait(*marks)
        self.steps.append(make)

    def dma(self, out, in_, sem, n, *marks, **kw):
        self.wait(*marks)
        self.steps.append(lambda e: e.dma_start(out, in_, **kw).then_inc(sem, 16))
        return (sem, 16 * n)

    def play(self, engine):
        for step in self.steps:
            step(engine)


class Slots:

    def __init__(self, buffers):
        self.free = deque((b, ()) for b in buffers)

    def take(self):
        return self.free.popleft()

    def give(self, buffer, *marks):
        self.free.append((buffer, marks))


class Block:

    def __init__(self, matrix, first, n, tiles=TILES, name=None):
        self.matrix, self.c0, self.n, self.tiles, self.name = matrix, first, n, tiles, name
        self.pieces = matrix.shape[0] // (P * PIECE_K)
        self.at = None

    def source(self, j):
        rows = self.matrix[j * PIECE_K * P:(j + 1) * PIECE_K * P, self.c0:self.c0 + self.n]
        return rows.rearrange("(c p) n -> p c n", p=P)


class Operand:

    def __init__(self, hi, lo):
        self.hi, self.lo, self.ready, self.free, self.scale = hi, lo, {}, {}, {}

    def forget(self, t):
        for key in [key for key in self.ready if key[0] == t]:
            del self.ready[key]


def column_blocks(matrix, width, tiles=TILES, name=None):
    return [Block(matrix, c, min(COLS, width - c), tiles, (name, c // COLS)) for c in range(0, width, COLS)]


def plan(w):

    def glu(w_in, w_out, tiles):
        up = []
        for c in range(0, D_FF, COLS):
            n = min(COLS, D_FF - c)
            up += [Block(w_in, c, n, tiles, ("gate", c // COLS)), Block(w_in, D_FF + c, n, tiles, ("up", c // COLS))]
        return up, column_blocks(w_out, D, tiles)

    s = {}
    s["ffn1_in"], s["ffn1_out"] = glu(w["ffn1_w_in"][0], w["ffn1_w_out"][0], ALL_TILES)
    w_in = w["w_in"][0]
    s["mix_in"] = [Block(w_in, C_VA, FOX_W, ALL_TILES, "va"), Block(w_in, C_KA, FOX_W, ALL_TILES, "ka"),
                   Block(w_in, C_QA, FOX_W, TILES, "qa"),
                   Block(w_in, C_KB, 2 * KV_W, ALL_TILES, "kvb"), Block(w_in, C_QB, FOX_W, TILES, "qb")]
    s["gates"] = [Block(w_in, C_GA + COLS * i, COLS, TILES, ("gates", i)) for i in range(4)]
    s["branch"] = [b for i in range(2) for b in (Block(w["w_branch_fox"][0], COLS * i, COLS, TILES, ("fox", i)),
                                                 Block(w["w_branch_swa"][0], COLS * i, COLS, TILES, ("swa", i)))]
    s["mix_out"] = column_blocks(w["w_out"][0], D)
    s["ffn2_in"], s["ffn2_out"] = glu(w["ffn2_w_in"][0], w["ffn2_w_out"][0], TILES)
    z = column_blocks(w["a_w_in_2"][0], 2 * D)
    s["gmlp_in"] = z[2:] + z[:2]
    s["gmlp_out"] = column_blocks(w["a_w_out_2"][0], D)
    q0, q1, k0, k1, v0, v1 = column_blocks(w["b_w_qkv_2"][0], 3 * D)
    s["qkv"] = [v0, v1, k0, q0]
    s["qkv_rest"] = [k1, q1]
    s["attn_out"] = column_blocks(w["b_w_o_2"][0], D)
    for i in range(2):
        s["mlp_in", i] = column_blocks(w["f_w_up_2"][i], D_FF_2)
        s["mlp_out", i] = column_blocks(w["f_w_down_2"][i], D)
        s["ple", i] = [b for c in range(2) for b in (Block(w["ple_w_gate_2"][i], COLS * c, COLS, TILES, ("gate", c)),
                                                     Block(w["ple_w_proj_2"][i], COLS * c, COLS, TILES, ("proj", c)))]
    order = ["ffn1_in", "ffn1_out", "mix_in", "gates", "branch", "mix_out", "ffn2_in", "ffn2_out",
             "gmlp_in", "gmlp_out", ("mlp_in", 0), ("mlp_out", 0), ("ple", 0),
             "qkv", "qkv_rest", "attn_out", ("mlp_in", 1), ("mlp_out", 1), ("ple", 1)]
    stream = []
    for name in order:
        for b in s[name]:
            b.at = len(stream)
            stream += [(b, j) for j in range(b.pieces)]
    return s, stream


def two_blocks(nc, w, out):
    stages, stream = plan(w)
    hold = ExitStack()

    def sb(name, shape, dt=F32, where=hold):
        return where.enter_context(nc.sbuf_tensor(name, shape, dt))

    def sem(name):
        return hold.enter_context(nc.semaphore(name))

    pe, act, dve, pool, sp = (Queue(sem(n)) for n in ("pe_done", "act_done", "dve_done", "pool_done", "sp_done"))
    last_square = []

    raw = sb("weights_raw", [P, RAW_SLOTS, PIECE_K, COLS])
    w_hi = sb("weights_hi", [P, SPLIT_SLOTS, PIECE_K, COLS], F32R)
    w_lo = sb("weights_lo", [P, SPLIT_SLOTS, PIECE_K, COLS], F32R)
    h_main = sb("h", [P, 2, D])
    h_meta = sb("h_meta", [N_META, D])
    row_main = sb("row", [P, 2, D])
    row_meta = sb("row_meta", [N_META, D])
    x_t = Operand(sb("x_t_hi", [P, KC, KEYS], F32R), sb("x_t_lo", [P, KC, KEYS], F32R))
    p_rows = sb("p_rows", [P, 2, PLE_DIM])
    p_t = Operand(sb("p_t_hi", [P, PLE_DIM // P, SEQ], F32R), sb("p_t_lo", [P, PLE_DIM // P, SEQ], F32R))
    gains_sb = sb("gains", [P, 3, D])
    temps = Slots([sb(f"temp{i}", [P, HEADS * FOX_D]) for i in range(4)])
    junk = sb("squares", [P, COLS])
    stats = sb("stats", [P, 1024])
    ident = sb("identity", [P, P])
    flip = sb("anti_identity", [P, P])
    causal = sb("causal_neg", [P, P])
    upto = sb("upto_and_ones", [P, 2 * P])
    ident_r = sb("identity_r", [P, P], F32R)
    causal_r = sb("causal_neg_r", [P, P], F32R)
    minus_half = sb("minus_half", [P, 16])
    fa_raw = sb("w_fa", [P, KC, HEADS])
    fa_hi = sb("w_fa_hi", [P, KC, HEADS], F32R)
    fa_lo = sb("w_fa_lo", [P, KC, HEADS], F32R)
    head_gains = sb("head_gains", [P, 4, HD])
    forget_b = sb("forget_bias", [P, HEADS])
    sinks = sb("sinks", [P, HEADS])
    banks = Slots([hold.enter_context(nc.psum_tensor(f"bank{i}", [P, 512], F32)) for i in range(8)])

    h = [h_main[:, 0, :], h_main[:, 1, :], h_meta[:, :]]
    row = [row_main[:, 0, :], row_main[:, 1, :], row_meta[:, :]]
    h_ready = {}
    row_free = {t: () for t in ALL_TILES}
    used = [0]

    def stat(n=1):
        used[0] += n
        assert used[0] <= 1024
        return stats[:, used[0] - n:used[0]]

    def mm(o, lhs, rhs, start, stop, *marks):
        return pe.run(lambda e: e.matmul(o, lhs, rhs, start=start, stop=stop), *marks)

    def mm_quiet(o, lhs, rhs, start, stop, *marks):
        pe.quiet(lambda e: e.matmul(o, lhs, rhs, start=start, stop=stop), *marks)

    def turn(o, i, *marks):
        n = i.shape[0]
        return pe.run(lambda e: e.transpose(o, i, ident[0:n, 0:n]), *marks)

    def act_fn(o, i, f, *marks, **kw):
        return act.run(lambda e: e.activation(o, i, f, **kw), *marks)

    def tt(o, a, b, op, *marks, q=dve):
        return q.run(lambda e: e.tensor_tensor(o, a, b, op), *marks)

    def ts(o, a, s1, s2, op0, op1, *marks, q=dve):
        return q.run(lambda e: e.tensor_scalar(o, a, s1, s2, op0, op1) if op1 is not None
                     else e.tensor_scalar(o, a, s1, None, op0), *marks)

    def stt(o, a, s, b, op0, op1, *marks):
        return dve.run(lambda e: e.scalar_tensor_tensor(out=o, in0=a, scalar=s, in1=b, op0=op0, op1=op1), *marks)

    def reduce(o, a, op, *marks):
        return dve.run(lambda e: e.tensor_reduce(o, a, X, op), *marks)

    def rsqrt_mean(o, total, n, eps, *marks):
        m = stat(total.shape[1])[0:total.shape[0], :]
        a = ts(m, total, 1.0 / n, eps, ALU.mult, ALU.add, *marks, q=pool)
        return tt(o, m, minus_half[0:total.shape[0], 0:total.shape[1]], ALU.pow, a, half_set, q=pool)

    later = deque()

    def defer(fn, units=3):
        later.append([units, fn])

    chores = deque()

    def chore():
        try:
            next(chores[0])
        except StopIteration:
            chores.popleft()

    def tick():
        for item in later:
            item[0] -= 1
        while later and later[0][0] <= 0:
            later.popleft()[1]()
        if chores:
            chore()

    def flush():
        while later:
            later.popleft()[1]()

    def finish_chores():
        while chores:
            chore()

    raw_sems = [sem(f"raw{i}_loaded") for i in range(RAW_SLOTS)]
    loads, splits, released = [], [], []

    def load_next():
        n = len(loads)
        b, j = stream[n]
        marks = splits[n - RAW_SLOTS] if n >= RAW_SLOTS else ()
        loads.append(sp.dma(raw[:, n % RAW_SLOTS, :, 0:b.n], b.source(j), raw_sems[n % RAW_SLOTS],
                            n // RAW_SLOTS + 1, *marks))

    def split_next():
        n = len(splits)
        b, j = stream[n]
        source = raw[:, n % RAW_SLOTS, :, 0:b.n]
        hi, lo = w_hi[:, n % SPLIT_SLOTS, :, 0:b.n], w_lo[:, n % SPLIT_SLOTS, :, 0:b.n]
        former = (released[n - SPLIT_SLOTS],) if n >= SPLIT_SLOTS else ()
        a = act_fn(hi, source, ACT.Copy, loads[n], *former)
        v = tt(lo, source, hi.bitcast(F32), ALU.subtract, a)
        splits.append((a, v))
        if len(loads) < len(stream):
            load_next()

    def advance():
        while len(splits) < min(len(released) + SPLIT_SLOTS, len(stream)):
            split_next()

    def release(mark):
        released.append(mark)
        advance()

    gain_order = [w["ffn1_norm"][0:1], w["mix_norm"][0:1], w["ffn2_norm"][0:1],
                  w["g_mix_pre_2"][0:1], w["a_ln_g_2"][0:1], w["a_ln_b_2"][0:1], w["g_mix_post_2"][0:1],
                  w["g_ffn_pre_2"][0:1], w["g_ffn_post_2"][0:1], w["g_ple_pre_2"][0:1], w["ple_b_gate_2"][0:1],
                  w["g_ple_post_2"][0:1],
                  w["g_mix_pre_2"][1:2], w["g_mix_post_2"][1:2],
                  w["g_ffn_pre_2"][1:2], w["g_ffn_post_2"][1:2], w["g_ple_pre_2"][1:2], w["ple_b_gate_2"][1:2],
                  w["g_ple_post_2"][1:2]]
    gain_sems = [sem(f"gain{i}_loaded") for i in range(3)]
    gain_marks = []

    def load_gain(*marks):
        n = len(gain_marks)
        if n < len(gain_order):
            gain_marks.append(sp.dma(gains_sb[:, n % 3, :], gain_order[n].broadcast_to([P, D]), gain_sems[n % 3], n // 3 + 1, *marks))

    class Gain:

        def __init__(self, n, uses):
            self.n, self.left, self.marks = n, uses, []

        def ap(self, rows, c0=0, n=D):
            return gains_sb[0:rows, self.n % 3, c0:c0 + n]

        def mark(self):
            return gain_marks[self.n]

        def done(self, mark):
            self.marks.append(mark)
            self.left -= 1
            if not self.left:
                load_gain(*self.marks)

    small_sems = [0]

    def small(q, o, i, *marks, **kw):
        small_sems[0] += 1
        return q.dma(o, i, sem(f"small{small_sems[0]}"), 1, *marks, **kw)

    h_ready[0] = small(sp, h_main[:, 0, :], w["x"][0, 0:P, :])
    load_gain()
    h_ready[1] = small(sp, h_main[:, 1, :], w["x"][0, P:SEQ, :])
    h_ready[META] = small(sp, h_meta[:, :], w["meta_tokens"])
    for _ in range(RAW_SLOTS):
        load_next()
    load_gain()
    load_gain()

    m_id = pool.run(lambda e: e.memset(ident[:, :], 0.0))
    half_set = pool.run(lambda e: e.memset(minus_half[:, :], -0.5))

    def select(o, i, base, cm, pattern, cmp, fill, *marks):
        return pool.run(lambda e: e.affine_select(out=o, in_=i, compare_op=cmp, fill=fill, base=base,
                                                  pattern=pattern, channel_multiplier=cm), *marks)

    ident_set = select(ident[:, :], ident[:, :], 0, 1, [[-1, P]], ALU.not_equal, 1.0, m_id)
    a = pool.run(lambda e: e.memset(flip[:, :], 0.0))
    flip_set = select(flip[:, :], flip[:, :], -(P - 1), 1, [[1, P]], ALU.not_equal, 1.0, a)
    a = pool.run(lambda e: e.memset(causal[:, :], 0.0))
    causal_set = select(causal[:, :], causal[:, :], 0, 1, [[-1, P]], ALU.is_ge, NEG, a)
    a = pool.run(lambda e: e.memset(upto[:, :], 1.0))
    upto_set = select(upto[:, 0:P], upto[:, 0:P], 0, -1, [[1, P]], ALU.is_ge, 0.0, a)

    m_fa = small(pool, fa_raw[:, :, :], w["w_in"][0][:, C_FA:C_FA + HEADS].rearrange("(c p) n -> p c n", p=P))
    m_fb = small(pool, forget_b[:, :], w["forget_bias"].broadcast_to([P, HEADS]))
    m_sink = small(pool, sinks[:, :], w["swa_sinks"].broadcast_to([P, HEADS]))
    m_hg = [small(pool, head_gains[:, i, :], w[k].broadcast_to([P, HD]))
            for i, k in enumerate(("fox_q_norm", "fox_k_norm", "swa_q_norm", "swa_k_norm"))]

    advance()

    masks_ready = [act_fn(o[:, :], i[:, :], ACT.Copy, m) for o, i, m in
                   ((ident_r, ident, ident_set), (causal_r, causal, causal_set))]

    def turn_split(source, t, chunks, to, first_chunk, *marks):
        n, c0 = ROWS[t], FIRST_TOKEN[t]
        last = None
        for c in range(0, chunks, 4):
            k = min(4, chunks - c)
            bank, free = banks.take()
            for i in range(k):
                last = turn(bank[:, i * n:(i + 1) * n], source[0:n, (c + i) * P:(c + i + 1) * P], *marks, *free, ident_set)
            got = bank[:, 0:k * n].rearrange("p (c n) -> p c n", n=n)
            hi = to.hi[:, first_chunk + c:first_chunk + c + k, c0:c0 + n]
            lo = to.lo[:, first_chunk + c:first_chunk + c + k, c0:c0 + n]
            a = act_fn(hi, got, ACT.Copy, last, *to.free.get(t, ()))
            v = tt(lo, got, hi.bitcast(F32), ALU.subtract, a)
            banks.give(bank, v)
            for i in range(k):
                to.ready[t, first_chunk + c + i] = (a, v)
        return last

    def products(blocks, x, epilogue, lead=SPLIT_SLOTS, tail=SPLIT_SLOTS):
        pieces = [(b, j) for b in blocks for j in range(b.pieces)]
        held = {}

        def go(b, j, t):
            if t not in b.tiles:
                return
            operand, k0 = x(b)
            if (b, t) not in held:
                held[b, t], free = banks.take()
                pe.wait(*free)
            n, c0, slot = ROWS[t], FIRST_TOKEN[t], (b.at + j) % SPLIT_SLOTS
            o = held[b, t][0:n, 0:b.n]
            mark = None
            for i in range(PIECE_K):
                k = k0 + j * PIECE_K + i
                if (t, k) not in operand.ready:
                    flush()
                while (t, k) not in operand.ready:
                    chore()
                xh, xl = operand.hi[:, k, c0:c0 + n], operand.lo[:, k, c0:c0 + n]
                wh, wl = w_hi[:, slot, i, 0:b.n], w_lo[:, slot, i, 0:b.n]
                last = j == b.pieces - 1 and i == PIECE_K - 1
                mm_quiet(o, xh, wh, j == 0 and i == 0, False, *operand.ready[t, k], *splits[b.at + j])
                mm_quiet(o, xh, wl, False, False)
                if i == PIECE_K - 1:
                    mark = mm(o, xl, wh, False, last)
                else:
                    mm_quiet(o, xl, wh, False, last)
            operand.free[t] = (mark,)
            if t == b.tiles[-1]:
                release(mark)
            if j == b.pieces - 1:
                epilogue(b, t, held.pop((b, t)), mark)
            tick()

        lead = min(lead, len(pieces))
        cut = max(lead, len(pieces) - tail)
        for t in ALL_TILES:
            for b, j in pieces[:lead]:
                go(b, j, t)
        for b, j in pieces[lead:cut]:
            for t in b.tiles:
                go(b, j, t)
        for t in ALL_TILES:
            for b, j in pieces[cut:]:
                go(b, j, t)

    def products_by_feature(blocks, epilogue):
        for b in blocks:
            held = []
            for f in range(b.n // P):
                bank, free = banks.take()
                held.append((bank, free))
            for j in range(b.pieces):
                slot = (b.at + j) % SPLIT_SLOTS
                for f, (bank, free) in enumerate(held):
                    if j == 0:
                        pe.wait(*free)
                    for i in range(PIECE_K):
                        k = j * PIECE_K + i
                        xh, xl = x_t.hi[:, k, :], x_t.lo[:, k, :]
                        wh, wl = (s[:, slot, i, f * P:(f + 1) * P] for s in (w_hi, w_lo))
                        pe.wait(*splits[b.at + j], *[m for t in ALL_TILES for m in x_t.ready[t, k]])
                        first, last = k == 0, k == KC - 1
                        mm_quiet(bank[:, 0:KEYS], wh, xh, first, False)
                        mm_quiet(bank[:, 0:KEYS], wh, xl, False, False)
                        mark = mm(bank[:, 0:KEYS], wl, xh, False, last)
                    if j == b.pieces - 1:
                        epilogue(b, f, bank, mark)
                    if f % 2:
                        tick()
                release(mark)
                for t in ALL_TILES:
                    x_t.free[t] = (mark,)

    def square_sum(source, *marks):
        n, width = source.shape
        ss = stat()[0:n, :]
        a = act_fn(junk[0:n, 0:width], source, ACT.Square, *marks, *last_square, accum_out=ss)
        last_square[:] = [a]
        return ss, a

    def rsqrt_of_halves(o, sums, eps):
        total = stat()[0:o.shape[0], :]
        p = tt(total, sums[0][0], sums[1][0], ALU.add, sums[0][1], sums[1][1], q=pool)
        return rsqrt_mean(o, total, D, eps, p)

    halves = (slice(0, COLS), slice(COLS, D))

    def pre_norm(t, gain, units=4):
        n = ROWS[t]
        marks, sums = [], []
        x_t.forget(t)
        for half in range(2):
            s = halves[half]
            marks.append(tt(row[t][0:n, s], h[t][0:n, s], gain.ap(n, half * COLS, COLS), ALU.mult,
                            h_ready[t][half], gain.mark(), *row_free[t]))
        gain.done(marks[1])
        r = stat()[0:n, :]
        sums = [square_sum(h[t][0:n, s], h_ready[t][i]) for i, s in enumerate(halves)]
        x_t.scale[t] = (r, rsqrt_of_halves(r, sums, EPS))

        def turn_it():
            for half in range(2):
                last = turn_split(row[t][:, halves[half]], t, 4, x_t, 4 * half, marks[half])
            row_free[t] = (last,)

        defer(turn_it, units)

    def pre_norm_whole(t, gain, units=0):
        n = ROWS[t]
        r = stat()[0:n, :]
        x_t.forget(t)
        sums = [square_sum(h[t][0:n, s], h_ready[t][i]) for i, s in enumerate(halves)]
        p = rsqrt_of_halves(r, sums, EPS)
        marks = [stt(row[t][0:n, s], h[t][0:n, s], r, gain.ap(n, i * COLS, COLS), ALU.mult, ALU.mult, p,
                     gain.mark(), *row_free[t]) for i, s in enumerate(halves)]
        gain.done(marks[1])

        def turn_it():
            for half in range(2):
                last = turn_split(row[t][:, halves[half]], t, 4, x_t, 4 * half, marks[half])
            row_free[t] = (last,)

        defer(turn_it, units)

    parts = {}

    def post_norm_part(t, half, source, mark, bank, gain, then):
        ss, a = square_sum(source, mark)
        tmp, free = temps.take()
        v = tt(tmp[:, 0:COLS], source, gain.ap(P, half * COLS, COLS), ALU.mult, a, gain.mark(), *free)
        if bank is not None:
            banks.give(bank, v)
        parts.setdefault(t, []).append((half, tmp, v, (ss, a)))
        if len(parts[t]) < 2:
            return
        both = parts.pop(t)
        r = stat()
        p = rsqrt_of_halves(r, [x[3] for x in both], EPS)
        ready = {}
        for half, tmp, v, _ in both:
            to = h[t][:, halves[half]]
            ready[half] = stt(to, tmp[:, 0:COLS], r, to, ALU.mult, ALU.add, p, v)
            temps.give(tmp, ready[half])
        gain.done(v)
        h_ready[t] = (ready[0], ready[1])
        then(t)

    def glu(name, region, then):
        hid = Operand(sb(f"{name}_hid_hi", [P, D_FF // P, KEYS], F32R, region),
                      sb(f"{name}_hid_lo", [P, D_FF // P, KEYS], F32R, region))
        fresh = region_marks()
        held = {}

        def hidden(b, t, bank, mark):
            n = ROWS[t]
            if b.name[0] == "gate":
                buf, free = temps.take()
                r, scaled = x_t.scale.get(t, (1.0, mark))
                a = act_fn(buf[0:n, 0:b.n], bank[0:n, 0:b.n], ACT.Silu, mark, scaled, *free, scale=r)
                held[t] = (buf, a)
                banks.give(bank, a)
                return
            buf, a = held.pop(t)
            r, scaled = x_t.scale.get(t, (1.0, mark))
            v = stt(buf[0:n, 0:b.n], bank[0:n, 0:b.n], r, buf[0:n, 0:b.n], ALU.mult, ALU.mult, mark, a, scaled)
            banks.give(bank, v)

            def turn_it():
                act.wait(*fresh)
                dve.wait(*fresh)
                temps.give(buf, turn_split(buf, t, b.n // P, hid, b.name[1] * (COLS // P), v))

            defer(turn_it, 4)

        products(stages[name + "_in"], lambda b: (x_t, 0), hidden)
        add_half(name, hid, then)

    def add_half(name, hid, then):
        def residual(b, t, bank, mark):
            n, c = ROWS[t], b.c0
            to = h[t][0:n, c:c + b.n]
            v = stt(to, bank[0:n, 0:b.n], 0.5, to, ALU.mult, ALU.add, mark)
            banks.give(bank, v)
            if b.name[1] == 0:
                h_ready[t] = (v,)
            else:
                h_ready[t] += (v,)
                then(t)

        products(stages[name + "_out"], lambda b: (hid, 0), residual)

    def region_marks():
        return [(q.sem, q.count) for q in (pe, act, dve, pool) if q.count]

    pre = Gain(0, 3)
    for t in ALL_TILES:
        h_ready[t] = (h_ready[t], h_ready[t])
    for t in ALL_TILES:
        pre_norm_whole(t, pre)
    flush()

    mix_pre = Gain(1, 3)
    region = ExitStack()

    selector = sb("bias_selector_and_table", [N_BUCKETS + 1, U_ALL + HEADS], F32, region)
    sel_sb, table_sb = selector[:, 0:U_ALL], selector[:, U_ALL:U_ALL + HEADS]
    a = pool.run(lambda e: e.memset(table_sb, 1.0))
    m_table = small(pool, table_sb[0:N_BUCKETS, :], w["rel_bias_table"], a)
    m_sel = small(pool, sel_sb, w["bias_selector"])
    bias_dram = nc.dram_tensor("bias_rows", [HEADS, U_ALL], F32, kind="Internal").ap()
    bias_marks = []

    def bias_rows():
        for c in range(0, U_ALL, 512):
            n = min(512, U_ALL - c)
            bank, free = banks.take()
            a = mm(bank[0:HEADS, 0:n], table_sb, sel_sb[:, c:c + n], True, True, m_table, m_sel, *free)
            tmp, free = temps.take()
            v = dve.run(lambda e, o=tmp[0:HEADS, 0:n], s=bank[0:HEADS, 0:n]: e.tensor_copy(o, s), a, *free)
            banks.give(bank, v)
            bias_marks.append(small(sp, bias_dram[:, c:c + n], tmp[0:HEADS, 0:n], v))
            temps.give(tmp, bias_marks[-1])

    hid = Operand(sb("ffn1_hid_hi", [P, D_FF // P, KEYS], F32R, region),
                  sb("ffn1_hid_lo", [P, D_FF // P, KEYS], F32R, region))

    silu = sb("silu_of_gate", [P, COLS // P, KEYS], F32, region)

    def hidden_by_feature(b, f, bank, mark):
        kind, i = b.name
        k = i * (COLS // P) + f
        hi, lo = hid.hi[:, k, :], hid.lo[:, k, :]
        got, kept = bank[:, 0:KEYS], silu[:, f, :]
        if kind == "gate":
            silu_ready[f] = act_fn(kept, got, ACT.Silu, mark, *silu_free.get(f, ()))
            banks.give(bank, silu_ready[f])
            return
        v = tt(kept, got, kept, ALU.mult, mark, silu_ready[f])
        banks.give(bank, v)
        a = act_fn(hi, kept, ACT.Copy, v)
        v = tt(lo, kept, hi.bitcast(F32), ALU.subtract, a)
        silu_free[f] = (v,)
        for t in ALL_TILES:
            hid.ready[t, k] = (a, v)

    silu_ready, silu_free = {}, {}
    defer(bias_rows, 16)
    products_by_feature(stages["ffn1_in"], hidden_by_feature)
    add_half("ffn1", hid, lambda t: pre_norm(t, mix_pre))
    region.close()

    region = ExitStack()

    def rsb(name, shape, dt=F32):
        return sb(name, shape, dt, region)

    fresh = region_marks()
    va, va_m = rsb("va", [P, 2, FOX_W]), rsb("va_meta", [N_META, FOX_W])
    vb, vb_m = rsb("vb", [P, 2, KV_W]), rsb("vb_meta", [N_META, KV_W])
    gates = rsb("gates", [P, 2, 2 * D])
    qa_t, qb_t = rsb("qa_t", [FOX_D, HEADS, SEQ]), rsb("qb_t", [P, 4, SEQ])
    ka_t, kb_t = rsb("ka_t", [FOX_D, HEADS, KEYS]), rsb("kb_t", [P, SWA_KV, KEYS])
    window_b = rsb("window_bias", [P, HEADS, 2 * P])
    meta_b = rsb("meta_bias", [P, 2, HEADS, N_META])
    prob = Slots([rsb(f"prob{i}", [P, KEYS]) for i in range(3)])
    prob_t = Slots([rsb(f"prob_t{i}", [P, 3, P]) for i in range(2)])
    log_f = rsb("log_f", [P, 3, HEADS])
    log_f_sum = rsb("log_f_sum", [P, 3, HEADS])

    def diagonals(u0, width):
        return bass.AP(bias_dram.tensor, u0, [[1, P], [U_ALL, HEADS], [1, width]])

    bias_loaded = [small(pool, window_b[:, :, :], diagonals(0, 2 * P), *fresh, *bias_marks),
                   small(pool, meta_b[:, 0, :, :], diagonals(U_WINDOW, N_META)),
                   small(pool, meta_b[:, 1, :, :], diagonals(U_WINDOW + U_META, N_META))]
    act.wait(*fresh)
    dve.wait(*fresh)
    key0 = (N_META, N_META + P, 0)
    v_ready, gate_ready = {}, {}

    def head_norm(t, source, heads, gain_i, twice, mark, stride=HD):
        n = ROWS[t]
        width = heads * HD
        sq, free = temps.take()
        rx, scaled = x_t.scale[t]
        a = act_fn(sq[0:n, 0:width], source, ACT.Square, mark, scaled, *free, scale=rx)
        ss, r = stat(heads)[0:n, :], stat(heads)[0:n, :]
        v = reduce(ss, sq[0:n, 0:width].rearrange("p (h d) -> p h d", d=HD), ALU.add, a)
        p = rsqrt_mean(r, ss, HD, EPS, v)
        p = ts(r, r, rx, None, ALU.mult, None, p, q=pool)
        buf = sq
        by_head = buf[0:n, 0:heads * stride].rearrange("p (h d) -> p h d", d=stride)[:, :, 0:HD]
        v = tt(by_head, source.rearrange("p (h d) -> p h d", d=HD),
               r.unsqueeze(2).broadcast_to([n, heads, HD]), ALU.mult, p)
        g = head_gains[0:n, gain_i, :].unsqueeze(1).broadcast_to([n, heads, HD])
        if not twice:
            v = tt(by_head, by_head, g, ALU.mult, v, m_hg[gain_i])
        else:
            for c in range(2):
                v2 = tt(buf[0:n, 2 * width:4 * width].rearrange("p (h c d) -> p h c d", c=2, d=HD)[:, :, c, :],
                        by_head, g, ALU.mult, v, m_hg[gain_i])
            v = v2
        return buf, v

    def store_turned(t, buf, c0, chunks, to, col0, mark, scale, ready):
        def turn_it():
            n = ROWS[t]
            bank, free = banks.take()
            last = None
            for i in range(chunks):
                last = turn(bank[:, i * n:(i + 1) * n], buf[0:n, c0 + i * P:c0 + (i + 1) * P], mark, *free)
            a = act_fn(to[:, 0:chunks, col0:col0 + n], bank[:, 0:chunks * n].rearrange("p (c n) -> p c n", n=n),
                       ACT.Copy, last, scale=scale)
            banks.give(bank, a)
            temps.give(buf, last)
            ready.append(a)

        defer(turn_it, 6)

    def store_fox(t, buf, to, col0, mark, scale):
        n = ROWS[t]
        rows = buf[0:n, 0:HEADS * FOX_D].rearrange("p (h d) -> p h d", d=FOX_D)
        one, c = (1, 0) if to is qa_t else (0, 1)

        def turn_it():
            factor = 1 / scale if to is qa_t else -1.0
            v1 = dve.run(lambda e: e.memset(rows[:, :, HD + one:HD + one + 1], 1 / scale), mark)
            v1 = ts(rows[:, :, HD + c], log_f_sum[0:n, t, :], factor, None, ALU.mult, None, v1, *sum_ready)

            def turn_heads():
                last = None
                for g in range(0, HEADS, 4):
                    bank, free = banks.take()
                    for i in range(4):
                        last = turn(bank[0:FOX_D, i * n:(i + 1) * n], rows[:, g + i, :], v1, *free)
                    a = act_fn(to[:, g:g + 4, col0:col0 + n],
                               bank[0:FOX_D, 0:4 * n].rearrange("p (c n) -> p c n", n=n), ACT.Copy, last, scale=scale)
                    banks.give(bank, a)
                temps.give(buf, last)
                fox_ready.append(a)

            defer(turn_heads, 1)

        defer(turn_it, 4)

    fox_ready, swa_ready, sum_ready = [], [], []

    def mixer_in(b, t, bank, mark):
        n = ROWS[t]
        got = bank[0:n, 0:b.n]
        if b.name == "ka":
            buf, v = head_norm(t, got, HEADS, 1, False, mark, FOX_D)
            banks.give(bank, v)
            store_fox(t, buf, ka_t, key0[t], v, 1.0)
        elif b.name == "qa":
            buf, v = head_norm(t, got, HEADS, 0, False, mark, FOX_D)
            banks.give(bank, v)
            store_fox(t, buf, qa_t, P * t, v, HD ** -0.5)
        elif b.name == "qb":
            buf, v = head_norm(t, got, HEADS, 2, False, mark)
            banks.give(bank, v)
            store_turned(t, buf, 0, 4, qb_t, P * t, v, HD ** -0.5, swa_ready)
        elif b.name == "va":
            to = va[:, t, :] if t != META else va_m[:, :]
            rx, scaled = x_t.scale[t]
            a = act_fn(to, got, ACT.Copy, mark, scaled, scale=rx)
            v_ready["fox", t] = a
            banks.give(bank, a)
            if t == META:
                defer(forget_gates, 1)
        elif b.name == "kvb":
            buf, v = head_norm(t, bank[0:n, 0:KV_W], SWA_KV, 3, True, mark)
            store_turned(t, buf, 2 * KV_W, SWA_KV, kb_t, key0[t], v, 1.0, swa_ready)
            to = vb[:, t, :] if t != META else vb_m[:, :]
            a = act_fn(to, bank[0:n, KV_W:2 * KV_W], ACT.Copy, mark, v, scale=x_t.scale[t][0])
            v_ready["swa", t] = a
            banks.give(bank, a)
        else:
            i = b.name[1]
            rx, scaled = x_t.scale[t]
            v = ts(gates[:, t, i * COLS:(i + 1) * COLS], got, rx, None, ALU.mult, None, mark, scaled)
            gate_ready[t, i] = v
            banks.give(bank, v)

    a_fa = act_fn(fa_hi[:, :, :], fa_raw[:, :, :], ACT.Copy, m_fa)
    v_fa = tt(fa_lo[:, :, :], fa_raw[:, :, :], fa_hi[:, :, :].bitcast(F32), ALU.subtract, a_fa)
    log_f_ready = {}

    def forget_gates():
        f_bank, free = banks.take()
        for t in ALL_TILES:
            n, c0 = ROWS[t], FIRST_TOKEN[t]
            o = f_bank[0:n, t * HEADS:(t + 1) * HEADS]
            for k in range(KC):
                xh, xl = x_t.hi[:, k, c0:c0 + n], x_t.lo[:, k, c0:c0 + n]
                mm_quiet(o, xh, fa_hi[:, k, :], k == 0, False, v_fa, *free, *x_t.ready[t, k])
                mm_quiet(o, xh, fa_lo[:, k, :], False, False)
                mark = mm(o, xl, fa_hi[:, k, :], False, k == KC - 1)
        fx, fl, fe = stat(3 * HEADS), stat(3 * HEADS), stat(3 * HEADS)
        for t in ALL_TILES:
            n, s = ROWS[t], slice(t * HEADS, (t + 1) * HEADS)
            rx, scaled = x_t.scale[t]
            v = stt(fx[0:n, s], f_bank[0:n, s], rx, forget_b[0:n, :], ALU.mult, ALU.add, mark, m_fb, scaled)
            v1 = ts(fl[0:n, s], fx[0:n, s], -1.0, None, ALU.mult, None, v)
            v2 = tt(fl[0:n, s], fl[0:n, s], fx[0:n, s], ALU.min, v1)
            a = act_fn(fe[0:n, s], fl[0:n, s], ACT.Exp, v2)
            a = act_fn(fe[0:n, s], fe[0:n, s], ACT.Ln, a, bias=1.0)
            log_f_ready[t] = stt(log_f[0:n, t, :], fx[0:n, s], 0.0, fe[0:n, s], ALU.min, ALU.subtract, a)
        banks.give(f_bank, v)
        defer(sum_log_f, 4)

    def sum_log_f():
        bank, free = banks.take()
        for t in ALL_TILES:
            n = ROWS[t]
            before = {META: [], 0: [META], 1: [META, 0]}[t]
            for part in before:
                mm_quiet(bank[0:n, t * HEADS:(t + 1) * HEADS], upto[0:ROWS[part], P:P + n], log_f[0:ROWS[part], part, :],
                         part == META, False, upto_set, *free, *log_f_ready.values())
            last = mm(bank[0:n, t * HEADS:(t + 1) * HEADS], upto[0:n, 0:n], log_f[0:n, t, :], not before, True)
        v = None
        for t in ALL_TILES:
            n = ROWS[t]
            v = dve.run(lambda e, o=log_f_sum[0:n, t, :], i=bank[0:n, t * HEADS:(t + 1) * HEADS]:
                        e.tensor_copy(o, i), last)
        banks.give(bank, v)
        sum_ready.append(v)

    def key_parts(t):
        return [(0, N_META, META), (N_META, P, 0)] + ([(N_META + P, P, 1)] if t else [])

    def fox_scores(t, hd):
        keys = N_META + P * (t + 1)
        bank, free = banks.take()
        mm_quiet(bank[:, 0:keys], qa_t[:, hd, P * t:P * t + P], ka_t[:, hd, 0:keys], True, False, *fox_ready, *free)
        last = mm(bank[:, keys - P:keys], ident_r[:, :], causal_r[:, :], False, True, *masks_ready)
        return bank, last, keys

    def swa_scores(t, hd):
        keys = N_META + P * (t + 1)
        c, b, g = hd // 2, HD * (hd % 2), hd // (HEADS // SWA_KV)
        bank, free = banks.take()
        o = bank[:, 0:keys]
        mm_quiet(o, qb_t[b:b + HD, c, P * t:P * t + P], kb_t[b:b + HD, g, 0:keys], True, False, *swa_ready, *free)
        mm_quiet(bank[:, 0:N_META], flip[:, :], meta_b[:, t, hd, :], False, False, flip_set, *bias_loaded)
        last = mm(bank[:, N_META:keys], flip[:, :], window_b[:, hd, P * (1 - t):2 * P], False, True)
        return bank, last, keys

    def softmax(bank, mark, keys, sink, o_sum):
        mx, neg = stat(), stat()
        v = reduce(mx, bank[:, 0:keys], ALU.max, mark)
        if sink is None:
            v = ts(neg, mx, -1.0, None, ALU.mult, None, v)
        else:
            v = ts(neg, mx, sink, -1.0, ALU.max, ALU.mult, v, m_sink)
        pr, free = prob.take()
        if sink is None:
            a = act_fn(pr[:, 0:keys], bank[:, 0:keys], ACT.Exp, v, *free, bias=neg, accum_out=o_sum)
        else:
            part, extra = stat(), stat()
            a = act_fn(pr[:, 0:keys], bank[:, 0:keys], ACT.Exp, v, *free, bias=neg, accum_out=part)
            a2 = act_fn(extra, neg, ACT.Exp, v, bias=sink)
            tt(o_sum, part, extra, ALU.add, a2)
        banks.give(bank, a)
        return pr, a

    def turn_prob(pr, mark, t):
        bank, free = banks.take()
        last = None
        for i, (k0, n, _) in enumerate(key_parts(t)):
            last = turn(bank[0:n, i * P:(i + 1) * P], pr[:, k0:k0 + n], mark, *free)
        prob.give(pr, last)
        pt, free = prob_t.take()
        v = dve.run(lambda e, o=pt[0:N_META, 0, :], s=bank[0:N_META, 0:P]: e.tensor_copy(o, s), last, *free)
        k = t + 1
        a = act_fn(pt[:, 1:1 + k, :], bank[:, P:P + P * k].rearrange("p (k n) -> p k n", n=P), ACT.Copy, v)
        banks.give(bank, a)
        return pt, a

    sums = {kind: stat(2 * HEADS) for kind in ("fox", "swa")}

    def attend(kind, t):
        while len(fox_ready if kind == "fox" else swa_ready) < len(ALL_TILES) + len(TILES):
            yield
        o_bank, o_free = banks.take()
        total = sums[kind][:, t * HEADS:(t + 1) * HEADS]
        scored, turned = {}, {}
        for i in range(HEADS + 3):
            if i < HEADS:
                sc = fox_scores(t, i) if kind == "fox" else swa_scores(t, i)
                scored[i] = softmax(*sc, None if kind == "fox" else sinks[:, i:i + 1], total[:, i:i + 1])
                if i == HEADS - 1:
                    all_summed = [(act.sem, act.count), (dve.sem, dve.count)]
            if 2 <= i < HEADS + 2:
                turned[i - 2] = turn_prob(*scored.pop(i - 2), t)
            if i >= 3:
                hd = i - 3
                pt, mark = turned.pop(hd)
                ks = key_parts(t)
                for j, (_, n, part) in enumerate(ks):
                    if kind == "fox":
                        v = (va[:, part, :] if part != META else va_m[:, :])[:, hd * HD:(hd + 1) * HD]
                    else:
                        g = hd // (HEADS // SWA_KV)
                        v = (vb[:, part, :] if part != META else vb_m[:, :])[:, g * HD:(g + 1) * HD]
                    last = mm(o_bank[:, hd * HD:(hd + 1) * HD], pt[0:n, j, :], v, j == 0, j == len(ks) - 1,
                              mark, *o_free, *[v_ready[kind, p] for _, _, p in ks])
                prob_t.give(pt, last)
            if i < HEADS + 2:
                yield
        inv = stat(HEADS)
        v = dve.run(lambda e: e.reciprocal(inv, total), *all_summed)
        c0 = 0 if kind == "fox" else FOX_W
        to = row[t][:, c0:c0 + FOX_W].rearrange("p (h d) -> p h d", d=HD)
        v = tt(to, o_bank[:, :].rearrange("p (h d) -> p h d", d=HD), inv.unsqueeze(2).broadcast_to([P, HEADS, HD]),
               ALU.mult, v, last, *row_free[t])
        banks.give(o_bank, v)
        attended[kind, t] = v
        if gates_done:
            turn_kind(kind, t)

    attended, gates_done = {}, []

    def turn_kind(kind, t):
        half = 0 if kind == "fox" else 1
        last = turn_split(row[t][:, halves[half]], t, 4, x_t, 4 * half, attended.pop((kind, t)))
        row_free[t] = (last,)

    products(stages["mix_in"][:3], lambda b: (x_t, 0), mixer_in, tail=0)
    chores.extend(attend(kind, t) for kind in ("fox", "swa") for t in TILES)
    products(stages["mix_in"][3:] + stages["gates"], lambda b: (x_t, 0), mixer_in, lead=0, tail=0)
    for t in TILES:
        x_t.forget(t)
    gates_done.append(True)
    for kind, t in list(attended):
        turn_kind(kind, t)

    def branch(b, t, bank, mark):
        kind, i = b.name
        c = i * COLS + (0 if kind == "fox" else D)
        g = gates[:, t, c:c + COLS]
        a = act_fn(g, g, ACT.Sigmoid, gate_ready[t, c // COLS])
        v = tt(g, bank[:, :], g, ALU.mult, mark, a)
        banks.give(bank, v)
        if kind == "swa":
            y = gates[:, t, i * COLS:(i + 1) * COLS]
            v = tt(y, y, g, ALU.add, v)
            y_ready[t, i] = v
            if i == 1:
                def turn_it():
                    x_t.forget(t)
                    for half in range(2):
                        turn_split(gates[:, t, halves[half]], t, 4, x_t, 4 * half, y_ready[t, half])

                defer(turn_it, 1)

    y_ready = {}
    products(stages["branch"], lambda b: (x_t, 0 if b.name[0] == "fox" else 4), branch, lead=4, tail=4)

    ffn2_pre = Gain(2, 2)

    def mixer_out(b, t, bank, mark):
        to = h[t][:, b.c0:b.c0 + b.n]
        v = tt(to, bank[:, :], to, ALU.add, mark)
        banks.give(bank, v)
        if b.name[1] == 0:
            h_ready[t] = (v,)
        else:
            h_ready[t] += (v,)
            pre_norm(t, ffn2_pre)

    products(stages["mix_out"], lambda b: (x_t, 0), mixer_out)
    region.close()

    region = ExitStack()
    gmlp_pre = Gain(3, 2)
    glu("ffn2", region, lambda t: pre_norm(t, gmlp_pre))
    region.close()

    def load_p(layer):
        marks = p_free[0]
        m = small(pool, p_rows[:, :, :], w["p_2"][layer, 0].rearrange("(t p) n -> p t n", p=P), *marks)

        def turn_it():
            for t in TILES:
                p_t.forget(t)
                last = turn_split(p_rows[:, t, :], t, PLE_DIM // P, p_t, 0, m)
            p_free[0] = (last,)

        return turn_it

    p_free = [()]

    def mlp(i, region, pre_next):
        hid = Operand(sb(f"mlp{i}_hid_hi", [P, D_FF_2 // P, SEQ], F32R, region),
                      sb(f"mlp{i}_hid_lo", [P, D_FF_2 // P, SEQ], F32R, region))
        fresh = region_marks()

        def hidden(b, t, bank, mark):
            buf, free = temps.take()
            r, scaled = x_t.scale[t]
            a = act_fn(buf[:, 0:COLS], bank[:, :], ACT.Relu, mark, scaled, *free, scale=r)
            banks.give(bank, a)
            v = tt(buf[:, 0:COLS], buf[:, 0:COLS], buf[:, 0:COLS], ALU.mult, a)

            def turn_it():
                act.wait(*fresh)
                dve.wait(*fresh)
                temps.give(buf, turn_split(buf, t, COLS // P, hid, b.name[1] * (COLS // P), v))

            defer(turn_it, 4)

        products(stages["mlp_in", i], lambda b: (x_t, 0), hidden)
        gain = Gain(gain_at["ffn_post", i], 2)
        products(stages["mlp_out", i], lambda b: (hid, 0),
                 lambda b, t, bank, mark: post_norm_part(t, b.name[1], bank[:, :], mark, bank, gain, pre_next))

    gain_at = {("ffn_post", 0): 8, ("ffn_post", 1): 15, ("ple_b", 0): 10, ("ple_b", 1): 17,
               ("ple_post", 0): 11, ("ple_post", 1): 18}

    def ple(i, then):
        bias, gain = Gain(gain_at["ple_b", i], 4), Gain(gain_at["ple_post", i], 2)
        held = {}

        def gated(b, t, bank, mark):
            kind, c = b.name
            if kind == "gate":
                buf, free = temps.take()
                r, scaled = x_t.scale[t]
                v = stt(buf[:, 0:COLS], bank[:, :], r, bias.ap(P, c * COLS, COLS), ALU.mult, ALU.add, mark, bias.mark(),
                        scaled, *free)
                banks.give(bank, v)
                bias.done(v)
                held[t] = (buf, act_fn(buf[:, 0:COLS], buf[:, 0:COLS], ACT.Sigmoid, v))
            else:
                buf, a = held.pop(t)
                to = row[t][:, c * COLS:(c + 1) * COLS]
                v = tt(to, bank[:, :], buf[:, 0:COLS], ALU.mult, mark, a, *row_free[t])
                banks.give(bank, v)
                temps.give(buf, v)
                post_norm_part(t, c, to, v, None, gain, then)

        products(stages["ple", i], lambda b: (x_t if b.name[0] == "gate" else p_t, 0), gated, lead=5, tail=5)

    region = ExitStack()
    fresh = region_marks()
    z = rsb("z", [P, 2, 2 * D])
    ws_rows = rsb("w_s_rows", [P, HEADS, P])
    ws_t = rsb("w_s_t", [P, HEADS, P])
    b_s = rsb("b_s", [P, HEADS])
    m_ws = small(pool, ws_rows[:, :, :], w["a_w_s_2"][0].rearrange("g t s -> t g s"), *fresh)
    m_bs = small(pool, b_s[:, :], w["a_b_s_2"][0].rearrange("g t -> t g"), allow_slow_non_contiguous=True)
    turn_p = load_p(0)
    act.wait(*fresh)
    dve.wait(*fresh)
    ws_marks = []

    def turn_ws():
        for g0 in range(0, HEADS, 4):
            bank, free = banks.take()
            for i in range(4):
                last = turn(bank[:, i * P:(i + 1) * P], ws_rows[:, g0 + i, :], m_ws, *free)
            v = tt(ws_t[:, g0:g0 + 4, :], bank[:, :].rearrange("p (g t) -> p g t", t=P),
                   upto[:, 0:P].unsqueeze(1).broadcast_to([P, 4, P]), ALU.mult, last, upto_set)
            banks.give(bank, v)
            ws_marks.append(v)

    z_sum = {t: [] for t in TILES}
    ln_g, ln_b = Gain(4, 2), Gain(5, 2)

    def gmlp_in(b, t, bank, mark):
        i = b.name[1]
        rx, scaled = x_t.scale[t]
        kw = {}
        if i >= 2:
            s = stat()
            z_sum[t].append(s)
            kw = {"accum_out": s}
        cols = z[:, t, i * COLS:(i + 1) * COLS]
        a = act_fn(cols, bank[:, :], ACT.Gelu_apprx_tanh, mark, scaled, scale=rx, **kw)
        banks.give(bank, a)
        v_rows = z[:, t, D:2 * D]
        if i == 2:
            return
        if i == 3:
            total, minus_mean, ss, r = stat(), stat(), stat(), stat()
            v = tt(total, z_sum[t][0], z_sum[t][1], ALU.add, a)
            v = ts(minus_mean, total, -1.0 / D, None, ALU.mult, None, v)
            a = act_fn(row[t][:, :], v_rows, ACT.Square, v, *row_free[t], bias=minus_mean, accum_out=ss)
            row_free[t] = (a,)
            p = rsqrt_mean(r, ss, D, LN_EPS, a)
            v = ts(v_rows, v_rows, minus_mean, r, ALU.add, ALU.mult, p)
            v = tt(v_rows, v_rows, ln_g.ap(P), ALU.mult, v, ln_g.mark())
            ln_g.done(v)
            v = tt(v_rows, v_rows, ln_b.ap(P), ALU.add, v, ln_b.mark())
            ln_b.done(v)

            def mix_tokens():
                mixed = []
                for g0 in range(0, HEADS, 4):
                    bank, free = banks.take()
                    for g in range(g0, g0 + 4):
                        last = mm(bank[:, (g - g0) * P:(g - g0 + 1) * P], ws_t[:, g, :],
                                  v_rows[:, g * P:(g + 1) * P], True, True, v, *ws_marks, *free)
                    for g in range(g0, g0 + 4):
                        o = act_fn(v_rows[:, g * P:(g + 1) * P], bank[:, (g - g0) * P:(g - g0 + 1) * P],
                                   ACT.Identity, last, m_bs, bias=b_s[:, g:g + 1])
                    banks.give(bank, o)
                    mixed.append(o)
                s_marks[t] = mixed

            defer(mix_tokens, 6)
            return

        def gate_u():
            y = z[:, t, i * COLS:(i + 1) * COLS]
            v = tt(y, y, z[:, t, (i + 2) * COLS:(i + 3) * COLS], ALU.mult, a, s_marks[t][i])
            if i == 0:
                half_done[t] = v
                return
            x_t.forget(t)
            turn_split(z[:, t, 0:COLS], t, 4, x_t, 0, half_done[t])
            turn_split(z[:, t, COLS:D], t, 4, x_t, 4, v)

        defer(gate_u, 1)

    s_marks, half_done = {}, {}
    defer(turn_ws, 8)
    defer(turn_p, 1)
    products(stages["gmlp_in"], lambda b: (x_t, 0), gmlp_in)
    mix_post, ffn_pre = Gain(6, 2), Gain(7, 2)
    products(stages["gmlp_out"], lambda b: (x_t, 0),
             lambda b, t, bank, mark: post_norm_part(t, b.name[1], bank[:, :], mark, bank, mix_post,
                                                     lambda t: pre_norm(t, ffn_pre)))
    region.close()

    region = ExitStack()
    ple_pre = Gain(9, 2)
    mlp(0, region, lambda t: pre_norm(t, ple_pre))
    region.close()
    attn_pre = Gain(12, 2)
    ple(0, lambda t: pre_norm(t, attn_pre))

    lambda_init = 0.8 - 0.6 * math.exp(-0.3)
    region = ExitStack()
    fresh = region_marks()
    qk = rsb("qk_rows", [P, 2, 2 * D])
    vv = rsb("v_rows", [P, 2, D])
    q_t, k_t = rsb("q_t", [P, HEADS, SEQ]), rsb("k_t", [P, HEADS, SEQ])
    prob2 = Slots([rsb(f"prob2_{i}", [P, 2, SEQ]) for i in range(3)])
    diff = Slots([rsb(f"diff{i}", [P, SEQ]) for i in range(4)])
    diff_t = Slots([rsb(f"diff_t{i}", [P, 2, P]) for i in range(2)])
    rot = [rsb(f"rot{i}", [P, 2, 8, ROT // 2]) for i in range(4)]
    pos_i = rsb("positions", [P, 2], I32)
    lam_in = rsb("lambda_in", [P, 4, HD])
    subln = rsb("subln_g", [P, P])
    freq = rsb("frequencies", [P, ROT // 2])
    angles = rsb("angles", [P, 8, 2, ROT // 2])
    dve.wait(*fresh)
    act.wait(*fresh)
    m_pos = small(pool, pos_i[:, :], w["positions_2"][0].rearrange("(t p) -> p t", p=P), *fresh,
                  allow_slow_non_contiguous=True)
    m_lam = [small(pool, lam_in[:, i, :], w[k].broadcast_to([P, HD]))
             for i, k in enumerate(("b_lam_q1_2", "b_lam_k1_2", "b_lam_q2_2", "b_lam_k2_2"))]
    m_sub = small(pool, subln[:, :], w["b_subln_g_2"].broadcast_to([P, P]))
    m_frq = small(pool, freq[:, :], w["frequencies"].broadcast_to([P, ROT // 2]))
    turn_p = load_p(1)

    lam_sum, lam_exp, minus_lam = stat(2), stat(2), stat()
    v = tt(lam_in[:, 0, :], lam_in[:, 0, :], lam_in[:, 1, :], ALU.mult, m_lam[0], m_lam[1])
    v2 = tt(lam_in[:, 2, :], lam_in[:, 2, :], lam_in[:, 3, :], ALU.mult, m_lam[2], m_lam[3])
    v = reduce(lam_sum[:, 0:1], lam_in[:, 0, :], ALU.add, v)
    v = reduce(lam_sum[:, 1:2], lam_in[:, 2, :], ALU.add, v2)
    a = act_fn(lam_exp, lam_sum, ACT.Exp, v)
    v = tt(minus_lam, lam_exp[:, 1:2], lam_exp[:, 0:1], ALU.subtract, a)
    lam_ready = ts(minus_lam, minus_lam, lambda_init, None, ALU.subtract, None, v)
    sub_ready = ts(subln[:, :], subln[:, :], 1.0 - lambda_init, None, ALU.mult, None, m_sub)

    two_pi = 2 * math.pi
    part1 = 6.28125
    part2 = float(np.float32(np.round((two_pi - part1) * 2 ** 20) / 2 ** 20))
    part3 = float(np.float32(two_pi - part1 - part2))
    big = 1.5 * 2.0 ** 23
    pos_f = stat(2)
    v = dve.run(lambda e: e.tensor_copy(pos_f, pos_i[:, :]), m_pos)
    ang, turns, cut, rest = (angles[:, i, :, :] for i in range(4))
    sin_, cos_ = angles[:, 4, :, :], angles[:, 5, :, :]
    for t in TILES:
        v0 = ts(ang[:, t, :], freq[:, :], pos_f[:, t:t + 1], None, ALU.mult, None, v, m_frq)
    trig_ready = []
    for shift, o in ((0.0, sin_), (0.25, cos_)):
        v1 = ts(turns, ang, 1.0 / two_pi, shift, ALU.mult, ALU.add, v0, *trig_ready)
        v1 = ts(turns, turns, big, None, ALU.add, None, v1)
        v1 = ts(turns, turns, big, None, ALU.subtract, None, v1)
        v1 = stt(rest, turns, -part1, ang, ALU.mult, ALU.add, v1)
        v1 = stt(rest, turns, -part2, rest, ALU.mult, ALU.add, v1)
        v1 = stt(rest, turns, -part3, rest, ALU.mult, ALU.add, v1)
        v1 = ts(rest, rest, two_pi * shift, None, ALU.add, None, v1)
        limit = 3.1415925
        v1 = ts(rest, rest, limit, -limit, ALU.min, ALU.max, v1)
        trig_ready = [act_fn(o, rest, ACT.Sin, v1)]

    v_marks, rot_free = [], []
    qk_marks = {}
    turned_qk = {0: [], 1: []}

    def qkv(b, t, bank, mark):
        i = b.name[1]
        rx, scaled = x_t.scale[t]
        if i >= 4:
            a = act_fn(vv[:, t, (i - 4) * COLS:(i - 3) * COLS], bank[:, :], ACT.Copy, mark, scaled, scale=rx)
            banks.give(bank, a)
            v_marks.append(a)
            return
        a = act_fn(qk[:, t, i * COLS:(i + 1) * COLS], bank[:, :], ACT.Copy, mark, scaled, scale=rx)
        banks.give(bank, a)
        if i >= 2:
            qk_marks[t] = a
            return
        x = qk[:, t, :].rearrange("p (s c g d) -> p s c g d", s=2, c=2, d=HD)[:, :, i, :, :]
        x1, x2 = x[:, :, :, 0:ROT // 2], x[:, :, :, ROT // 2:ROT]
        shape = [P, 2, 8, ROT // 2]
        c, s = [o[:, t, :].unsqueeze(1).unsqueeze(1).broadcast_to(shape) for o in (cos_, sin_)]
        tt(rot[0][:, :, :, :], x1, c, ALU.mult, *trig_ready, a, qk_marks[t], *rot_free)
        tt(rot[1][:, :, :, :], x2, s, ALU.mult)
        tt(rot[2][:, :, :, :], x2, c, ALU.mult)
        v = tt(rot[3][:, :, :, :], x1, s, ALU.mult)
        tt(x1, rot[0][:, :, :, :], rot[1][:, :, :, :], ALU.subtract, v)
        v = tt(x2, rot[2][:, :, :, :], rot[3][:, :, :, :], ALU.add)
        rot_free[:] = [v]

        def turn_it():
            for to, c0, scale in ((q_t, 0, HD ** -0.5), (k_t, D, 1.0)):
                bank, free = banks.take()
                for j in range(4):
                    g = 4 * i + j
                    last = turn(bank[:, j * P:(j + 1) * P], qk[:, t, c0 + g * P:c0 + (g + 1) * P], v, *free)
                a = act_fn(to[:, 4 * i:4 * i + 4, P * t:P * t + P], bank[:, :].rearrange("p (g n) -> p g n", n=P),
                           ACT.Copy, last, scale=scale)
                banks.give(bank, a)
                turned_qk[i].append(a)

        defer(turn_it, 3)

    defer(turn_p, 4)
    products(stages["qkv"], lambda b: (x_t, 0), qkv, tail=0)
    flush()

    def diff_scores(t, hd):
        keys = P * (t + 1)
        bank, free = banks.take()
        last = free[0] if free else ident_set
        for c in range(2):
            b = HD * c
            mm_quiet(bank[:, c * SEQ:c * SEQ + keys], q_t[b:b + HD, hd, P * t:P * t + P], k_t[b:b + HD, hd, 0:keys],
                     True, False, *turned_qk[hd // 4], *free, last)
            last = mm(bank[:, c * SEQ + keys - P:c * SEQ + keys], ident_r[:, :], causal_r[:, :], False, True, *masks_ready)
        mx, neg, total, inv = stat(2), stat(2), stat(2), stat(2)
        got = bank[:, :].rearrange("p (c k) -> p c k", c=2)
        v = reduce(mx, got[:, :, 0:keys], ALU.max, last)
        v = ts(neg, mx, -1.0, None, ALU.mult, None, v)
        pr, free = prob2.take()
        for c in range(2):
            a = act_fn(pr[:, c, 0:keys], got[:, c, 0:keys], ACT.Exp, v, *free, bias=neg[:, c:c + 1],
                       accum_out=total[:, c:c + 1])
        banks.give(bank, a)
        v = dve.run(lambda e: e.reciprocal(inv, total), a)
        w1 = stat()
        v = tt(w1, inv[:, 1:2], minus_lam, ALU.mult, v, lam_ready)
        v = ts(pr[:, 1, 0:keys], pr[:, 1, 0:keys], w1, None, ALU.mult, None, v)
        df, free = diff.take()
        v = stt(df[:, 0:keys], pr[:, 0, 0:keys], inv[:, 0:1], pr[:, 1, 0:keys], ALU.mult, ALU.add, v, *free)
        prob2.give(pr, v)
        return df, v

    def turn_diff(df, mark, t):
        bank, free = banks.take()
        for i in range(t + 1):
            last = turn(bank[:, i * P:(i + 1) * P], df[:, i * P:(i + 1) * P], mark, *free)
        diff.give(df, last)
        dt_, free = diff_t.take()
        a = act_fn(dt_[:, 0:t + 1, :], bank[:, 0:(t + 1) * P].rearrange("p (k n) -> p k n", n=P), ACT.Copy, last, *free)
        banks.give(bank, a)
        return dt_, a

    def attend_diff(t, g):
        scored, turned = {}, {}
        o_bank, o_free = banks.take()
        for i in range(4 + 3):
            if i < 4:
                scored[i] = diff_scores(t, 4 * g + i)
            if 2 <= i < 6:
                turned[i - 2] = turn_diff(*scored.pop(i - 2), t)
            if i >= 3:
                j = i - 3
                dt_, mark = turned.pop(j)
                for k in range(t + 1):
                    last = mm(o_bank[:, j * P:(j + 1) * P], dt_[:, k, :], vv[:, k, (4 * g + j) * P:(4 * g + j + 1) * P],
                              k == 0, k == t, mark, *o_free, *v_marks)
                diff_t.give(dt_, last)
            if i < 6:
                yield
        got = o_bank[:, :].rearrange("p (h d) -> p h d", d=P)
        sq, free = temps.take()
        a = act_fn(sq[:, 0:COLS], o_bank[:, :], ACT.Square, last, *free)
        ss, r = stat(4), stat(4)
        v = reduce(ss, sq[:, 0:COLS].rearrange("p (h d) -> p h d", d=P), ALU.add, a)
        temps.give(sq, v)
        p = rsqrt_mean(r, ss, P, SUBLN_EPS, v)
        to = row[t][:, halves[g]].rearrange("p (h d) -> p h d", d=P)
        v = tt(to, got, r.unsqueeze(2).broadcast_to([P, 4, P]), ALU.mult, p, *row_free[t])
        banks.give(o_bank, v)
        v = tt(to, to, subln[:, :].unsqueeze(1).broadcast_to([P, 4, P]), ALU.mult, v, sub_ready)
        normed[t, g] = v
        if g == 1:
            yield
            yield
            for half in range(2):
                last = turn_split(row[t][:, halves[half]], t, 4, x_t, 4 * half, normed[t, half])
            row_free[t] = (last,)

    normed = {}
    chores.extend(attend_diff(t, 0) for t in TILES)
    products(stages["qkv_rest"], lambda b: (x_t, 0), qkv, lead=0, tail=0)
    flush()
    finish_chores()
    for t in TILES:
        x_t.forget(t)
    chores.extend(attend_diff(t, 1) for t in TILES)

    attn_post, ffn_pre2 = Gain(13, 2), Gain(14, 2)
    products(stages["attn_out"], lambda b: (x_t, 0),
             lambda b, t, bank, mark: post_norm_part(t, b.name[1], bank[:, :], mark, bank, attn_post,
                                                     lambda t: pre_norm(t, ffn_pre2)))
    region.close()

    region = ExitStack()
    ple_pre2 = Gain(16, 2)
    mlp(1, region, lambda t: pre_norm(t, ple_pre2))
    region.close()

    stored = []

    def store(t):
        stored.append(small(sp, out[0, t * P:(t + 1) * P, :], h[t], *h_ready[t]))

    ple(1, store)
    flush()
    sp.wait(*stored)

    with hold:
        with nc.Block() as block:
            @block.sync
            def _(engine):
                sp.play(engine)

            @block.scalar
            def _(engine):
                act.play(engine)

            @block.vector
            def _(engine):
                dve.play(engine)

            @block.gpsimd
            def _(engine):
                pool.play(engine)

            @block.tensor
            def _(engine):
                pe.play(engine)


_INS = [
    "x", "meta_tokens", "rel_bias_table", "ffn1_norm", "ffn1_w_in", "ffn1_w_out", "mix_norm", "w_in",
    "forget_bias", "fox_q_norm", "fox_k_norm", "swa_q_norm", "swa_k_norm", "swa_sinks", "w_branch_fox",
    "w_branch_swa", "w_out", "ffn2_norm", "ffn2_w_in", "ffn2_w_out", "p_2", "positions_2", "g_mix_pre_2",
    "g_mix_post_2", "g_ffn_pre_2", "g_ffn_post_2", "g_ple_pre_2", "g_ple_post_2", "a_w_in_2", "a_ln_g_2",
    "a_ln_b_2", "a_w_s_2", "a_b_s_2", "a_w_out_2", "b_w_qkv_2", "b_lam_q1_2", "b_lam_k1_2", "b_lam_q2_2",
    "b_lam_k2_2", "b_subln_g_2", "b_w_o_2", "f_w_up_2", "f_w_down_2", "ple_w_proj_2", "ple_w_gate_2",
    "ple_b_gate_2",
]


def kernel(**inputs):
    import concourse.bacc as bacc
    from concourse.bass_utils import run_bass_kernel_spmd

    nc = bacc.Bacc("TRN2", target_bir_lowering=False, num_devices=1)
    arrays, aps = {}, {}
    given = {name: np.ascontiguousarray(inputs[name]) for name in _INS}
    given["bias_selector"] = bias_selector()
    given["frequencies"] = rotary_frequencies()[None, :]
    for name, a in given.items():
        arrays[f"in_{name}"] = a
        aps[name] = nc.dram_tensor(f"in_{name}", a.shape, mybir.dt.from_np(a.dtype), kind="ExternalInput").ap()
    out = nc.dram_tensor("out_0", (1, SEQ, D), F32, kind="ExternalOutput").ap()
    two_blocks(nc, aps, out)
    r = run_bass_kernel_spmd(nc, [arrays], core_ids=[0])
    return r.results[0]["out_0"]
```

```python
import math
from collections import deque
from contextlib import ExitStack

import numpy as np

import concourse.bass as bass
from concourse import mybir

F32 = mybir.dt.float32
F32R = mybir.dt.float32r
I32 = mybir.dt.int32
ALU = mybir.AluOpType
ACT = mybir.ActivationFunctionType
X = mybir.AxisListType.X

P = 128
D = 1024
SEQ = 256
N_META = 16
D_FF = 2816
D_FF_2 = 4096
HEADS = 8
HD = 64
SWA_KV = 2
WINDOW = 128
N_BUCKETS = 32
MAX_DISTANCE = 128
PLE_DIM = 256
ROT = 16
ROPE_THETA = 500000.0
NEG = -1e30
EPS = 1e-6
LN_EPS = 1e-5
SUBLN_EPS = 1e-5
META = 2
TILES = (0, 1)
ALL_TILES = (0, 1, META)
ROWS = (P, P, N_META)
FIRST_TOKEN = (0, P, SEQ)
KEYS = N_META + SEQ
FOX_D = HD + 2
KC = D // P
COLS = 512
PIECE_K = 2
RAW_SLOTS = 4
SPLIT_SLOTS = 6

FOX_W = HEADS * HD
KV_W = SWA_KV * HD
C_QA, C_KA, C_VA = 0, FOX_W, 2 * FOX_W
C_FA = 3 * FOX_W
C_QB = C_FA + HEADS
C_KB = C_QB + FOX_W
C_GA = C_KB + 2 * KV_W

U_WINDOW = 3 * P - 1
U_META = P + N_META - 1
U_ALL = U_WINDOW + 2 * U_META


def bias_selector():
    distance = np.concatenate([2 * P - 1 - np.arange(U_WINDOW), P + N_META - 1 - np.arange(U_META),
                               2 * P + N_META - 1 - np.arange(U_META)])
    seen = np.ones(U_ALL, bool)
    seen[:U_WINDOW] = (distance[:U_WINDOW] >= 0) & (distance[:U_WINDOW] < WINDOW)
    half = N_BUCKETS // 2
    n = np.maximum(distance, 0)
    far = np.log(np.maximum(n, 1).astype(np.float32) / half) / math.log(MAX_DISTANCE / half) * half
    bucket = np.where(n < half, n, np.minimum(half + far.astype(np.int32), N_BUCKETS - 1))
    out = np.zeros((N_BUCKETS + 1, U_ALL), np.float32)
    out[bucket[seen], np.nonzero(seen)[0]] = 1.0
    out[N_BUCKETS, ~seen] = NEG
    return out


def rotary_frequencies():
    return (ROPE_THETA ** (-(np.arange(0, ROT, 2, dtype=np.float32) / ROT))).astype(np.float32)


class Queue:

    def __init__(self, sem):
        self.sem, self.count, self.steps, self.reached = sem, 0, [], {}

    def wait(self, *marks):
        for sem, value in marks:
            if self.reached.get(sem.name, 0) < value:
                self.reached[sem.name] = value
                self.steps.append(lambda e, sem=sem, value=value: e.wait_ge(sem, value))

    def run(self, make, *marks):
        self.wait(*marks)
        self.count += 1
        self.steps.append(lambda e: make(e).then_inc(self.sem, 1))
        return (self.sem, self.count)

    def quiet(self, make, *marks):
        self.wait(*marks)
        self.steps.append(make)

    def dma(self, out, in_, sem, n, *marks, **kw):
        self.wait(*marks)
        self.steps.append(lambda e: e.dma_start(out, in_, **kw).then_inc(sem, 16))
        return (sem, 16 * n)

    def play(self, engine):
        for step in self.steps:
            step(engine)


class Slots:

    def __init__(self, buffers):
        self.free = deque((b, ()) for b in buffers)

    def take(self):
        return self.free.popleft()

    def give(self, buffer, *marks):
        self.free.append((buffer, marks))


class Block:

    def __init__(self, matrix, first, n, tiles=TILES, name=None):
        self.matrix, self.c0, self.n, self.tiles, self.name = matrix, first, n, tiles, name
        self.pieces = matrix.shape[0] // (P * PIECE_K)
        self.at = None

    def source(self, j):
        rows = self.matrix[j * PIECE_K * P:(j + 1) * PIECE_K * P, self.c0:self.c0 + self.n]
        return rows.rearrange("(c p) n -> p c n", p=P)


class Operand:

    def __init__(self, hi, lo):
        self.hi, self.lo, self.ready, self.free, self.scale, self.mean = hi, lo, {}, {}, {}, {}

    def forget(self, t):
        for key in [key for key in self.ready if key[0] == t]:
            del self.ready[key]


def column_blocks(matrix, width, tiles=TILES, name=None):
    return [Block(matrix, c, min(COLS, width - c), tiles, (name, c // COLS)) for c in range(0, width, COLS)]


def plan(w):

    def glu(w_in, w_out, tiles):
        up = []
        for c in range(0, D_FF, COLS):
            n = min(COLS, D_FF - c)
            up += [Block(w_in, c, n, tiles, ("gate", c // COLS)), Block(w_in, D_FF + c, n, tiles, ("up", c // COLS))]
        return up, column_blocks(w_out, D, tiles)

    s = {}
    s["ffn1_in"], s["ffn1_out"] = glu(w["ffn1_w_in"][0], w["ffn1_w_out"][0], ALL_TILES)
    w_in = w["w_in"][0]
    s["mix_in"] = [Block(w_in, C_VA, FOX_W, ALL_TILES, "va"), Block(w_in, C_KA, FOX_W, ALL_TILES, "ka"),
                   Block(w_in, C_QA, FOX_W, TILES, "qa"),
                   Block(w_in, C_KB, 2 * KV_W, ALL_TILES, "kvb"), Block(w_in, C_QB, FOX_W, TILES, "qb")]
    s["gates"] = [Block(w_in, C_GA + COLS * i, COLS, TILES, ("gates", i)) for i in range(4)]
    s["branch"] = [b for i in range(2) for b in (Block(w["w_branch_fox"][0], COLS * i, COLS, TILES, ("fox", i)),
                                                 Block(w["w_branch_swa"][0], COLS * i, COLS, TILES, ("swa", i)))]
    s["mix_out"] = column_blocks(w["w_out"][0], D)
    s["ffn2_in"], s["ffn2_out"] = glu(w["ffn2_w_in"][0], w["ffn2_w_out"][0], TILES)
    z = column_blocks(w["a_w_in_2"][0], 2 * D)
    s["gmlp_in"] = z[2:] + z[:2]
    s["gmlp_out"] = column_blocks(w["a_w_out_2"][0], D)
    q0, q1, k0, k1, v0, v1 = column_blocks(w["b_w_qkv_2"][0], 3 * D)
    s["qkv"] = [k0, q0, v0]
    s["qkv_rest"] = [k1, q1, v1]
    s["attn_out"] = column_blocks(w["b_w_o_2"][0], D)
    for i in range(2):
        s["mlp_in", i] = column_blocks(w["f_w_up_2"][i], D_FF_2)
        s["mlp_out", i] = column_blocks(w["f_w_down_2"][i], D)
        s["ple", i] = [b for c in range(2) for b in (Block(w["ple_w_gate_2"][i], COLS * c, COLS, TILES, ("gate", c)),
                                                     Block(w["ple_w_proj_2"][i], COLS * c, COLS, TILES, ("proj", c)))]
    order = ["ffn1_in", "ffn1_out", "mix_in", "gates", "branch", "mix_out", "ffn2_in", "ffn2_out",
             "gmlp_in", "gmlp_out", ("mlp_in", 0), ("mlp_out", 0), ("ple", 0),
             "qkv", "qkv_rest", "attn_out", ("mlp_in", 1), ("mlp_out", 1), ("ple", 1)]
    stream = []
    for name in order:
        for b in s[name]:
            b.at = len(stream)
            stream += [(b, j) for j in range(b.pieces)]
    return s, stream


def two_blocks(nc, w, out):
    stages, stream = plan(w)
    hold = ExitStack()

    def sb(name, shape, dt=F32, where=hold):
        return where.enter_context(nc.sbuf_tensor(name, shape, dt))

    def sem(name):
        return hold.enter_context(nc.semaphore(name))

    pe, act, dve, pool, sp = (Queue(sem(n)) for n in ("pe_done", "act_done", "dve_done", "pool_done", "sp_done"))
    last_square = []

    raw = sb("weights_raw", [P, RAW_SLOTS, PIECE_K, COLS])
    w_hi = sb("weights_hi", [P, SPLIT_SLOTS, PIECE_K, COLS], F32R)
    w_lo = sb("weights_lo", [P, SPLIT_SLOTS, PIECE_K, COLS], F32R)
    h_main = sb("h", [P, 2, D])
    h_meta = sb("h_meta", [N_META, D])
    row_main = sb("row", [P, 2, D])
    row_meta = sb("row_meta", [N_META, D])
    x_t = Operand(sb("x_t_hi", [P, KC, KEYS], F32R), sb("x_t_lo", [P, KC, KEYS], F32R))
    p_rows = sb("p_rows", [P, 2, PLE_DIM])
    p_t = Operand(sb("p_t_hi", [P, PLE_DIM // P, SEQ], F32R), sb("p_t_lo", [P, PLE_DIM // P, SEQ], F32R))
    gains_sb = sb("gains", [P, 3, D])
    temps = Slots([sb(f"temp{i}", [P, HEADS * FOX_D]) for i in range(4)])
    junk = sb("squares", [P, COLS])
    stats = sb("stats", [P, 1024])
    ident = sb("identity", [P, P])
    flip = sb("anti_identity", [P, P])
    causal = sb("causal_neg", [P, P])
    upto = sb("upto_and_ones", [P, 2 * P])
    ident_r = sb("identity_r", [P, P], F32R)
    causal_r = sb("causal_neg_r", [P, P], F32R)
    minus_half = sb("minus_half", [P, 16])
    fa_raw = sb("w_fa", [P, KC, HEADS])
    fa_hi = sb("w_fa_hi", [P, KC, HEADS], F32R)
    fa_lo = sb("w_fa_lo", [P, KC, HEADS], F32R)
    head_gains = sb("head_gains", [P, 4, HD])
    forget_b = sb("forget_bias", [P, HEADS])
    sinks = sb("sinks", [P, HEADS])
    banks = Slots([hold.enter_context(nc.psum_tensor(f"bank{i}", [P, 512], F32)) for i in range(8)])

    h = [h_main[:, 0, :], h_main[:, 1, :], h_meta[:, :]]
    row = [row_main[:, 0, :], row_main[:, 1, :], row_meta[:, :]]
    h_ready = {}
    row_free = {t: () for t in ALL_TILES}
    used = [0]

    def stat(n=1):
        used[0] += n
        assert used[0] <= 1024
        return stats[:, used[0] - n:used[0]]

    def mm(o, lhs, rhs, start, stop, *marks):
        return pe.run(lambda e: e.matmul(o, lhs, rhs, start=start, stop=stop), *marks)

    def mm_quiet(o, lhs, rhs, start, stop, *marks):
        pe.quiet(lambda e: e.matmul(o, lhs, rhs, start=start, stop=stop), *marks)

    def turn(o, i, *marks):
        n = i.shape[0]
        return pe.run(lambda e: e.transpose(o, i, ident[0:n, 0:n]), *marks)

    def act_fn(o, i, f, *marks, **kw):
        return act.run(lambda e: e.activation(o, i, f, **kw), *marks)

    def tt(o, a, b, op, *marks, q=dve):
        return q.run(lambda e: e.tensor_tensor(o, a, b, op), *marks)

    def ts(o, a, s1, s2, op0, op1, *marks, q=dve):
        return q.run(lambda e: e.tensor_scalar(o, a, s1, s2, op0, op1) if op1 is not None
                     else e.tensor_scalar(o, a, s1, None, op0), *marks)

    def stt(o, a, s, b, op0, op1, *marks):
        return dve.run(lambda e: e.scalar_tensor_tensor(out=o, in0=a, scalar=s, in1=b, op0=op0, op1=op1), *marks)

    def reduce(o, a, op, *marks):
        return dve.run(lambda e: e.tensor_reduce(o, a, X, op), *marks)

    def rsqrt_mean(o, total, n, eps, *marks):
        m = stat(total.shape[1])[0:total.shape[0], :]
        a = ts(m, total, 1.0 / n, eps, ALU.mult, ALU.add, *marks)
        return tt(o, m, minus_half[0:total.shape[0], 0:total.shape[1]], ALU.pow, a, half_set, q=pool)

    later = deque()

    def defer(fn, units=3):
        later.append([units, fn])

    chores = deque()
    ticks = [0]

    def chore():
        try:
            next(chores[0])
        except StopIteration:
            chores.popleft()

    def tick():
        for item in later:
            item[0] -= 1
        while later and later[0][0] <= 0:
            later.popleft()[1]()
        ticks[0] += 1
        for _ in range(2 if ticks[0] % 5 == 0 else 1):
            if chores:
                chore()

    def flush():
        while later:
            later.popleft()[1]()

    raw_sems = [sem(f"raw{i}_loaded") for i in range(RAW_SLOTS)]
    loads, splits, released = [], [], []

    def load_next():
        n = len(loads)
        b, j = stream[n]
        marks = splits[n - RAW_SLOTS] if n >= RAW_SLOTS else ()
        loads.append(sp.dma(raw[:, n % RAW_SLOTS, :, 0:b.n], b.source(j), raw_sems[n % RAW_SLOTS],
                            n // RAW_SLOTS + 1, *marks))

    def split_next():
        n = len(splits)
        b, j = stream[n]
        source = raw[:, n % RAW_SLOTS, :, 0:b.n]
        hi, lo = w_hi[:, n % SPLIT_SLOTS, :, 0:b.n], w_lo[:, n % SPLIT_SLOTS, :, 0:b.n]
        former = (released[n - SPLIT_SLOTS],) if n >= SPLIT_SLOTS else ()
        a = act_fn(hi, source, ACT.Copy, loads[n], *former)
        v = tt(lo, source, hi.bitcast(F32), ALU.subtract, a)
        splits.append((a, v))
        if len(loads) < len(stream):
            load_next()

    def advance():
        while len(splits) < min(len(released) + SPLIT_SLOTS, len(stream)):
            split_next()

    def release(mark):
        released.append(mark)
        advance()

    gain_order = [w["ffn1_norm"][0:1], w["mix_norm"][0:1], w["ffn2_norm"][0:1],
                  w["g_mix_pre_2"][0:1], w["a_ln_g_2"][0:1], w["a_ln_b_2"][0:1], w["g_mix_post_2"][0:1],
                  w["g_ffn_pre_2"][0:1], w["g_ffn_post_2"][0:1], w["g_ple_pre_2"][0:1], w["ple_b_gate_2"][0:1],
                  w["g_ple_post_2"][0:1],
                  w["g_mix_pre_2"][1:2], w["g_mix_post_2"][1:2],
                  w["g_ffn_pre_2"][1:2], w["g_ffn_post_2"][1:2], w["g_ple_pre_2"][1:2], w["ple_b_gate_2"][1:2],
                  w["g_ple_post_2"][1:2]]
    gain_sems = [sem(f"gain{i}_loaded") for i in range(3)]
    gain_marks = []

    def load_gain(*marks):
        n = len(gain_marks)
        if n < len(gain_order):
            gain_marks.append(sp.dma(gains_sb[:, n % 3, :], gain_order[n].broadcast_to([P, D]), gain_sems[n % 3], n // 3 + 1, *marks))

    class Gain:

        def __init__(self, n, uses):
            self.n, self.left, self.marks = n, uses, []

        def ap(self, rows, c0=0, n=D):
            return gains_sb[0:rows, self.n % 3, c0:c0 + n]

        def mark(self):
            return gain_marks[self.n]

        def done(self, mark):
            self.marks.append(mark)
            self.left -= 1
            if not self.left:
                load_gain(*self.marks)

    small_sems = [0]

    def small(q, o, i, *marks, **kw):
        small_sems[0] += 1
        return q.dma(o, i, sem(f"small{small_sems[0]}"), 1, *marks, **kw)

    h_ready[0] = small(sp, h_main[:, 0, :], w["x"][0, 0:P, :])
    load_gain()
    h_ready[1] = small(sp, h_main[:, 1, :], w["x"][0, P:SEQ, :])
    h_ready[META] = small(sp, h_meta[:, :], w["meta_tokens"])
    for _ in range(RAW_SLOTS):
        load_next()
    load_gain()
    load_gain()

    m_id = pool.run(lambda e: e.memset(ident[:, :], 0.0))
    half_set = pool.run(lambda e: e.memset(minus_half[:, :], -0.5))

    def select(o, i, base, cm, pattern, cmp, fill, *marks):
        return pool.run(lambda e: e.affine_select(out=o, in_=i, compare_op=cmp, fill=fill, base=base,
                                                  pattern=pattern, channel_multiplier=cm), *marks)

    ident_set = select(ident[:, :], ident[:, :], 0, 1, [[-1, P]], ALU.not_equal, 1.0, m_id)
    def turn_split(source, t, chunks, to, first_chunk, *marks):
        n, c0 = ROWS[t], FIRST_TOKEN[t]
        last = None
        for c in range(0, chunks, 4):
            k = min(4, chunks - c)
            bank, free = banks.take()
            for i in range(k):
                last = turn(bank[:, i * n:(i + 1) * n], source[0:n, (c + i) * P:(c + i + 1) * P], *marks, *free, ident_set)
            got = bank[:, 0:k * n].rearrange("p (c n) -> p c n", n=n)
            hi = to.hi[:, first_chunk + c:first_chunk + c + k, c0:c0 + n]
            lo = to.lo[:, first_chunk + c:first_chunk + c + k, c0:c0 + n]
            a = act_fn(hi, got, ACT.Copy, last, *to.free.get(t, ()))
            v = tt(lo, got, hi.bitcast(F32), ALU.subtract, a)
            banks.give(bank, v)
            for i in range(k):
                to.ready[t, first_chunk + c + i] = (a, v)
        return last

    def products(blocks, x, epilogue, lead=SPLIT_SLOTS, tail=SPLIT_SLOTS, skew=0):
        pieces = [(b, j) for b in blocks for j in range(b.pieces)]
        held = {}

        def go(b, j, t):
            if t not in b.tiles:
                return
            operand, k0 = x(b)
            if (b, t) not in held:
                held[b, t], free = banks.take()
                pe.wait(*free)
            n, c0, slot = ROWS[t], FIRST_TOKEN[t], (b.at + j) % SPLIT_SLOTS
            o = held[b, t][0:n, 0:b.n]
            mark = None
            for i in range(PIECE_K):
                k = k0 + j * PIECE_K + i
                if (t, k) not in operand.ready:
                    flush()
                while (t, k) not in operand.ready:
                    chore()
                xh, xl = operand.hi[:, k, c0:c0 + n], operand.lo[:, k, c0:c0 + n]
                wh, wl = w_hi[:, slot, i, 0:b.n], w_lo[:, slot, i, 0:b.n]
                last = j == b.pieces - 1 and i == PIECE_K - 1
                mm_quiet(o, xh, wh, j == 0 and i == 0, False, *operand.ready[t, k], *splits[b.at + j])
                mm_quiet(o, xh, wl, False, False)
                if i == PIECE_K - 1:
                    mark = mm(o, xl, wh, False, last)
                else:
                    mm_quiet(o, xl, wh, False, last)
            operand.free[t] = (mark,)
            if t == b.tiles[-1]:
                release(mark)
            if j == b.pieces - 1:
                epilogue(b, t, held.pop((b, t)), mark)
            tick()

        if skew:
            for i in range(len(pieces) + skew):
                if i >= skew:
                    go(*pieces[i - skew], 1)
                if i < len(pieces):
                    go(*pieces[i], 0)
            return
        lead = min(lead, len(pieces))
        cut = max(lead, len(pieces) - tail)
        for t in ALL_TILES:
            for b, j in pieces[:lead]:
                go(b, j, t)
        for b, j in pieces[lead:cut]:
            for t in b.tiles:
                go(b, j, t)
        for t in ALL_TILES:
            for b, j in pieces[cut:]:
                go(b, j, t)

    def products_by_feature(blocks, epilogue):
        for b in blocks:
            held = []
            for f in range(b.n // P):
                bank, free = banks.take()
                held.append((bank, free))
            for j in range(b.pieces):
                slot = (b.at + j) % SPLIT_SLOTS
                for f, (bank, free) in enumerate(held):
                    if j == 0:
                        pe.wait(*free)
                    for i in range(PIECE_K):
                        k = j * PIECE_K + i
                        xh, xl = x_t.hi[:, k, :], x_t.lo[:, k, :]
                        wh, wl = (s[:, slot, i, f * P:(f + 1) * P] for s in (w_hi, w_lo))
                        pe.wait(*splits[b.at + j], *[m for t in ALL_TILES for m in x_t.ready[t, k]])
                        first, last = k == 0, k == KC - 1
                        mm_quiet(bank[:, 0:KEYS], wh, xh, first, False)
                        mm_quiet(bank[:, 0:KEYS], wh, xl, False, False)
                        mark = mm(bank[:, 0:KEYS], wl, xh, False, last)
                    if j == b.pieces - 1:
                        epilogue(b, f, bank, mark)
                    if f % 2:
                        tick()
                release(mark)
                for t in ALL_TILES:
                    x_t.free[t] = (mark,)

    def square_sum(source, *marks):
        n, width = source.shape
        ss = stat()[0:n, :]
        a = act_fn(junk[0:n, 0:width], source, ACT.Square, *marks, *last_square, accum_out=ss)
        last_square[:] = [a]
        return ss, a

    def rsqrt_of_halves(o, sums, eps):
        n = o.shape[0]
        m0, m = stat()[0:n, :], stat()[0:n, :]
        v = ts(m0, sums[0][0], 1.0 / D, eps, ALU.mult, ALU.add, sums[0][1])
        v = ts(m, sums[1][0], 1.0 / D, m0, ALU.mult, ALU.add, v, sums[1][1])
        return tt(o, m, minus_half[0:n, 0:1], ALU.pow, v, half_set, q=pool), (m, v)

    halves = (slice(0, COLS), slice(COLS, D))

    def settle(t, half):
        if callable(h_ready[t][half]):
            mark = h_ready[t][half](half)
            h_ready[t] = (mark, h_ready[t][1]) if half == 0 else (h_ready[t][0], mark)
        return h_ready[t][half]

    def pre_norm(t, gain, units=5):
        n = ROWS[t]
        marks = []
        x_t.forget(t)
        for half in range(2):
            s = halves[half]
            marks.append(tt(row[t][0:n, s], h[t][0:n, s], gain.ap(n, half * COLS, COLS), ALU.mult,
                            settle(t, half), gain.mark(), *row_free[t]))
        gain.done(marks[1])
        added = h_ready[t]

        def find_scale():
            r = stat()[0:n, :]
            sums = [square_sum(h[t][0:n, s], added[i]) for i, s in enumerate(halves)]
            p, x_t.mean[t] = rsqrt_of_halves(r, sums, EPS)
            x_t.scale[t] = (r, p)

        def turn_it():
            for half in range(2):
                last = turn_split(row[t][:, halves[half]], t, 4, x_t, 4 * half, marks[half])
            row_free[t] = (last,)

        defer(turn_it, units)
        defer(find_scale, 0)

    def pre_norm_whole(t, gain, units=0):
        n = ROWS[t]
        r = stat()[0:n, :]
        x_t.forget(t)
        sums = [square_sum(h[t][0:n, s], h_ready[t][i]) for i, s in enumerate(halves)]
        p, _ = rsqrt_of_halves(r, sums, EPS)
        marks = [stt(row[t][0:n, s], h[t][0:n, s], r, gain.ap(n, i * COLS, COLS), ALU.mult, ALU.mult, p,
                     gain.mark(), *row_free[t]) for i, s in enumerate(halves)]
        gain.done(marks[1])

        def turn_it():
            for half in range(2):
                last = turn_split(row[t][:, halves[half]], t, 4, x_t, 4 * half, marks[half])
            row_free[t] = (last,)

        defer(turn_it, units)

    parts = {}

    def post_norm_part(t, half, source, mark, bank, gain, then):
        ss, a = square_sum(source, mark)
        tmp, free = temps.take()
        v = tt(tmp[:, 0:COLS], source, gain.ap(P, half * COLS, COLS), ALU.mult,
               a if bank is not None else mark, gain.mark(), *free)
        if bank is not None:
            banks.give(bank, v)
        parts.setdefault(t, []).append((half, tmp, v, (ss, a)))
        if len(parts[t]) < 2:
            return
        both = parts.pop(t)
        r = stat()
        p, _ = rsqrt_of_halves(r, [x[3] for x in both], EPS)
        gain.done(v)
        both.sort(key=lambda x: x[0])

        def add(half):
            _, tmp, v, _ = both[half]
            to = h[t][:, halves[half]]
            ready = stt(to, tmp[:, 0:COLS], r, to, ALU.mult, ALU.add, p, v)
            temps.give(tmp, ready)
            return ready

        h_ready[t] = (add, add)
        then(t)

    def glu(name, region, then):
        hid = Operand(sb(f"{name}_hid_hi", [P, D_FF // P, KEYS], F32R, region),
                      sb(f"{name}_hid_lo", [P, D_FF // P, KEYS], F32R, region))
        fresh = region_marks()
        held = {}

        def hidden(b, t, bank, mark):
            n = ROWS[t]
            if b.name[0] == "gate":
                buf, free = temps.take()
                r, scaled = x_t.scale.get(t, (1.0, mark))
                a = act_fn(buf[0:n, 0:b.n], bank[0:n, 0:b.n], ACT.Silu, mark, scaled, *free, scale=r)
                held[t] = (buf, a)
                banks.give(bank, a)
                return
            buf, a = held.pop(t)
            r, scaled = x_t.scale.get(t, (1.0, mark))
            v = stt(buf[0:n, 0:b.n], bank[0:n, 0:b.n], r, buf[0:n, 0:b.n], ALU.mult, ALU.mult, mark, a, scaled)
            banks.give(bank, v)

            def turn_it():
                act.wait(*fresh)
                dve.wait(*fresh)
                temps.give(buf, turn_split(buf, t, b.n // P, hid, b.name[1] * (COLS // P), v))

            defer(turn_it, 5)

        products(stages[name + "_in"], lambda b: (x_t, 0), hidden)
        add_half(name, hid, then)

    def add_half(name, hid, then):
        def residual(b, t, bank, mark):
            n, c = ROWS[t], b.c0
            to = h[t][0:n, c:c + b.n]
            v = stt(to, bank[0:n, 0:b.n], 0.5, to, ALU.mult, ALU.add, mark)
            banks.give(bank, v)
            if b.name[1] == 0:
                h_ready[t] = (v,)
            else:
                h_ready[t] += (v,)
                then(t)

        products(stages[name + "_out"], lambda b: (hid, 0), residual)

    def region_marks():
        return [(q.sem, q.count) for q in (pe, act, dve) if q.count]

    pre = Gain(0, 3)
    for t in ALL_TILES:
        h_ready[t] = (h_ready[t], h_ready[t])
    pre_norm_whole(0, pre)
    pre_norm_whole(1, pre)
    split_next()
    pre_norm_whole(META, pre)
    flush()
    advance()

    a = pool.run(lambda e: e.memset(flip[:, :], 0.0))
    flip_set = select(flip[:, :], flip[:, :], -(P - 1), 1, [[1, P]], ALU.not_equal, 1.0, a)
    a = pool.run(lambda e: e.memset(causal[:, :], 0.0))
    causal_set = select(causal[:, :], causal[:, :], 0, 1, [[-1, P]], ALU.is_ge, NEG, a)
    a = pool.run(lambda e: e.memset(upto[:, :], 1.0))
    upto_set = select(upto[:, 0:P], upto[:, 0:P], 0, -1, [[1, P]], ALU.is_ge, 0.0, a)

    m_fa = small(pool, fa_raw[:, :, :], w["w_in"][0][:, C_FA:C_FA + HEADS].rearrange("(c p) n -> p c n", p=P))
    m_fb = small(pool, forget_b[:, :], w["forget_bias"].broadcast_to([P, HEADS]))
    m_sink = small(pool, sinks[:, :], w["swa_sinks"].broadcast_to([P, HEADS]))
    m_hg = [small(pool, head_gains[:, i, :], w[k].broadcast_to([P, HD]))
            for i, k in enumerate(("fox_q_norm", "fox_k_norm", "swa_q_norm", "swa_k_norm"))]

    masks_ready = [act_fn(o[:, :], i[:, :], ACT.Copy, m) for o, i, m in
                   ((ident_r, ident, ident_set), (causal_r, causal, causal_set))]

    mix_pre = Gain(1, 3)
    region = ExitStack()

    selector = sb("bias_selector_and_table", [N_BUCKETS + 1, U_ALL + HEADS], F32, region)
    sel_sb, table_sb = selector[:, 0:U_ALL], selector[:, U_ALL:U_ALL + HEADS]
    a = pool.run(lambda e: e.memset(table_sb, 1.0))
    m_table = small(pool, table_sb[0:N_BUCKETS, :], w["rel_bias_table"], a)
    m_sel = small(pool, sel_sb, w["bias_selector"])
    bias_dram = nc.dram_tensor("bias_rows", [HEADS, U_ALL], F32, kind="Internal").ap()
    bias_marks = []

    def bias_rows():
        for c in range(0, U_ALL, 512):
            n = min(512, U_ALL - c)
            bank, free = banks.take()
            a = mm(bank[0:HEADS, 0:n], table_sb, sel_sb[:, c:c + n], True, True, m_table, m_sel, *free)
            tmp, free = temps.take()
            v = dve.run(lambda e, o=tmp[0:HEADS, 0:n], s=bank[0:HEADS, 0:n]: e.tensor_copy(o, s), a, *free)
            banks.give(bank, v)
            bias_marks.append(small(sp, bias_dram[:, c:c + n], tmp[0:HEADS, 0:n], v))
            temps.give(tmp, bias_marks[-1])

    hid = Operand(sb("ffn1_hid_hi", [P, D_FF // P, KEYS], F32R, region),
                  sb("ffn1_hid_lo", [P, D_FF // P, KEYS], F32R, region))

    silu = sb("silu_of_gate", [P, COLS // P, KEYS], F32, region)

    def hidden_by_feature(b, f, bank, mark):
        kind, i = b.name
        k = i * (COLS // P) + f
        hi, lo = hid.hi[:, k, :], hid.lo[:, k, :]
        got, kept = bank[:, 0:KEYS], silu[:, f, :]
        if kind == "gate":
            silu_ready[f] = act_fn(kept, got, ACT.Silu, mark, *silu_free.get(f, ()))
            banks.give(bank, silu_ready[f])
            return
        v = tt(kept, got, kept, ALU.mult, mark, silu_ready[f])
        banks.give(bank, v)
        a = act_fn(hi, kept, ACT.Copy, v)
        v = tt(lo, kept, hi.bitcast(F32), ALU.subtract, a)
        silu_free[f] = (v,)
        for t in ALL_TILES:
            hid.ready[t, k] = (a, v)

    silu_ready, silu_free = {}, {}
    defer(bias_rows, 16)
    products_by_feature(stages["ffn1_in"], hidden_by_feature)
    add_half("ffn1", hid, lambda t: pre_norm(t, mix_pre))
    region.close()

    region = ExitStack()

    def rsb(name, shape, dt=F32):
        return sb(name, shape, dt, region)

    fresh = region_marks()
    va, va_m = rsb("va", [P, 2, FOX_W]), rsb("va_meta", [N_META, FOX_W])
    vb, vb_m = rsb("vb", [P, 2, KV_W]), rsb("vb_meta", [N_META, KV_W])
    gates = rsb("gates", [P, 2, 2 * D])
    qa_t, qb_t = rsb("qa_t", [FOX_D, HEADS, SEQ]), rsb("qb_t", [P, 4, SEQ])
    ka_t, kb_t = rsb("ka_t", [FOX_D, HEADS, KEYS]), rsb("kb_t", [P, SWA_KV, KEYS])
    window_b = rsb("window_bias", [P, HEADS, 2 * P])
    meta_b = rsb("meta_bias", [P, 2, HEADS, N_META])
    prob = Slots([rsb(f"prob{i}", [P, KEYS]) for i in range(3)])
    prob_t = Slots([rsb(f"prob_t{i}", [P, 3, P]) for i in range(3)])
    log_f = rsb("log_f", [P, 3, HEADS])
    log_f_sum = rsb("log_f_sum", [P, 3, HEADS])

    def diagonals(u0, width):
        return bass.AP(bias_dram.tensor, u0, [[1, P], [U_ALL, HEADS], [1, width]])

    bias_loaded = [small(pool, window_b[:, :, :], diagonals(0, 2 * P), *fresh, *bias_marks),
                   small(pool, meta_b[:, 0, :, :], diagonals(U_WINDOW, N_META)),
                   small(pool, meta_b[:, 1, :, :], diagonals(U_WINDOW + U_META, N_META))]
    act.wait(*fresh)
    dve.wait(*fresh)
    key0 = (N_META, N_META + P, 0)
    v_ready, gate_ready = {}, {}

    fox_rows = [gates[:, :, :].rearrange("p t c -> p (t c)")[:, i * HEADS * FOX_D:(i + 1) * HEADS * FOX_D]
                for i in range(5)]
    fox_turned = []

    def head_norm(t, source, heads, gain_i, twice, mark, then, stride=HD, buf=None):
        n = ROWS[t]
        width = heads * HD
        buf, free = temps.take() if buf is None else (buf, ())
        a = act_fn(buf[0:n, 0:width], source, ACT.Square, mark, *free)
        ss, m, r, e = stat(heads)[0:n, :], stat(heads)[0:n, :], stat(heads)[0:n, :], stat()[0:n, :]
        mean, mean_ready = x_t.mean[t]
        v = ts(e, mean, EPS, None, ALU.mult, None, mean_ready)
        v = reduce(ss, buf[0:n, 0:width].rearrange("p (h d) -> p h d", d=HD), ALU.add, a)
        v = ts(m, ss, 1.0 / HD, e, ALU.mult, ALU.add, v)
        p = tt(r, m, minus_half[0:n, 0:heads], ALU.pow, v, half_set, q=pool)

        def scale_rows():
            by_head = buf[0:n, 0:heads * stride].rearrange("p (h d) -> p h d", d=stride)[:, :, 0:HD]
            v = tt(by_head, source.rearrange("p (h d) -> p h d", d=HD),
                   r.unsqueeze(2).broadcast_to([n, heads, HD]), ALU.mult, p)
            read = v
            g = head_gains[0:n, gain_i, :].unsqueeze(1).broadcast_to([n, heads, HD])
            if not twice:
                v = tt(by_head, by_head, g, ALU.mult, v, m_hg[gain_i])
            else:
                for c in range(2):
                    last = tt(buf[0:n, 2 * width:4 * width].rearrange("p (h c d) -> p h c d", c=2, d=HD)[:, :, c, :],
                              by_head, g, ALU.mult, v, m_hg[gain_i])
                v = last
            then(buf, read, v)

        defer(scale_rows, 2 if stride == HD else 3)

    def store_turned(t, buf, c0, chunks, to, col0, scale, mark):
        def turn_it():
            n = ROWS[t]
            bank, free = banks.take()
            last = None
            for i in range(chunks):
                last = turn(bank[:, i * n:(i + 1) * n], buf[0:n, c0 + i * P:c0 + (i + 1) * P], mark, *free)
            a = act_fn(to[:, 0:chunks, col0:col0 + n], bank[:, 0:chunks * n].rearrange("p (c n) -> p c n", n=n),
                       ACT.Copy, last, scale=scale)
            banks.give(bank, a)
            temps.give(buf, last)
            swa_ready.append(a)

        defer(turn_it, 4)

    def store_fox(t, buf, to, col0, scale, mark):
        n = ROWS[t]
        rows = buf[0:n, 0:HEADS * FOX_D].rearrange("p (h d) -> p h d", d=FOX_D)
        one, c = (1, 0) if to is qa_t else (0, 1)

        def turn_it():
            factor = 1 / scale if to is qa_t else -1.0
            v1 = dve.run(lambda e: e.memset(rows[:, :, HD + one:HD + one + 1], 1 / scale), mark)
            v1 = ts(rows[:, :, HD + c], log_f_sum[0:n, t, :], factor, None, ALU.mult, None, v1, *sum_ready)

            def turn_heads():
                last = None
                for g in range(0, HEADS, 4):
                    bank, free = banks.take()
                    for i in range(4):
                        last = turn(bank[0:FOX_D, i * n:(i + 1) * n], rows[:, g + i, :], v1, *free)
                    a = act_fn(to[:, g:g + 4, col0:col0 + n],
                               bank[0:FOX_D, 0:4 * n].rearrange("p (c n) -> p c n", n=n), ACT.Copy, last, scale=scale)
                    banks.give(bank, a)
                fox_turned.append(last)
                fox_ready.append(a)

            defer(turn_heads, 6)

        defer(turn_it, 1)

    fox_ready, swa_ready, sum_ready = [], [], []

    def mixer_in(b, t, bank, mark):
        n = ROWS[t]
        got = bank[0:n, 0:b.n]

        def store(store_fn, *args):
            def go(buf, read, v):
                banks.give(bank, read)
                store_fn(t, buf, *args, v)

            return go

        if b.name == "ka":
            head_norm(t, got, HEADS, 1, False, mark, store(store_fox, ka_t, key0[t], 1.0), FOX_D, fox_rows.pop())
        elif b.name == "qa":
            head_norm(t, got, HEADS, 0, False, mark, store(store_fox, qa_t, P * t, HD ** -0.5), FOX_D, fox_rows.pop())
        elif b.name == "qb":
            head_norm(t, got, HEADS, 2, False, mark, store(store_turned, 0, 4, qb_t, P * t, HD ** -0.5))
        elif b.name == "va":
            to = va[:, t, :] if t != META else va_m[:, :]
            rx, scaled = x_t.scale[t]
            a = act_fn(to, got, ACT.Copy, mark, scaled, scale=rx)
            v_ready["fox", t] = a
            banks.give(bank, a)
            if t == META:
                defer(forget_gates, 1)
        elif b.name == "kvb":
            to = vb[:, t, :] if t != META else vb_m[:, :]
            rx, scaled = x_t.scale[t]
            v_ready["swa", t] = act_fn(to, bank[0:n, KV_W:2 * KV_W], ACT.Copy, mark, scaled, scale=rx)

            def keys_ready(buf, read, v):
                banks.give(bank, read, v_ready["swa", t])
                store_turned(t, buf, 2 * KV_W, SWA_KV, kb_t, key0[t], 1.0, v)

            head_norm(t, bank[0:n, 0:KV_W], SWA_KV, 3, True, v_ready["swa", t], keys_ready)
        else:
            i = b.name[1]
            rx, scaled = x_t.scale[t]
            v = ts(gates[:, t, i * COLS:(i + 1) * COLS], got, rx, None, ALU.mult, None, mark, scaled, *fox_turned)
            gate_ready[t, i] = v
            banks.give(bank, v)

    a_fa = act_fn(fa_hi[:, :, :], fa_raw[:, :, :], ACT.Copy, m_fa)
    v_fa = tt(fa_lo[:, :, :], fa_raw[:, :, :], fa_hi[:, :, :].bitcast(F32), ALU.subtract, a_fa)
    log_f_ready = {}

    def forget_gates():
        f_bank, free = banks.take()
        for t in ALL_TILES:
            n, c0 = ROWS[t], FIRST_TOKEN[t]
            o = f_bank[0:n, t * HEADS:(t + 1) * HEADS]
            for k in range(KC):
                xh, xl = x_t.hi[:, k, c0:c0 + n], x_t.lo[:, k, c0:c0 + n]
                mm_quiet(o, xh, fa_hi[:, k, :], k == 0, False, v_fa, *free, *x_t.ready[t, k])
                mm_quiet(o, xh, fa_lo[:, k, :], False, False)
                mark = mm(o, xl, fa_hi[:, k, :], False, k == KC - 1)
        fx, fl, fe = stat(3 * HEADS), stat(3 * HEADS), stat(3 * HEADS)
        parts = [(t, ROWS[t], slice(t * HEADS, (t + 1) * HEADS)) for t in ALL_TILES]
        exps = {}
        for t, n, s in parts:
            rx, scaled = x_t.scale[t]
            v = stt(fx[0:n, s], f_bank[0:n, s], rx, forget_b[0:n, :], ALU.mult, ALU.add, mark, m_fb, scaled)
            v1 = ts(fl[0:n, s], fx[0:n, s], -1.0, None, ALU.mult, None, v)
            v2 = tt(fl[0:n, s], fl[0:n, s], fx[0:n, s], ALU.min, v1)
            exps[t] = act_fn(fe[0:n, s], fl[0:n, s], ACT.Exp, v2)
        lns = {t: act_fn(fe[0:n, s], fe[0:n, s], ACT.Ln, exps[t], bias=1.0) for t, n, s in parts}

        def subtract():
            for t, n, s in parts:
                log_f_ready[t] = stt(log_f[0:n, t, :], fx[0:n, s], 0.0, fe[0:n, s], ALU.min, ALU.subtract, lns[t])
            defer(sum_log_f, 2)

        defer(subtract, 3)
        banks.give(f_bank, v)

    def sum_log_f():
        bank, free = banks.take()
        for t in ALL_TILES:
            n = ROWS[t]
            before = {META: [], 0: [META], 1: [META, 0]}[t]
            for part in before:
                mm_quiet(bank[0:n, t * HEADS:(t + 1) * HEADS], upto[0:ROWS[part], P:P + n], log_f[0:ROWS[part], part, :],
                         part == META, False, upto_set, *free, *log_f_ready.values())
            last = mm(bank[0:n, t * HEADS:(t + 1) * HEADS], upto[0:n, 0:n], log_f[0:n, t, :], not before, True)
        v = None
        for t in ALL_TILES:
            n = ROWS[t]
            v = dve.run(lambda e, o=log_f_sum[0:n, t, :], i=bank[0:n, t * HEADS:(t + 1) * HEADS]:
                        e.tensor_copy(o, i), last)
        banks.give(bank, v)
        sum_ready.append(v)

    def key_parts(t):
        return [(0, N_META, META), (N_META, P, 0)] + ([(N_META + P, P, 1)] if t else [])

    def fox_scores(t, hd):
        keys = N_META + P * (t + 1)
        bank, free = banks.take()
        mm_quiet(bank[:, 0:keys], qa_t[:, hd, P * t:P * t + P], ka_t[:, hd, 0:keys], True, False, *fox_ready, *free)
        last = mm(bank[:, keys - P:keys], ident_r[:, :], causal_r[:, :], False, True, *masks_ready)
        return bank, last, keys

    def swa_scores(t, hd):
        keys = N_META + P * (t + 1)
        c, b, g = hd // 2, HD * (hd % 2), hd // (HEADS // SWA_KV)
        bank, free = banks.take()
        o = bank[:, 0:keys]
        mm_quiet(o, qb_t[b:b + HD, c, P * t:P * t + P], kb_t[b:b + HD, g, 0:keys], True, False, *swa_ready, *free)
        mm_quiet(bank[:, 0:N_META], flip[:, :], meta_b[:, t, hd, :], False, False, flip_set, *bias_loaded)
        last = mm(bank[:, N_META:keys], flip[:, :], window_b[:, hd, P * (1 - t):2 * P], False, True)
        return bank, last, keys

    def softmax(bank, mark, keys, sink, o_sum):
        mx, neg = stat(), stat()
        v = reduce(mx, bank[:, 0:keys], ALU.max, mark)
        if sink is None:
            v = ts(neg, mx, -1.0, None, ALU.mult, None, v)
        else:
            v = ts(neg, mx, sink, -1.0, ALU.max, ALU.mult, v, m_sink)
        pr, free = prob.take()
        if sink is None:
            a = act_fn(pr[:, 0:keys], bank[:, 0:keys], ACT.Exp, v, *free, bias=neg, accum_out=o_sum)
        else:
            part, extra = stat(), stat()
            a = act_fn(pr[:, 0:keys], bank[:, 0:keys], ACT.Exp, v, *free, bias=neg, accum_out=part)
            a2 = act_fn(extra, neg, ACT.Exp, v, bias=sink)
            tt(o_sum, part, extra, ALU.add, a2)
        banks.give(bank, a)
        return pr, a

    def turn_prob(pr, mark, t):
        bank, free = banks.take()
        last = None
        for i, (k0, n, _) in enumerate(key_parts(t)):
            last = turn(bank[0:n, i * P:(i + 1) * P], pr[:, k0:k0 + n], mark, *free)
        prob.give(pr, last)
        pt, free = prob_t.take()
        act_fn(pt[0:N_META, 0, :], bank[0:N_META, 0:P], ACT.Copy, last, *free)
        k = t + 1
        a = act_fn(pt[:, 1:1 + k, :], bank[:, P:P + P * k].rearrange("p (k n) -> p k n", n=P), ACT.Copy, last, *free)
        banks.give(bank, a)
        return pt, (a,)

    sums = {kind: stat(2 * HEADS) for kind in ("fox", "swa")}

    def attend(kind, t):
        while len(fox_ready if kind == "fox" else swa_ready) < len(ALL_TILES) + len(TILES):
            yield
        o_bank, o_free = banks.take()
        total = sums[kind][:, t * HEADS:(t + 1) * HEADS]
        scored, turned = {}, {}
        for i in range(HEADS + 4):
            if i < HEADS:
                sc = fox_scores(t, i) if kind == "fox" else swa_scores(t, i)
                scored[i] = softmax(*sc, None if kind == "fox" else sinks[:, i:i + 1], total[:, i:i + 1])
                if i == HEADS - 1:
                    all_summed = [(act.sem, act.count), (dve.sem, dve.count)]
            if 2 <= i < HEADS + 2:
                turned[i - 2] = turn_prob(*scored.pop(i - 2), t)
            if i >= 4:
                hd = i - 4
                pt, marks = turned.pop(hd)
                ks = key_parts(t)
                for j, (_, n, part) in enumerate(ks):
                    if kind == "fox":
                        v = (va[:, part, :] if part != META else va_m[:, :])[:, hd * HD:(hd + 1) * HD]
                    else:
                        g = hd // (HEADS // SWA_KV)
                        v = (vb[:, part, :] if part != META else vb_m[:, :])[:, g * HD:(g + 1) * HD]
                    last = mm(o_bank[:, hd * HD:(hd + 1) * HD], pt[0:n, j, :], v, j == 0, j == len(ks) - 1,
                              *marks, *o_free, *[v_ready[kind, p] for _, _, p in ks])
                prob_t.give(pt, last)
            if i < HEADS + 3:
                yield
        inv = stat(HEADS)
        v = dve.run(lambda e: e.reciprocal(inv, total), *all_summed)
        c0 = 0 if kind == "fox" else FOX_W
        to = row[t][:, c0:c0 + FOX_W].rearrange("p (h d) -> p h d", d=HD)
        v = tt(to, o_bank[:, :].rearrange("p (h d) -> p h d", d=HD), inv.unsqueeze(2).broadcast_to([P, HEADS, HD]),
               ALU.mult, v, last, *row_free[t])
        banks.give(o_bank, v)
        attended[kind, t] = v
        if gates_done:
            turn_kind(kind, t)

    attended, gates_done = {}, []

    def turn_kind(kind, t):
        half = 0 if kind == "fox" else 1
        last = turn_split(row[t][:, halves[half]], t, 4, x_t, 4 * half, attended.pop((kind, t)))
        row_free[t] = (last,)

    products(stages["mix_in"][:3], lambda b: (x_t, 0), mixer_in, tail=0)
    chores.extend(attend(kind, t) for kind in ("fox", "swa") for t in TILES)
    products(stages["mix_in"][3:] + stages["gates"], lambda b: (x_t, 0), mixer_in, lead=0, tail=0)
    for t in TILES:
        x_t.forget(t)
    gates_done.append(True)
    for kind, t in list(attended):
        turn_kind(kind, t)

    def branch(b, t, bank, mark):
        kind, i = b.name
        c = i * COLS + (0 if kind == "fox" else D)
        g = gates[:, t, c:c + COLS]
        a = act_fn(g, g, ACT.Sigmoid, gate_ready[t, c // COLS])
        v = tt(g, bank[:, :], g, ALU.mult, mark, a)
        banks.give(bank, v)
        if kind == "swa":
            y = gates[:, t, i * COLS:(i + 1) * COLS]
            v = tt(y, y, g, ALU.add, v)
            y_ready[t, i] = v
            if i == 1:
                def turn_it():
                    x_t.forget(t)
                    for half in range(2):
                        turn_split(gates[:, t, halves[half]], t, 4, x_t, 4 * half, y_ready[t, half])

                defer(turn_it, 4)

    y_ready = {}
    products(stages["branch"], lambda b: (x_t, 0 if b.name[0] == "fox" else 4), branch, lead=3, tail=5)

    ffn2_pre = Gain(2, 2)

    def mixer_out(b, t, bank, mark):
        to = h[t][:, b.c0:b.c0 + b.n]
        v = tt(to, bank[:, :], to, ALU.add, mark)
        banks.give(bank, v)
        if b.name[1] == 0:
            h_ready[t] = (v,)
        else:
            h_ready[t] += (v,)
            pre_norm(t, ffn2_pre)

    products(stages["mix_out"], lambda b: (x_t, 0), mixer_out, skew=SPLIT_SLOTS - 1)
    region.close()

    region = ExitStack()
    gmlp_pre = Gain(3, 2)
    glu("ffn2", region, lambda t: pre_norm(t, gmlp_pre))
    region.close()

    def load_p(layer):
        marks = p_free[0]
        m = small(pool, p_rows[:, :, :], w["p_2"][layer, 0].rearrange("(t p) n -> p t n", p=P), *marks)

        def turn_it():
            for t in TILES:
                p_t.forget(t)
                last = turn_split(p_rows[:, t, :], t, PLE_DIM // P, p_t, 0, m)
            p_free[0] = (last,)

        return turn_it

    p_free = [()]

    def mlp(i, region, pre_next):
        hid = Operand(sb(f"mlp{i}_hid_hi", [P, D_FF_2 // P, SEQ], F32R, region),
                      sb(f"mlp{i}_hid_lo", [P, D_FF_2 // P, SEQ], F32R, region))
        fresh = region_marks()

        def hidden(b, t, bank, mark):
            buf, free = temps.take()
            r, scaled = x_t.scale[t]
            a = act_fn(buf[:, 0:COLS], bank[:, :], ACT.Relu, mark, scaled, *free, scale=r)
            banks.give(bank, a)
            v = tt(buf[:, 0:COLS], buf[:, 0:COLS], buf[:, 0:COLS], ALU.mult, a)

            def turn_it():
                act.wait(*fresh)
                dve.wait(*fresh)
                temps.give(buf, turn_split(buf, t, COLS // P, hid, b.name[1] * (COLS // P), v))

            defer(turn_it, 5)

        products(stages["mlp_in", i], lambda b: (x_t, 0), hidden)
        gain = Gain(gain_at["ffn_post", i], 2)
        products(stages["mlp_out", i], lambda b: (hid, 0),
                 lambda b, t, bank, mark: post_norm_part(t, b.name[1], bank[:, :], mark, bank, gain, pre_next))

    gain_at = {("ffn_post", 0): 8, ("ffn_post", 1): 15, ("ple_b", 0): 10, ("ple_b", 1): 17,
               ("ple_post", 0): 11, ("ple_post", 1): 18}

    def ple(i, then):
        bias, gain = Gain(gain_at["ple_b", i], 4), Gain(gain_at["ple_post", i], 2)
        held = {}

        def gated(b, t, bank, mark):
            kind, c = b.name
            if kind == "gate":
                buf, free = temps.take()
                r, scaled = x_t.scale[t]
                v = stt(buf[:, 0:COLS], bank[:, :], r, bias.ap(P, c * COLS, COLS), ALU.mult, ALU.add, mark, bias.mark(),
                        scaled, *free)
                banks.give(bank, v)
                bias.done(v)
                held[t] = (buf, act_fn(buf[:, 0:COLS], buf[:, 0:COLS], ACT.Sigmoid, v))
            else:
                buf, a = held.pop(t)
                to = row[t][:, c * COLS:(c + 1) * COLS]
                v = tt(to, bank[:, :], buf[:, 0:COLS], ALU.mult, mark, a, *row_free[t])
                banks.give(bank, v)
                temps.give(buf, v)
                post_norm_part(t, c, to, v, None, gain, then)

        products(stages["ple", i], lambda b: (x_t if b.name[0] == "gate" else p_t, 0), gated, lead=5, tail=5)

    region = ExitStack()
    fresh = region_marks()
    z = rsb("z", [P, 2, 2 * D])
    ws_rows = rsb("w_s_rows", [P, HEADS, P])
    ws_t = rsb("w_s_t", [P, HEADS, P])
    b_s = rsb("b_s", [P, HEADS])
    m_ws = small(pool, ws_rows[:, :, :], w["a_w_s_2"][0].rearrange("g t s -> t g s"), *fresh)
    m_bs = small(pool, b_s[:, :], w["a_b_s_2"][0].rearrange("g t -> t g"), allow_slow_non_contiguous=True)
    turn_p = load_p(0)
    act.wait(*fresh)
    dve.wait(*fresh)
    ws_marks = []

    def turn_ws():
        for g0 in range(0, HEADS, 4):
            bank, free = banks.take()
            for i in range(4):
                last = turn(bank[:, i * P:(i + 1) * P], ws_rows[:, g0 + i, :], m_ws, *free)
            v = tt(ws_t[:, g0:g0 + 4, :], bank[:, :].rearrange("p (g t) -> p g t", t=P),
                   upto[:, 0:P].unsqueeze(1).broadcast_to([P, 4, P]), ALU.mult, last, upto_set)
            banks.give(bank, v)
            ws_marks.append(v)

    z_sum = {t: [] for t in TILES}
    ln_g, ln_b = Gain(4, 2), Gain(5, 2)

    def gmlp_in(b, t, bank, mark):
        i = b.name[1]
        rx, scaled = x_t.scale[t]
        kw = {}
        if i >= 2:
            s = stat()
            z_sum[t].append(s)
            kw = {"accum_out": s}
        cols = z[:, t, i * COLS:(i + 1) * COLS]
        a = act_fn(cols, bank[:, :], ACT.Gelu_apprx_tanh, mark, scaled, scale=rx, **kw)
        banks.give(bank, a)
        v_rows = z[:, t, D:2 * D]
        if i == 2:
            return
        if i == 3:
            total, minus_mean, ss, r = stat(), stat(), stat(), stat()
            v = tt(total, z_sum[t][0], z_sum[t][1], ALU.add, a)
            v = ts(minus_mean, total, -1.0 / D, None, ALU.mult, None, v)
            a = act_fn(row[t][:, :], v_rows, ACT.Square, v, *row_free[t], bias=minus_mean, accum_out=ss)
            row_free[t] = (a,)
            p = rsqrt_mean(r, ss, D, LN_EPS, a)
            v = ts(v_rows, v_rows, minus_mean, r, ALU.add, ALU.mult, p)
            v = tt(v_rows, v_rows, ln_g.ap(P), ALU.mult, v, ln_g.mark())
            ln_g.done(v)
            v = tt(v_rows, v_rows, ln_b.ap(P), ALU.add, v, ln_b.mark())
            ln_b.done(v)

            def mix_tokens():
                mixed = []
                for g0 in range(0, HEADS, 4):
                    bank, free = banks.take()
                    for g in range(g0, g0 + 4):
                        last = mm(bank[:, (g - g0) * P:(g - g0 + 1) * P], ws_t[:, g, :],
                                  v_rows[:, g * P:(g + 1) * P], True, True, v, *ws_marks, *free)
                    for g in range(g0, g0 + 4):
                        o = act_fn(v_rows[:, g * P:(g + 1) * P], bank[:, (g - g0) * P:(g - g0 + 1) * P],
                                   ACT.Identity, last, m_bs, bias=b_s[:, g:g + 1])
                    banks.give(bank, o)
                    mixed.append(o)
                s_marks[t] = mixed

            defer(mix_tokens, 9)
            return

        def gate_u():
            y = z[:, t, i * COLS:(i + 1) * COLS]
            v = tt(y, y, z[:, t, (i + 2) * COLS:(i + 3) * COLS], ALU.mult, a, s_marks[t][i])
            if i == 0:
                half_done[t] = v
                return

            def turn_it():
                x_t.forget(t)
                turn_split(z[:, t, 0:COLS], t, 4, x_t, 0, half_done[t])
                turn_split(z[:, t, COLS:D], t, 4, x_t, 4, v)

            defer(turn_it, 4)

        defer(gate_u, 1)

    s_marks, half_done = {}, {}
    defer(turn_ws, 8)
    defer(turn_p, 1)
    products(stages["gmlp_in"], lambda b: (x_t, 0), gmlp_in)
    mix_post, ffn_pre = Gain(6, 2), Gain(7, 2)
    products(stages["gmlp_out"], lambda b: (x_t, 0),
             lambda b, t, bank, mark: post_norm_part(t, b.name[1], bank[:, :], mark, bank, mix_post,
                                                     lambda t: pre_norm(t, ffn_pre)), skew=SPLIT_SLOTS - 1)
    region.close()

    region = ExitStack()
    ple_pre = Gain(9, 2)
    mlp(0, region, lambda t: pre_norm(t, ple_pre))
    region.close()
    turn_p = load_p(1)

    lambda_init = 0.8 - 0.6 * math.exp(-0.3)
    region = ExitStack()
    fresh = region_marks()
    qk = rsb("qk_rows", [P, 2, 2 * D])
    vv = rsb("v_rows", [P, 2, D])
    q_t, k_t = rsb("q_t", [P, HEADS, SEQ]), rsb("k_t", [P, HEADS, SEQ])
    prob2 = Slots([rsb(f"prob2_{i}", [P, 2, SEQ]) for i in range(3)])
    diff = Slots([rsb(f"diff{i}", [P, SEQ]) for i in range(4)])
    diff_t = Slots([rsb(f"diff_t{i}", [P, 2, P]) for i in range(3)])
    rot = [rsb(f"rot{i}", [P, 2, 8, ROT // 2]) for i in range(4)]
    pos_i = rsb("positions", [P, 2], I32)
    lam_in = rsb("lambda_in", [P, 4, HD])
    subln = rsb("subln_g", [P, P])
    freq = rsb("frequencies", [P, ROT // 2])
    angles = rsb("angles", [P, 8, 2, ROT // 2])
    m_pos = small(pool, pos_i[:, :], w["positions_2"][0].rearrange("(t p) -> p t", p=P), *fresh,
                  allow_slow_non_contiguous=True)
    m_lam = [small(pool, lam_in[:, i, :], w[k].broadcast_to([P, HD]))
             for i, k in enumerate(("b_lam_q1_2", "b_lam_k1_2", "b_lam_q2_2", "b_lam_k2_2"))]
    m_sub = small(pool, subln[:, :], w["b_subln_g_2"].broadcast_to([P, P]))
    m_frq = small(pool, freq[:, :], w["frequencies"].broadcast_to([P, ROT // 2]))

    minus_lam = stat()
    sin_, cos_ = angles[:, 4, :, :], angles[:, 5, :, :]
    ready = {}

    def set_up():
        dve.wait(*fresh)
        act.wait(*fresh)

        lam_sum, lam_exp = stat(2), stat(2)
        v = tt(lam_in[:, 0, :], lam_in[:, 0, :], lam_in[:, 1, :], ALU.mult, m_lam[0], m_lam[1])
        v2 = tt(lam_in[:, 2, :], lam_in[:, 2, :], lam_in[:, 3, :], ALU.mult, m_lam[2], m_lam[3])
        v = reduce(lam_sum[:, 0:1], lam_in[:, 0, :], ALU.add, v)
        v = reduce(lam_sum[:, 1:2], lam_in[:, 2, :], ALU.add, v2)
        a = act_fn(lam_exp, lam_sum, ACT.Exp, v)
        v = tt(minus_lam, lam_exp[:, 1:2], lam_exp[:, 0:1], ALU.subtract, a)
        ready["lambda"] = ts(minus_lam, minus_lam, lambda_init, None, ALU.subtract, None, v)
        ready["subln"] = ts(subln[:, :], subln[:, :], 1.0 - lambda_init, None, ALU.mult, None, m_sub)

        two_pi = 2 * math.pi
        part1 = 6.28125
        part2 = float(np.float32(np.round((two_pi - part1) * 2 ** 20) / 2 ** 20))
        part3 = float(np.float32(two_pi - part1 - part2))
        big = 1.5 * 2.0 ** 23
        pos_f = stat(2)
        v = dve.run(lambda e: e.tensor_copy(pos_f, pos_i[:, :]), m_pos)
        ang, turns, cut, rest = (angles[:, i, :, :] for i in range(4))
        for t in TILES:
            v0 = ts(ang[:, t, :], freq[:, :], pos_f[:, t:t + 1], None, ALU.mult, None, v, m_frq)
        trig_ready = []
        for shift, o in ((0.0, sin_), (0.25, cos_)):
            v1 = ts(turns, ang, 1.0 / two_pi, shift, ALU.mult, ALU.add, v0, *trig_ready)
            v1 = ts(turns, turns, big, None, ALU.add, None, v1)
            v1 = ts(turns, turns, big, None, ALU.subtract, None, v1)
            v1 = stt(rest, turns, -part1, ang, ALU.mult, ALU.add, v1)
            v1 = stt(rest, turns, -part2, rest, ALU.mult, ALU.add, v1)
            v1 = stt(rest, turns, -part3, rest, ALU.mult, ALU.add, v1)
            v1 = ts(rest, rest, two_pi * shift, None, ALU.add, None, v1)
            limit = 3.1415925
            v1 = ts(rest, rest, limit, -limit, ALU.min, ALU.max, v1)
            trig_ready = [act_fn(o, rest, ACT.Sin, v1)]
        ready["trig"] = trig_ready

    attn_pre = Gain(12, 2)
    ple(0, lambda t: pre_norm(t, attn_pre))

    v_marks, rot_free = {0: [], 1: []}, []
    qk_marks = {}
    turned_qk = {0: [], 1: []}

    def qkv(b, t, bank, mark):
        i = b.name[1]
        rx, scaled = x_t.scale[t]
        if i >= 4:
            a = act_fn(vv[:, t, (i - 4) * COLS:(i - 3) * COLS], bank[:, :], ACT.Copy, mark, scaled, scale=rx)
            banks.give(bank, a)
            v_marks[i - 4].append(a)
            return
        a = act_fn(qk[:, t, i * COLS:(i + 1) * COLS], bank[:, :], ACT.Copy, mark, scaled, scale=rx)
        banks.give(bank, a)
        if i >= 2:
            qk_marks[t] = a
            return
        x = qk[:, t, :].rearrange("p (s c g d) -> p s c g d", s=2, c=2, d=HD)[:, :, i, :, :]
        x1, x2 = x[:, :, :, 0:ROT // 2], x[:, :, :, ROT // 2:ROT]
        shape = [P, 2, 8, ROT // 2]
        c, s = [o[:, t, :].unsqueeze(1).unsqueeze(1).broadcast_to(shape) for o in (cos_, sin_)]
        tt(rot[0][:, :, :, :], x1, c, ALU.mult, *ready["trig"], a, qk_marks[t], *rot_free)
        tt(rot[1][:, :, :, :], x2, s, ALU.mult)
        tt(rot[2][:, :, :, :], x2, c, ALU.mult)
        v = tt(rot[3][:, :, :, :], x1, s, ALU.mult)
        tt(x1, rot[0][:, :, :, :], rot[1][:, :, :, :], ALU.subtract, v)
        v = tt(x2, rot[2][:, :, :, :], rot[3][:, :, :, :], ALU.add)
        rot_free[:] = [v]

        def turn_it():
            for to, c0, scale in ((q_t, 0, HD ** -0.5), (k_t, D, 1.0)):
                bank, free = banks.take()
                for j in range(4):
                    g = 4 * i + j
                    last = turn(bank[:, j * P:(j + 1) * P], qk[:, t, c0 + g * P:c0 + (g + 1) * P], v, *free)
                a = act_fn(to[:, 4 * i:4 * i + 4, P * t:P * t + P], bank[:, :].rearrange("p (g n) -> p g n", n=P),
                           ACT.Copy, last, scale=scale)
                banks.give(bank, a)
                turned_qk[i].append(a)

        defer(turn_it, 5)

    defer(turn_p, 4)
    defer(set_up, 9)
    products(stages["qkv"], lambda b: (x_t, 0), qkv, tail=0)

    def diff_scores(t, hd):
        keys = P * (t + 1)
        bank, free = banks.take()
        last = free[0] if free else ident_set
        for c in range(2):
            b = HD * c
            mm_quiet(bank[:, c * SEQ:c * SEQ + keys], q_t[b:b + HD, hd, P * t:P * t + P], k_t[b:b + HD, hd, 0:keys],
                     True, False, *turned_qk[hd // 4], *free, last)
            last = mm(bank[:, c * SEQ + keys - P:c * SEQ + keys], ident_r[:, :], causal_r[:, :], False, True, *masks_ready)
        mx, neg, total, inv = stat(2), stat(2), stat(2), stat(2)
        got = bank[:, :].rearrange("p (c k) -> p c k", c=2)
        v = reduce(mx, got[:, :, 0:keys], ALU.max, last)
        v = ts(neg, mx, -1.0, None, ALU.mult, None, v)
        pr, free = prob2.take()
        for c in range(2):
            a = act_fn(pr[:, c, 0:keys], got[:, c, 0:keys], ACT.Exp, v, *free, bias=neg[:, c:c + 1],
                       accum_out=total[:, c:c + 1])
        banks.give(bank, a)
        v = dve.run(lambda e: e.reciprocal(inv, total), a)
        w1 = stat()
        v = tt(w1, inv[:, 1:2], minus_lam, ALU.mult, v, ready["lambda"])
        v = ts(pr[:, 1, 0:keys], pr[:, 1, 0:keys], w1, None, ALU.mult, None, v)
        df, free = diff.take()
        v = stt(df[:, 0:keys], pr[:, 0, 0:keys], inv[:, 0:1], pr[:, 1, 0:keys], ALU.mult, ALU.add, v, *free)
        prob2.give(pr, v)
        return df, v

    def turn_diff(df, mark, t):
        bank, free = banks.take()
        for i in range(t + 1):
            last = turn(bank[:, i * P:(i + 1) * P], df[:, i * P:(i + 1) * P], mark, *free)
        diff.give(df, last)
        dt_, free = diff_t.take()
        a = act_fn(dt_[:, 0:t + 1, :], bank[:, 0:(t + 1) * P].rearrange("p (k n) -> p k n", n=P), ACT.Copy, last, *free)
        banks.give(bank, a)
        return dt_, a

    def norm_heads(t, g, bank, mark):
        got = bank[:, :].rearrange("p (h d) -> p h d", d=P)
        sq, free = temps.take()
        a = act_fn(sq[:, 0:COLS], bank[:, :], ACT.Square, mark, *free)
        ss, r = stat(4), stat(4)
        v = reduce(ss, sq[:, 0:COLS].rearrange("p (h d) -> p h d", d=P), ALU.add, a)
        temps.give(sq, v)
        p = rsqrt_mean(r, ss, P, SUBLN_EPS, v)
        to = row[t][:, halves[g]].rearrange("p (h d) -> p h d", d=P)
        v = tt(to, got, r.unsqueeze(2).broadcast_to([P, 4, P]), ALU.mult, p, *row_free[t])
        banks.give(bank, v)
        v = tt(to, to, subln[:, :].unsqueeze(1).broadcast_to([P, 4, P]), ALU.mult, v, ready["subln"])
        normed[t, g] = v

    def attend_diff(g):
        while len(turned_qk[g]) < 4:
            yield
        heads = [(t, 4 * g + j) for t in TILES for j in range(4)]
        scored, turned, o_banks = {}, {}, {}
        for i in range(len(heads) + VALUE_LAG):
            if i < len(heads):
                scored[i] = diff_scores(*heads[i])
            if 0 <= i - TURN_LAG < len(heads):
                turned[i - TURN_LAG] = turn_diff(*scored.pop(i - TURN_LAG), heads[i - TURN_LAG][0])
            if i >= VALUE_LAG:
                while len(v_marks[g]) < 2:
                    yield
                t, hd = heads[i - VALUE_LAG]
                if t not in o_banks:
                    o_banks[t] = banks.take()
                bank, free = o_banks[t]
                dt_, mark = turned.pop(i - VALUE_LAG)
                j = hd - 4 * g
                for k in range(t + 1):
                    last = mm(bank[:, j * P:(j + 1) * P], dt_[:, k, :], vv[:, k, hd * P:(hd + 1) * P],
                              k == 0, k == t, mark, *free, *v_marks[g])
                diff_t.give(dt_, last)
                if j == 3:
                    norm_heads(t, g, bank, last)
                if g == 1 and (t, j) == (1, 2):
                    turn_rows(0)
            if i < len(heads) + VALUE_LAG - 1:
                yield
        if g == 1:
            for _ in range(3):
                yield
            turn_rows(1)

    def turn_rows(t):
        x_t.forget(t)
        for half in range(2):
            last = turn_split(row[t][:, halves[half]], t, 4, x_t, 4 * half, normed[t, half])
        row_free[t] = (last,)

    TURN_LAG, VALUE_LAG = 3, 5
    normed = {}
    chores.extend(attend_diff(g) for g in range(2))
    products(stages["qkv_rest"], lambda b: (x_t, 0), qkv, lead=0, tail=0)
    flush()
    for t in TILES:
        x_t.forget(t)

    attn_post, ffn_pre2 = Gain(13, 2), Gain(14, 2)
    products(stages["attn_out"], lambda b: (x_t, 0),
             lambda b, t, bank, mark: post_norm_part(t, b.name[1], bank[:, :], mark, bank, attn_post,
                                                     lambda t: pre_norm(t, ffn_pre2)), skew=SPLIT_SLOTS - 1)
    region.close()

    region = ExitStack()
    ple_pre2 = Gain(16, 2)
    mlp(1, region, lambda t: pre_norm(t, ple_pre2))
    region.close()

    stored = []

    def store(t):
        for half in range(2):
            stored.append(small(sp, out[0, t * P:(t + 1) * P, halves[half]], h[t][:, halves[half]], settle(t, half)))

    ple(1, store)
    flush()
    sp.wait(*stored)

    with hold:
        with nc.Block() as block:
            @block.sync
            def _(engine):
                sp.play(engine)

            @block.scalar
            def _(engine):
                act.play(engine)

            @block.vector
            def _(engine):
                dve.play(engine)

            @block.gpsimd
            def _(engine):
                pool.play(engine)

            @block.tensor
            def _(engine):
                pe.play(engine)


_INS = [
    "x", "meta_tokens", "rel_bias_table", "ffn1_norm", "ffn1_w_in", "ffn1_w_out", "mix_norm", "w_in",
    "forget_bias", "fox_q_norm", "fox_k_norm", "swa_q_norm", "swa_k_norm", "swa_sinks", "w_branch_fox",
    "w_branch_swa", "w_out", "ffn2_norm", "ffn2_w_in", "ffn2_w_out", "p_2", "positions_2", "g_mix_pre_2",
    "g_mix_post_2", "g_ffn_pre_2", "g_ffn_post_2", "g_ple_pre_2", "g_ple_post_2", "a_w_in_2", "a_ln_g_2",
    "a_ln_b_2", "a_w_s_2", "a_b_s_2", "a_w_out_2", "b_w_qkv_2", "b_lam_q1_2", "b_lam_k1_2", "b_lam_q2_2",
    "b_lam_k2_2", "b_subln_g_2", "b_w_o_2", "f_w_up_2", "f_w_down_2", "ple_w_proj_2", "ple_w_gate_2",
    "ple_b_gate_2",
]


def kernel(**inputs):
    import concourse.bacc as bacc
    from concourse.bass_utils import run_bass_kernel_spmd

    nc = bacc.Bacc("TRN2", target_bir_lowering=False, num_devices=1)
    arrays, aps = {}, {}
    given = {name: np.ascontiguousarray(inputs[name]) for name in _INS}
    given["bias_selector"] = bias_selector()
    given["frequencies"] = rotary_frequencies()[None, :]
    for name, a in given.items():
        arrays[f"in_{name}"] = a
        aps[name] = nc.dram_tensor(f"in_{name}", a.shape, mybir.dt.from_np(a.dtype), kind="ExternalInput").ap()
    out = nc.dram_tensor("out_0", (1, SEQ, D), F32, kind="ExternalOutput").ap()
    two_blocks(nc, aps, out)
    r = run_bass_kernel_spmd(nc, [arrays], core_ids=[0])
    return r.results[0]["out_0"]
```
